# Optimizing a Trainium2 kernel written in Bass

```python
import jax, jax.numpy as jnp
from jax import lax
import numpy as np

D_MODEL = 1024
BATCH = 1
SEQ = 512
DEPTH = 2

GRID_W = 64
CTX_LEN = 256
EXPAND = 2
D_INNER = EXPAND * D_MODEL
HG_HEAD_DIM = 128
HG_HEADS = D_INNER // HG_HEAD_DIM
HG_STREAMS = 5
FT_GROUPS = 8
FT_GROUP_DIM = D_INNER // FT_GROUPS
CHUNK = 64
N_MIXERS = 2
N_HGRN = (DEPTH + 1) // 2
N_FOURIER = DEPTH // 2
EPS = 1e-6


def rms_norm(x, g):
    xf = x.astype(jnp.float32)
    var = jnp.mean(xf * xf, axis=-1, keepdims=True)
    return (xf * lax.rsqrt(var + EPS)).astype(x.dtype) * g

def adaln(cvec, w, b):
    m = jax.nn.silu(cvec) @ w + b
    return jnp.split(m, 3, axis=-1)

def chunk_scan(q, k, v, g, s0):
    B, H, N, Dk = q.shape
    Dv = v.shape[-1]
    nc = N // CHUNK

    def to_chunks(a):
        a = a.astype(jnp.float32).reshape(B, H, nc, CHUNK, a.shape[-1])
        return jnp.moveaxis(a, 2, 0)

    causal = jnp.tril(jnp.ones((CHUNK, CHUNK), dtype=bool))[:, :, None]

    def step(S, inp):
        qc, kc, vc, gc = inp
        b = jnp.cumsum(gc, axis=-2)
        diff = b[..., :, None, :] - b[..., None, :, :]
        decay = jnp.exp(jnp.where(causal, diff, -jnp.inf))
        scores = jnp.einsum('bhtc,bhtsc,bhsc->bhts', qc, decay, kc)
        o = (jnp.einsum('bhts,bhsv->bhtv', scores, vc)
             + jnp.einsum('bhtc,bhcv->bhtv', qc * jnp.exp(b), S))
        b_last = b[..., -1:, :]
        S_new = (jnp.exp(b_last)[..., 0, :, None] * S
                 + jnp.einsum('bhsc,bhsv->bhcv', kc * jnp.exp(b_last - b), vc))
        return S_new, o

    S_fin, o = lax.scan(step, s0, (to_chunks(q), to_chunks(k), to_chunks(v), to_chunks(g)))
    o = jnp.moveaxis(o, 0, 2).reshape(B, H, N, Dv)
    return o, S_fin

def hgrn_lower_bound(logits, j):
    p = jax.nn.softmax(logits.astype(jnp.float32), axis=0)
    return jnp.cumsum(p, axis=0)[j]

def hgrn_project(h, w_in, lb):
    B, N, _ = h.shape
    p = (h @ w_in).reshape(B, N, HG_STREAMS, HG_HEADS, HG_HEAD_DIM)
    p = jnp.transpose(p, (2, 0, 3, 1, 4))
    q = jax.nn.silu(p[0])
    lbh = lb.reshape(2, 1, HG_HEADS, 1, HG_HEAD_DIM)
    f = lbh + (1.0 - lbh) * jax.nn.sigmoid(p[1:3].astype(jnp.float32))
    return q, 1.0 - f, jnp.log(f), p[3], p[4]

def hgrn_readout(o, z, norm_g, w_out):
    y = rms_norm(o, norm_g).astype(z.dtype) * jax.nn.silu(z)
    B, H, N, d = y.shape
    return jnp.transpose(y, (0, 2, 1, 3)).reshape(B, N, H * d) @ w_out

def hgrn_mixer(h_ctx, h_lat, w_in, lb, norm_g, w_out, ctx_out):
    qc, kc, gc, vc, zc = hgrn_project(h_ctx, w_in, lb)
    ql, kl, gl, vl, zl = hgrn_project(h_lat, w_in, lb)
    B = h_lat.shape[0]
    s0 = jnp.zeros((B, HG_HEADS, HG_HEAD_DIM, HG_HEAD_DIM), jnp.float32)
    flip = lambda a: jnp.flip(a, axis=2)
    o_cf, s_cf = chunk_scan(qc, kc[0], vc, gc[0], s0)
    o_cb, s_cb = chunk_scan(flip(qc), flip(kc[1]), flip(vc), flip(gc[1]), s0)
    o_lf, _ = chunk_scan(ql, kl[0], vl, gl[0], s_cf)
    o_lb, _ = chunk_scan(flip(ql), flip(kl[1]), flip(vl), flip(gl[1]), s_cb)
    y_lat = hgrn_readout(o_lf + flip(o_lb), zl, norm_g, w_out)
    y_ctx = hgrn_readout(o_cf + flip(o_cb), zc, norm_g, w_out) if ctx_out else None
    return y_lat, y_ctx

def fourier_mixer(h, w_in, w_out):
    B, N, _ = h.shape
    u, z = jnp.split(h @ w_in, 2, axis=-1)
    ug = u.astype(jnp.float32).reshape(B, N, FT_GROUPS, FT_GROUP_DIM)
    y = jnp.fft.fft2(ug, axes=(1, 3), norm='ortho').real.reshape(B, N, D_INNER)
    return (y.astype(h.dtype) * jax.nn.silu(z)) @ w_out

def first_inputs(seed: int = 0) -> dict:
    key = jax.random.key(seed)
    ks = jax.random.split(key, 14)
    D, E = D_MODEL, D_INNER
    nrm = jax.random.normal
    return {
        'x': nrm(ks[0], (BATCH, SEQ, D), jnp.float32),
        'c': nrm(ks[1], (BATCH, D), jnp.float32),
        'ctx': nrm(ks[2], (BATCH, CTX_LEN, D), jnp.float32),
        'c_ctx': nrm(ks[3], (D,), jnp.float32),
        'ada_w': nrm(ks[4], (DEPTH, D, 3 * D), jnp.float32) * (0.5 * D ** -0.5),
        'ada_b': nrm(ks[5], (DEPTH, 3 * D), jnp.float32) * 0.01,
        'norm_g': 1.0 + 0.05 * nrm(ks[6], (DEPTH, D), jnp.float32),
        'hg_w_in': nrm(ks[7], (N_HGRN, D, HG_STREAMS * E), jnp.float32) * D ** -0.5,
        'hg_lb_logits': 0.5 * nrm(ks[8], (N_HGRN + 1, 2, E), jnp.float32),
        'hg_norm_g': 1.0 + 0.05 * nrm(ks[9], (N_HGRN, HG_HEAD_DIM), jnp.float32),
        'hg_w_out': nrm(ks[10], (N_HGRN, E, D), jnp.float32) * E ** -0.5,
        'ft_w_in': nrm(ks[11], (N_FOURIER, D, 2 * E), jnp.float32) * D ** -0.5,
        'ft_w_out': nrm(ks[12], (N_FOURIER, E, D), jnp.float32) * E ** -0.5,
        'final_g': 1.0 + 0.05 * nrm(ks[13], (D,), jnp.float32),
    }

def first_block(x, c, ctx, c_ctx, ada_w, ada_b, norm_g, hg_w_in, hg_lb_logits, hg_norm_g,
              hg_w_out, ft_w_in, ft_w_out, final_g):
    x_lat, x_ctx = x, ctx
    for i in range(DEPTH):
        ctx_out = i < DEPTH - 1
        j = i // N_MIXERS
        sh_l, sc_l, gt_l = adaln(c, ada_w[i], ada_b[i])
        h_lat = rms_norm(x_lat, norm_g[i]) * (1.0 + sc_l[:, None]) + sh_l[:, None]
        if i % N_MIXERS == 0:
            sh_c, sc_c, gt_c = adaln(c_ctx, ada_w[i], ada_b[i])
            h_ctx = rms_norm(x_ctx, norm_g[i]) * (1.0 + sc_c) + sh_c
            lb = hgrn_lower_bound(hg_lb_logits, j)
            y_lat, y_ctx = hgrn_mixer(h_ctx, h_lat, hg_w_in[j], lb, hg_norm_g[j], hg_w_out[j], ctx_out)
        else:
            y_lat = fourier_mixer(h_lat, ft_w_in[j], ft_w_out[j])
            if ctx_out:
                sh_c, sc_c, gt_c = adaln(c_ctx, ada_w[i], ada_b[i])
                h_ctx = rms_norm(x_ctx, norm_g[i]) * (1.0 + sc_c) + sh_c
                y_ctx = fourier_mixer(h_ctx, ft_w_in[j], ft_w_out[j])
        x_lat = x_lat + gt_l[:, None] * y_lat
        if ctx_out:
            x_ctx = x_ctx + gt_c * y_ctx
    return rms_norm(x_lat, final_g)


DEPTH_2 = 1

N_META = 16
D_RNN = 1024
N_RNN_HEADS = 4
RNN_HEAD_DIM = D_RNN // N_RNN_HEADS
RNN_CONV_WIDTH = 4
RG_LRU_C = 8.0
D_CONV = 1024
CONV_WIDTH = 31
D_FF = 2816
FFN_RESIDUAL_WEIGHT = 0.5
IN_SIZES = (D_RNN, D_RNN, D_CONV, D_CONV, D_MODEL, D_MODEL)
IN_TOTAL = sum(IN_SIZES)
IN_SPLITS = tuple(int(v) for v in np.cumsum(IN_SIZES)[:-1])


def rmsnorm(x, g):
    xf = x.astype(jnp.float32)
    y = xf * lax.rsqrt(jnp.mean(xf * xf, axis=-1, keepdims=True) + EPS)
    return (y * g.astype(jnp.float32)).astype(x.dtype)

def layernorm(x, g, b):
    xf = x.astype(jnp.float32)
    mu = jnp.mean(xf, axis=-1, keepdims=True)
    var = jnp.mean(jnp.square(xf - mu), axis=-1, keepdims=True)
    y = (xf - mu) * lax.rsqrt(var + EPS)
    return (y * g.astype(jnp.float32) + b.astype(jnp.float32)).astype(x.dtype)

def swiglu_ffn(h, w_gu, w_down):
    gate, up = jnp.split(h @ w_gu, 2, axis=-1)
    return (jax.nn.silu(gate) * up) @ w_down

def causal_depthwise_conv(x, w, b):
    k_width, channels = w.shape
    out = lax.conv_general_dilated(
        x, w[:, None, :].astype(x.dtype), window_strides=(1,), padding=((k_width - 1, 0),),
        dimension_numbers=("NWC", "WIO", "NWC"), feature_group_count=channels)
    return out + b

def rg_lru(x, w_a, b_a, w_x, b_x, lam):
    bsz, t_len, _ = x.shape
    xb = x.reshape(bsz, t_len, N_RNN_HEADS, RNN_HEAD_DIM)
    r = jax.nn.sigmoid((jnp.einsum("bthi,hij->bthj", xb, w_a).reshape(bsz, t_len, D_RNN) + b_a).astype(jnp.float32))
    i = jax.nn.sigmoid((jnp.einsum("bthi,hij->bthj", xb, w_x).reshape(bsz, t_len, D_RNN) + b_x).astype(jnp.float32))
    log_a = -RG_LRU_C * r * jax.nn.softplus(-lam.astype(jnp.float32))
    a = jnp.exp(log_a)
    u = jnp.sqrt(-jnp.expm1(2.0 * log_a)) * (i * x.astype(jnp.float32))

    def combine(left, right):
        a_l, h_l = left
        a_r, h_r = right
        return a_l * a_r, a_r * h_l + h_r

    _, h = lax.associative_scan(combine, (a, u), axis=1)
    return h.astype(x.dtype)

def token_mixer(h, w_in, b_in, rnn_conv_w, rnn_conv_b, rg_w_a, rg_b_a, rg_w_x, rg_b_x, rg_lambda,
                rnn_w_proj, conv_dw_w, conv_dw_b, conv_ln_g, conv_ln_b, conv_w_proj, conv_b_proj, w_out):
    proj = h @ w_in + b_in
    x_rnn, y_rnn, glu_v, glu_g, gate_a, gate_b = jnp.split(proj, IN_SPLITS, axis=-1)
    xr = causal_depthwise_conv(x_rnn, rnn_conv_w, rnn_conv_b)
    xr = rg_lru(xr, rg_w_a, rg_b_a, rg_w_x, rg_b_x, rg_lambda)
    y_a = (xr * jax.nn.gelu(y_rnn)) @ rnn_w_proj
    v = glu_v * jax.nn.sigmoid(glu_g)
    v = causal_depthwise_conv(v, conv_dw_w, conv_dw_b)
    v = jax.nn.silu(layernorm(v, conv_ln_g, conv_ln_b))
    y_b = v @ conv_w_proj + conv_b_proj
    merged = jax.nn.sigmoid(gate_a) * y_a + jax.nn.sigmoid(gate_b) * y_b
    return merged @ w_out

def second_inputs(seed: int = 0) -> dict:
    key = jax.random.key(seed)
    ks = iter(jax.random.split(key, 40))
    L = DEPTH_2
    f32 = jnp.float32

    def nrm(shape, fan_in):
        return jax.random.normal(next(ks), shape, f32) * (fan_in ** -0.5)

    def gain(shape):
        return 1.0 + 0.02 * jax.random.normal(next(ks), shape, f32)

    def bias(shape):
        return 0.01 * jax.random.normal(next(ks), shape, f32)

    x = jax.random.normal(next(ks), (BATCH, SEQ, D_MODEL), f32)
    meta_tokens = jax.random.normal(next(ks), (N_META, D_MODEL), f32)
    u = jax.random.uniform(next(ks), (L, D_RNN), f32, minval=0.9, maxval=0.999)
    s = u ** (1.0 / RG_LRU_C)
    rg_lambda = jnp.log(s) - jnp.log1p(-s)
    return {
        "x": x,
        "meta_tokens": meta_tokens,
        "ffn1_norm": gain((L, D_MODEL)),
        "ffn1_w_gu": nrm((L, D_MODEL, 2 * D_FF), D_MODEL),
        "ffn1_w_down": nrm((L, D_FF, D_MODEL), D_FF),
        "mix_norm": gain((L, D_MODEL)),
        "w_in": nrm((L, D_MODEL, IN_TOTAL), D_MODEL),
        "b_in": bias((L, IN_TOTAL)),
        "rnn_conv_w": nrm((L, RNN_CONV_WIDTH, D_RNN), RNN_CONV_WIDTH),
        "rnn_conv_b": bias((L, D_RNN)),
        "rg_w_a": nrm((L, N_RNN_HEADS, RNN_HEAD_DIM, RNN_HEAD_DIM), RNN_HEAD_DIM),
        "rg_b_a": bias((L, D_RNN)),
        "rg_w_x": nrm((L, N_RNN_HEADS, RNN_HEAD_DIM, RNN_HEAD_DIM), RNN_HEAD_DIM),
        "rg_b_x": bias((L, D_RNN)),
        "rg_lambda": rg_lambda,
        "rnn_w_proj": nrm((L, D_RNN, D_MODEL), D_RNN),
        "conv_dw_w": nrm((L, CONV_WIDTH, D_CONV), CONV_WIDTH),
        "conv_dw_b": bias((L, D_CONV)),
        "conv_ln_g": gain((L, D_CONV)),
        "conv_ln_b": bias((L, D_CONV)),
        "conv_w_proj": nrm((L, D_CONV, D_MODEL), D_CONV),
        "conv_b_proj": bias((L, D_MODEL)),
        "w_out": nrm((L, D_MODEL, D_MODEL), D_MODEL),
        "ffn2_norm": gain((L, D_MODEL)),
        "ffn2_w_gu": nrm((L, D_MODEL, 2 * D_FF), D_MODEL),
        "ffn2_w_down": nrm((L, D_FF, D_MODEL), D_FF),
        "final_norm": gain((D_MODEL,)),
    }

def second_block(x, meta_tokens, ffn1_norm, ffn1_w_gu, ffn1_w_down, mix_norm, w_in, b_in,
              rnn_conv_w, rnn_conv_b, rg_w_a, rg_b_a, rg_w_x, rg_b_x, rg_lambda, rnn_w_proj,
              conv_dw_w, conv_dw_b, conv_ln_g, conv_ln_b, conv_w_proj, conv_b_proj, w_out,
              ffn2_norm, ffn2_w_gu, ffn2_w_down, final_norm):
    bsz = x.shape[0]
    meta = jnp.broadcast_to(meta_tokens.astype(x.dtype)[None], (bsz, N_META, x.shape[-1]))
    h = jnp.concatenate([meta, x], axis=1)
    for l in range(DEPTH_2):
        h = h + FFN_RESIDUAL_WEIGHT * swiglu_ffn(rmsnorm(h, ffn1_norm[l]), ffn1_w_gu[l], ffn1_w_down[l])
        h = h + token_mixer(rmsnorm(h, mix_norm[l]), w_in[l], b_in[l], rnn_conv_w[l], rnn_conv_b[l],
                            rg_w_a[l], rg_b_a[l], rg_w_x[l], rg_b_x[l], rg_lambda[l], rnn_w_proj[l],
                            conv_dw_w[l], conv_dw_b[l], conv_ln_g[l], conv_ln_b[l], conv_w_proj[l],
                            conv_b_proj[l], w_out[l])
        h = h + FFN_RESIDUAL_WEIGHT * swiglu_ffn(rmsnorm(h, ffn2_norm[l]), ffn2_w_gu[l], ffn2_w_down[l])
    return rmsnorm(h, final_norm)[:, N_META:, :]


def setup_inputs(seed=0):
    out = dict(first_inputs(seed))
    for name, value in second_inputs(seed + 1).items():
        if name != "x":
            out[name + "_2"] = value
    return out


def reference(
    x, c, ctx, c_ctx, ada_w, ada_b, norm_g, hg_w_in, hg_lb_logits, hg_norm_g, hg_w_out, ft_w_in,
    ft_w_out, final_g, meta_tokens_2, ffn1_norm_2, ffn1_w_gu_2, ffn1_w_down_2, mix_norm_2,
    w_in_2, b_in_2, rnn_conv_w_2, rnn_conv_b_2, rg_w_a_2, rg_b_a_2, rg_w_x_2, rg_b_x_2,
    rg_lambda_2, rnn_w_proj_2, conv_dw_w_2, conv_dw_b_2, conv_ln_g_2, conv_ln_b_2,
    conv_w_proj_2, conv_b_proj_2, w_out_2, ffn2_norm_2, ffn2_w_gu_2, ffn2_w_down_2,
    final_norm_2,
):
    x = first_block(
        x, c, ctx, c_ctx, ada_w, ada_b, norm_g, hg_w_in, hg_lb_logits, hg_norm_g, hg_w_out,
        ft_w_in, ft_w_out, final_g,
    )
    return second_block(
        x, meta_tokens_2, ffn1_norm_2, ffn1_w_gu_2, ffn1_w_down_2, mix_norm_2, w_in_2, b_in_2,
        rnn_conv_w_2, rnn_conv_b_2, rg_w_a_2, rg_b_a_2, rg_w_x_2, rg_b_x_2, rg_lambda_2,
        rnn_w_proj_2, conv_dw_w_2, conv_dw_b_2, conv_ln_g_2, conv_ln_b_2, conv_w_proj_2,
        conv_b_proj_2, w_out_2, ffn2_norm_2, ffn2_w_gu_2, ffn2_w_down_2, final_norm_2,
    )


_drawn_inputs = setup_inputs


def setup_inputs(seed=0):
    import zlib

    import numpy as np

    out = dict(_drawn_inputs(seed))
    spreads = {}
    factors = {'ctx': 7.924,
     'c_ctx': 8.0,
     'ada_b': 4.779,
     'norm_g': 3.14,
     'hg_lb_logits': 6.511,
     'hg_norm_g': 4.358,
     'ffn1_norm_2': 6.461,
     'mix_norm_2': 6.388,
     'b_in_2': 9.824,
     'rnn_conv_b_2': 12.127,
     'rg_b_a_2': 61.123,
     'rg_b_x_2': 49.451,
     'conv_dw_b_2': 64.0,
     'conv_ln_g_2': 61.368,
     'conv_ln_b_2': 200.0,
     'conv_b_proj_2': 200.0,
     'ffn2_norm_2': 21.987,
     'final_norm_2': 21.067}
    for name, (base, spread) in spreads.items():
        noise = np.random.default_rng([zlib.crc32(name.encode()), seed]).standard_normal(out[name].shape)
        drawn = base * np.exp(spread * noise) if base else spread * noise
        out[name] = __import__('jax').numpy.asarray(drawn.astype(out[name].dtype))
    for name, factor in factors.items():
        out[name] = (out[name] * factor).astype(out[name].dtype)
    return out
```

```python
from contextlib import ExitStack

import numpy as np

import concourse.bass as bass
from concourse import mybir

F32 = mybir.dt.float32
F32R = mybir.dt.float32r
I32 = mybir.dt.int32
ALU = mybir.AluOpType
ACT = mybir.ActivationFunctionType
ds = bass.ds

P = 128
D = 1024
KD = D // P
E = 2048
HEADS = E // P
T = 512
TT = T // P
TC = 256
CT = TC // P
TA = TC + T
AT = TA // P
GROUPS = 8
META = 16
TM = META + T
HALF = TM // 2
DFF = 2816
FT = DFF // P
FF_GROUPS = (8, 8, 6)
DW = 31
RW = 4
EPS = 1e-6
LEVELS = 7
BLK = KD * P
BF = 258

_sizes = [("c", 2 * KD), ("ada_b0", 24), ("ada_b1", 24), ("norm_g0", KD), ("norm_g1", KD),
          ("lb", 2 * 2 * HEADS), ("hg_g", 1), ("final_g", KD), ("ffn1_g", KD), ("mix_g", KD),
          ("b_in", 48), ("rw", RW * KD), ("rb", KD), ("b_a", KD), ("b_x", KD), ("lam", KD),
          ("dw", DW * KD), ("dwb", KD), ("ln_g", KD), ("ln_b", KD), ("cpb", KD), ("ffn2_g", KD),
          ("out_g", KD)]
VEC = {}
_at = 0
for _n, _s in _sizes:
    VEC[_n] = _at
    _at += _s
NVEC = _at


PER = {"head": 25, "mix": 80}

ORDER = ((0, 1, 2, 3, 4), (1, 0, 5, 4, 3))


class Own:

    def __init__(self, eng, sem):
        self.eng, self.sem, self.base, self.i, self.per, self.n = eng, sem, 0, 0, 0, 0

    def mark(self, instruction):
        instruction.then_inc(self.sem, 1)
        self.n += 1

    def wait(self):
        self.eng.wait_ge(self.sem, self.i * self.per + self.base + self.n)

    def link(self, instruction):
        self.mark(instruction)
        self.wait()

    def enter(self, i, per):
        self.base += self.n
        self.n, self.i, self.per = 0, i, per

    def leave(self, trips):
        assert self.n == self.per, f"{self.sem.name}: {self.n} signals an iteration, not {self.per}"
        self.base += trips * self.per
        self.n, self.i, self.per = 0, 0, 0


class Region:

    def __init__(self, nc, start):
        self.nc, self.at, self.start = nc, start, start

    def take(self, name, shape, dt=F32):
        size = int(np.prod(shape[1:])) * 4
        tensor = self.nc.alloc_sbuf_tensor_at(name, shape, dt, offset=self.at)
        self.at += (size + 31) // 32 * 32
        return tensor

    def over(self):
        return Region(self.nc, self.at)


def halves(ap):
    return ap.rearrange("p (a b) -> p a b", a=2)


def program(nc, wts, x_in, ctx_in, meta_in, vec_in, mask_in, ident_in, dft_in, chan_in, out):
    nblocks = wts.shape[0]
    with ExitStack() as top:
        def sem(name):
            return top.enter_context(nc.semaphore(name))

        g = Region(nc, (nc.sbuf_base + 63) // 64 * 64)
        w_raw = g.take("w_raw", [P, 2, BLK])
        w_hi = g.take("w_hi", [P, 2, BLK], F32R)
        w_lo = g.take("w_lo", [P, 2, BLK], F32R)
        vec = g.take("vec", [P, NVEC])
        ones_d = g.take("ones_d", [P, P])
        ones_h = g.take("ones_h", [P, P])
        ident = g.take("ident", [P, P])
        eps = g.take("eps", [P, 1])
        zero = g.take("zero", [P, 1])
        ada0 = g.take("ada0", [P, 24, 2])
        ada1 = g.take("ada1", [P, 24, 2])
        scale = g.take("scale", [P, 3, KD])
        csil = g.take("csil", [P, KD, 2])
        c_hi = g.take("c_hi", [P, KD, 2], F32R)
        c_lo = g.take("c_lo", [P, KD, 2], F32R)
        lbt = g.take("lbt", [P, 6, 2 * HEADS])
        rgc = g.take("rgc", [P, 8, KD])
        r = g.over()
        x0 = r.take("x0", [P, KD, T])
        xc = r.take("xc", [P, KD, TC])
        st_sum, st_sq = r.take("st_sum", [P, 2, T]), r.take("st_sq", [P, T])
        st_tmp = r.take("st_tmp", [P, 2, T])
        r = g.over()
        y_hi = r.take("y_hi", [P, HEADS, T], F32R)
        y_lo = r.take("y_lo", [P, HEADS, T], F32R)
        h = r.over()
        h_hi, h_lo = h.take("h_hi", [P, KD, T], F32R), h.take("h_lo", [P, KD, T], F32R)
        hc_hi, hc_lo = h.take("hc_hi", [P, KD, TC], F32R), h.take("hc_lo", [P, KD, TC], F32R)
        q_st = h.take("q_st", [P, T])
        f_st = h.take("f_st", [P, 2, TA])
        v_st = h.take("v_st", [P, TA])
        z_st = h.take("z_st", [P, T])
        z_cur = h.take("z_cur", [P, T])
        Q = h.take("Q", [P, 2, T])
        K = h.take("K", [P, 2, TA])
        ksum = h.take("ksum", [P, T])
        f_tree = h.take("f_tree", [P, 2, TA])
        V = h.take("V", [P, AT, P])
        KT = h.take("KT", [P, 4, P])
        ST = h.take("ST", [P, TT, P])
        states = h.take("states", [P, 5, 2, P])
        osq, rt, ytmp = h.take("osq", [P, T]), h.take("rt", [P, T]), h.take("ytmp", [P, T])
        masks = h.take("masks", [P, LEVELS + 1, P], I32)
        f = r.over()
        x1 = f.take("x1", [P, KD, T])
        n1 = {k: f.take(f"n1_{k}", [P, 2 if k == "tmp" else 1, T]) for k in ("sum", "sq", "tmp")}
        g_hi, g_lo = f.take("g_hi", [P, KD, T], F32R), f.take("g_lo", [P, KD, T], F32R)
        F_hi = f.take("F_hi", [P, TT, T], F32R)
        F_lo = f.take("F_lo", [P, TT, T], F32R)
        C_hi = f.take("C_hi", [P, 2, 2, 2, P], F32R)
        C_lo = f.take("C_lo", [P, 2, 2, 2, P], F32R)
        raw = f.over()
        F_raw, C_raw = raw.take("F_raw", [P, TT, T]), raw.take("C_raw", [P, 2, 2, 2, P])
        u_st, zf_st = f.take("u_st", [P, 2, T]), f.take("zf_st", [P, 2, T])
        u_hi, u_lo = f.take("u_hi", [P, 2, T], F32R), f.take("u_lo", [P, 2, T], F32R)
        p_hi, p_lo = f.take("p_hi", [P, 2, T], F32R), f.take("p_lo", [P, 2, T], F32R)
        o_sb, yf, yg = f.take("o_sb", [P, 256]), f.take("yf", [P, T]), f.take("yg", [P, T])
        b = g.over()
        hb = b.take("hb", [P, KD, TM])
        n2 = {k: b.take(f"n2_{k}", [P, 2 if k == "tmp" else 1, TM]) for k in ("sum", "sq", "tmp")}
        n_hi, n_lo = b.take("n_hi", [P, KD, TM], F32R), b.take("n_lo", [P, KD, TM], F32R)
        assert b.at <= r.at
        m = b.over()
        hid_hi, hid_lo = m.take("hid_hi", [P, 8, TM], F32R), m.take("hid_lo", [P, 8, TM], F32R)
        sg, hid = m.take("sg", [P, TM]), m.take("hid", [P, TM])
        m = b.over()
        a_hi, a_lo = m.take("a_hi", [P, KD, T], F32R), m.take("a_lo", [P, KD, T], F32R)
        gate = m.take("gate", [P, 2, KD, T])
        mk = m.over()
        cv = mk.take("cv", [P, KD, T])
        gvs, ggs = mk.take("gvs", [P, TM]), mk.take("ggs", [P, TM])
        vpad = mk.take("vpad", [P, DW - 1 + TM])
        xpad = mk.take("xpad", [P, 2, RW - 1 + TM + 1])
        xr = mk.take("xr", [P, 2, TM])
        xr_hi, xr_lo = mk.take("xr_hi", [P, 2, TM], F32R), mk.take("xr_lo", [P, 2, TM], F32R)
        yst = mk.take("yst", [P, 2, T])
        rr, ii = mk.take("rr", [P, 2, TM]), mk.take("ii", [P, 2, TM])
        pp, dd = mk.take("pp", [P, 2, TM]), n2["tmp"][:, 0]
        m = m.over()
        mg_hi, mg_lo = m.take("mg_hi", [P, KD, T], F32R), m.take("mg_lo", [P, KD, T], F32R)
        mt = m.take("mt", [P, 2, T])
        m = b.over()
        fin = m.take("fin", [P, KD, T])

        ps = top.enter_context(nc.psum_tensor("ps", [P, 8, T], F32))

        w_loaded = [sem(f"w_loaded{s}") for s in range(2)]
        hi_ready = [sem(f"hi_ready{s}") for s in range(2)]
        lo_ready = [sem(f"lo_ready{s}") for s in range(2)]
        w_used = [sem(f"w_used{s}") for s in range(2)]
        phase_over = sem("phase_over")
        vec_in_s, x_in_s, xc_in_s, const_in_s, dft_in_s, chan_in_s, x1_in_s, meta_in_s, out_s = [
            sem(n) for n in ("vec_loaded", "x_loaded", "ctx_loaded", "const_loaded", "dft_loaded",
                             "chan_loaded", "x1_loaded", "meta_loaded", "out_stored")]
        ident_in_s = sem("ident_loaded")
        consts_set = sem("consts_set")
        small = {e: sem(f"small_{e}") for e in ("act", "dve")}
        own_s = {e: sem(f"own_{e}") for e in ("act", "dve")}
        ada_done = sem("ada_done")
        acc_free = sem("acc_free")
        pe_scan, act_scan, dve_scan = sem("pe_scan"), sem("act_scan"), sem("dve_scan")
        PE_SCAN, ACT_SCAN, DVE_SCAN = 18, 8, 14

        def residual_sems(tag):
            return {k: sem(f"{tag}_{k}") for k in ("res", "sq", "add")}

        def norm_sems(tag):
            return {k: sem(f"{tag}_{k}") for k in ("sum", "mean", "root", "tmp", "hi", "lo")}

        N0, N0C, N1, NFIN, NF1, NMIX, NF2, NOUT = [
            norm_sems(t) for t in ("n0", "n0c", "n1", "nfin", "nf1", "nmix", "nf2", "nout")]
        R0, R0C, RC, RF, RA, RD1, RM, RD2 = [
            residual_sems(t) for t in ("r0", "r0c", "rc", "rf", "ra", "rd1", "rm", "rd2")]
        ada_c = sem("ada_c")
        ft_acc, pe_ft, act_ft, dve_ft = sem("ft_acc"), sem("pe_ft"), sem("act_ft"), sem("dve_ft")
        dft_split = {e: sem(f"dft_split_{e}") for e in ("act", "dve")}
        ffn = {t: {k: sem(f"{t}_{k}") for k in ("gate", "up", "hi", "lo")}
               for t in ("f1a", "f1b", "f1c", "f2a", "f2b", "f2c")}
        RP = {t: residual_sems(t) for t in ("f1a", "f1b", "f2a", "f2b")}
        mx_acc, mx_act, mx_dve = sem("mx_acc"), sem("mx_act"), sem("mx_dve")
        ln_pe, ln_act, ln_dve = sem("ln_pe"), sem("ln_act"), sem("ln_dve")
        mg_dve, mg_act = sem("mg_dve"), sem("mg_act")

        def col(name, j, n=1):
            return vec[:, ds(VEC[name] + j, n)]

        def row(t, j):
            return t[:, j] if isinstance(j, int) else t[:, ds(j, 1)].rearrange("p a n -> p (a n)")

        def rate(j):
            return rgc[:, 6:8].rearrange("p a k -> p (a k)")[:, ds(j, 1)]

        class Stream:

            def __init__(self):
                self.base, self.i, self.per = 0, 0, 0

            def enter(self, i, per):
                self.i, self.per = i, per

            def leave(self, trips):
                self.base += trips * self.per
                self.i = self.per = 0

            def slot(self, k):
                return k % 2, self.i * (self.per // 2) + (self.base // 2 + k // 2)

            def wait_done(self, eng, k):
                s, use = self.slot(k)
                eng.wait_ge(w_used[s], use + 2)

        block = top.enter_context(nc.Block())

        @block.sync
        def _(sp):
            with sp.Fori(0, nblocks // 2) as i:
                for s in range(2):
                    sp.wait_ge(lo_ready[s], i + 1)
                    sp.dma_start(w_raw[:, s], wts[ds(i * 2 + s, 1)].rearrange("a p n -> p (a n)")
                                 ).then_inc(w_loaded[s], 16)

        @block.gpsimd
        def _(pool):
            pool.dma_start(vec[:], vec_in).then_inc(vec_in_s, 16)
            pool.dma_start(x0[:], x_in).then_inc(x_in_s, 16)
            pool.dma_start(xc[:], ctx_in).then_inc(xc_in_s, 16)
            pool.dma_start(masks[:], mask_in).then_inc(const_in_s, 16)
            pool.dma_start(ident[:], ident_in).then_inc(ident_in_s, 16)
            pool.wait_ge(phase_over, 3 * 2)
            pool.dma_start(x1[:], x_in).then_inc(x1_in_s, 16)
            pool.dma_start(F_raw[:], dft_in).then_inc(dft_in_s, 16)
            pool.dma_start(C_raw[:], chan_in).then_inc(chan_in_s, 16)
            pool.wait_ge(phase_over, 3 * 4)
            pool.dma_start(hb[:, :, 0:META], meta_in).then_inc(meta_in_s, 16)
            pool.wait_ge(NOUT["lo"], KD)
            pool.dma_start(out, fin[:]).then_inc(out_s, 16)
            pool.wait_ge(out_s, 16)

        @block.tensor
        def _(pe):
            st = Stream()
            over = [0]

            def phase_end():
                over[0] += 1
                pe.drain().then_inc(phase_over, 1)
                pe.wait_ge(phase_over, 3 * over[0])

            def three(outs, whi, wlo, xhi, xlo, start, stop):
                for n, (w, x) in enumerate(((whi, xhi), (whi, xlo), (wlo, xhi))):
                    for o, xp in zip(outs, x):
                        last = nc.tensor.matmul(o, w, xp, start=start and n == 0,
                                                stop=stop and n == 2)
                return last

            def take(k):
                s, use = st.slot(k)
                pe.wait_ge(lo_ready[s], use + 2)
                return s

            def tiles(s, outs, xs, ks, start, stop, first=0):
                for n, k in enumerate(ks):
                    c = slice((first + n) * P, (first + n + 1) * P)
                    last = three(outs, w_hi[:, s, c], w_lo[:, s, c], *xs(k),
                                 start=start and n == 0, stop=stop and n == len(ks) - 1)
                return last

            def whole(hi, lo, a=0, b=T):
                return lambda k: ([hi[:, k, a:b]], [lo[:, k, a:b]])

            def halved(hi, lo):
                return lambda k: ([hi[:, k, 0:HALF], hi[:, k, HALF:TM]],
                                  [lo[:, k, 0:HALF], lo[:, k, HALF:TM]])

            def bank2(b):
                return [ps[:, b, 0:HALF], ps[:, b + 1, 0:HALF]]

            def mean(N, n, src):
                pe.wait_ge(N["sum"], 1)
                if n == TM:
                    for q in range(2):
                        last = nc.tensor.matmul(ps[:, 6 + q, 0:HALF], ones_d[:], src[:, q * HALF:(q + 1) * HALF],
                                                start=True, stop=True)
                else:
                    last = nc.tensor.matmul(ps[:, 6, 0:n], ones_d[:], src[:, 0:n], start=True, stop=True)
                last.then_inc(N["mean"], 1)

            pe.sem_inc(w_used[0], 1)
            pe.sem_inc(w_used[1], 1)

            pe.wait_ge(consts_set, 4)
            with pe.Fori(0, KD) as i:
                st.enter(i, 2)
                for k in range(2):
                    s = take(k)
                    o = ps[:, 7, ds(i * 4 + 2 * k, 2)]
                    tiles(s, [o], whole(c_hi, c_lo, 0, 2), range(KD), True, True).then_inc(w_used[s], 1)
            st.leave(KD)
            mean(N0, T, st_sum[:, 0])
            pe.wait_ge(N0["root"], 1)
            mean(N0C, TC, st_sum[:, 1])
            pe.wait_ge(N0C["lo"], KD)
            pe.wait_ge(ident_in_s, 16)
            phase_end()

            def tile(t):
                return slice(t * P, (t + 1) * P)

            def halves_of(ap, n, half):
                return ap.rearrange("p (m h n) -> p m h n", h=2, n=n)[:, :, half]

            def pe_head(i, j):
                def free(k):
                    pe.wait_ge(acc_free, i * 6 + (k + 1))

                def project(k, part):
                    if i is None:
                        return
                    a, c = k % 2, 2 + k % 2
                    if part == "a":
                        s = take(k)
                        free(k)
                        tiles(s, [ps[:, a]], whole(h_hi, h_lo), range(4), True, False)
                    elif part == "b":
                        last = tiles(k % 2, [ps[:, a]], whole(h_hi, h_lo), range(4, 8), False, True, 4)
                        if k in (0, 4):
                            last.then_inc(w_used[k % 2], 1)
                    elif part == "c":
                        tiles(k % 2, [ps[:, c, 0:TC]], whole(hc_hi, hc_lo, 0, TC), range(8), True, True
                              ).then_inc(w_used[k % 2], 1)
                    else:
                        s = take(k)
                        free(k)
                        tiles(s, [ps[:, c, 0:2]], whole(c_hi, c_lo, 0, 2), range(8), True, True
                              ).then_inc(w_used[s], 1)

                def dve(n):
                    pe.wait_ge(dve_scan, j * DVE_SCAN + n)

                def act(n):
                    pe.wait_ge(act_scan, j * ACT_SCAN + n)

                def turn_v(ts):
                    if j is None:
                        return
                    if len(ts) == TT:
                        pe.wait_ge(acc_free, j * 6 + 6)
                    else:
                        act(1)
                    for n, t in enumerate(ts):
                        last = nc.tensor.transpose(ps[:, 6, tile(n)], v_st[:, tile(t)], ident[:])
                    last.then_inc(pe_scan, 1)

                def diagonal():
                    if j is None:
                        return
                    dve(1)
                    for t in range(TT):
                        last = nc.tensor.matmul(ps[:, 4, tile(t)], ksum[:, tile(t)], q_st[:, tile(t)],
                                                start=True, stop=True)
                    last.then_inc(pe_scan, 1)

                def level(l):
                    if j is None:
                        return
                    dve(1 + l)
                    for t in range(TT):
                        for d in range(2):
                            last = nc.tensor.matmul(
                                halves_of(ps[:, 5 - l % 2, tile(t)], 2 ** l, 1 - d),
                                K[:, d, tile(CT + t)], halves_of(Q[:, d, tile(t)], 2 ** l, 1 - d),
                                start=True, stop=True)
                    last.then_inc(pe_scan, 1)

                def steps(g_):
                    return [(n, d) for n in range(2 * g_, min(2 * g_ + 2, 5)) for d in range(2)]

                def turn_k(g_):
                    if j is None:
                        return
                    dve(8)
                    act(2 + g_)
                    for x, (n, d) in enumerate(steps(g_)):
                        last = nc.tensor.transpose(ps[:, 6, tile(x)], K[:, d, tile(ORDER[d][n])], ident[:])
                    last.then_inc(pe_scan, 1)

                def outer(g_):
                    if j is None:
                        return
                    act(3 + g_)
                    dve((8, 9, 10)[g_])
                    for x, (n, d) in enumerate(steps(g_)):
                        last = nc.tensor.matmul(ps[:, 4 + g_ % 2, tile(x)], KT[:, x], V[:, ORDER[d][n]],
                                                start=True, stop=True)
                    last.then_inc(pe_scan, 1)

                def output():
                    if j is None:
                        return
                    dve(12)
                    for t in range(TT):
                        o = ps[:, 7, tile(t)]
                        nc.tensor.matmul(o, V[:, CT + t], ST[:, t], start=True, stop=False)
                        nc.tensor.matmul(o, states[:, 1 + t, 0], Q[:, 0, tile(t)], start=False, stop=False)
                        last = nc.tensor.matmul(o, states[:, 4 - t, 1], Q[:, 1, tile(t)], start=False, stop=True)
                    last.then_inc(pe_scan, 1)

                def norm():
                    if j is None:
                        return
                    act(6)
                    nc.tensor.matmul(ps[:, 5], ones_h[:], osq[:], start=True, stop=True).then_inc(pe_scan, 1)

                project(0, "a"); turn_v(range(CT, AT)); project(0, "b"); diagonal(); level(0)
                project(1, "a"); level(1); turn_v(range(CT)); project(1, "b"); level(2)
                project(1, "c"); level(3); project(2, "a"); level(4); project(2, "b"); level(5)
                project(2, "c"); level(6); project(3, "a"); turn_k(0); project(3, "b"); outer(0)
                turn_k(1); project(3, "c"); outer(1); turn_k(2); project(4, "a"); outer(2)
                project(4, "b"); output(); project(5, "ada"); norm()

            st.enter(0, 6)
            pe_head(0, None)
            st.leave(1)
            with pe.Fori(0, HEADS - 1) as j:
                st.enter(j, 6)
                pe_head(j + 1, j)
            st.leave(HEADS - 1)
            pe_head(None, HEADS - 1)
            pe.wait_ge(dve_scan, HEADS * DVE_SCAN)
            phase_end()

            with pe.Fori(0, KD) as i:
                st.enter(i, 4)
                s = take(0)
                pe.wait_ge(ada_c, i * 2 + 1)
                tiles(s, [ps[:, 2, 0:2]], whole(c_hi, c_lo, 0, 2), range(8), True, True).then_inc(w_used[s], 1)
                s = take(1)
                pe.wait_ge(RC["res"], i + 1)
                tiles(s, [ps[:, 0]], whole(y_hi, y_lo), range(8), True, False).then_inc(w_used[s], 1)
                s = take(2)
                tiles(s, [ps[:, 0]], whole(y_hi, y_lo), range(8, 16), False, True).then_inc(w_used[s], 1)
                s = take(3)
                pe.wait_ge(ada_c, i * 2 + 2)
                tiles(s, [ps[:, 3, 0:2]], whole(c_hi, c_lo, 0, 2), range(8), True, True).then_inc(w_used[s], 1)
            st.leave(KD)
            mean(N1, T, n1["sum"][:, 0])
            pe.wait_ge(N1["lo"], KD)
            pe.wait_ge(dft_split["dve"], 2)
            phase_end()

            def pe_group(i, j):
                def project(k):
                    if i is None:
                        return
                    s = take(k)
                    pe.wait_ge(ft_acc, i * 4 + (k + 1))
                    tiles(s, [ps[:, k % 2]], whole(g_hi, g_lo), range(8), True, True).then_inc(w_used[s], 1)

                def turn():
                    if j is None:
                        return
                    pe.wait_ge(ft_acc, j * 4 + 4)
                    pe.wait_ge(dve_ft, j * 8 + 1)
                    for a in range(2):
                        for t in range(TT):
                            last = nc.tensor.transpose(ps[:, 4 + a, tile(t)], u_st[:, a, tile(t)], ident[:])
                    last.then_inc(pe_ft, 1)

                def over_tokens(a):
                    if j is None:
                        return
                    pe.wait_ge(dve_ft, j * 8 + (2 + a))
                    for t in range(TT):
                        last = three([ps[:, 6 + a]], u_hi[:, a, tile(t)], u_lo[:, a, tile(t)],
                                     [F_hi[:, t]], [F_lo[:, t]], t == 0, t == TT - 1)
                    last.then_inc(pe_ft, 1)

                def over_channels(m_):
                    if j is None:
                        return
                    pe.wait_ge(dve_ft, j * 8 + 5)
                    for part, c0, n in ((0, 0, BF), (1, 256, 256)):
                        for kk in range(2):
                            last = three([ps[:, 4 + 2 * m_ + part, 0:n]], C_hi[:, part, kk, m_],
                                         C_lo[:, part, kk, m_], [p_hi[:, kk, c0:c0 + n]],
                                         [p_lo[:, kk, c0:c0 + n]], kk == 0, kk == 1)
                    last.then_inc(pe_ft, 1)

                turn(); project(0); over_tokens(0); project(1); over_tokens(1)
                project(2); over_channels(0); project(3); over_channels(1)

            st.enter(0, 4)
            pe_group(0, None)
            st.leave(1)
            with pe.Fori(0, GROUPS - 1) as j:
                st.enter(j, 4)
                pe_group(j + 1, j)
            st.leave(GROUPS - 1)
            pe_group(None, GROUPS - 1)
            pe.wait_ge(dve_ft, GROUPS * 8 + 1)

            def residual(R, trips, nb, xs, n, nk=KD):
                with pe.Fori(0, trips) as i:
                    st.enter(i, 2 * nb)
                    for a in range(2):
                        o = bank2(2 * a) if n == TM else [ps[:, 2 * a]]
                        for q in range(nb):
                            s = take(a * nb + q)
                            if q == 0:
                                pe.wait_ge(R["res"], i * 2 + (a + 1))
                            tiles(s, o, xs, range(q * KD, q * KD + nk), q == 0, q == nb - 1
                                  ).then_inc(w_used[s], 1)
                st.leave(trips)

            residual(RF, KD // 2, 2, whole(y_hi, y_lo), T)
            mean(NFIN, T, n1["sum"][:, 0])
            phase_end()
            mean(NF1, TM, n2["sum"][:, 0])

            def feed_forward(tags, N, last_tag, n):
                xs = halved(n_hi, n_lo) if n == TM else whole(n_hi, n_lo, META, TM)
                hs = halved(hid_hi, hid_lo) if n == TM else whole(hid_hi, hid_lo, META, TM)
                pe.wait_ge(N["lo"], KD)
                for tag, count in zip(tags, FF_GROUPS):
                    S = ffn[tag]
                    with pe.Fori(0, count) as i:
                        st.enter(i, 2)
                        for k, reader in ((0, "gate"), (1, "up")):
                            s = take(k)
                            pe.wait_ge(S[reader], i + 1)
                            o = bank2(2 * k) if n == TM else [ps[:, 2 * k]]
                            tiles(s, o, xs, range(KD), True, True).then_inc(w_used[s], 1)
                    st.leave(count)
                    pe.wait_ge(S["lo"], count + 1)
                    R = RP.get(tag, last_tag)
                    residual(R, KD // 2, 1, hs, n, count)
                    pe.wait_ge(R["res"], KD + 2)

            feed_forward(("f1a", "f1b", "f1c"), NF1, RD1, TM)
            mean(NMIX, TM, n2["sum"][:, 0])
            pe.wait_ge(NMIX["lo"], KD)
            phase_end()

            with pe.Fori(0, KD // 2) as i:
                st.enter(i, 14)
                for k in range(12):
                    s = take(k)
                    pe.wait_ge(mx_acc, i * 14 + (k + 1 if k else 2))
                    if k < 6:
                        tiles(s, bank2(2 * (k % 2)), halved(n_hi, n_lo), range(KD), True, True
                              ).then_inc(w_used[s], 1)
                    else:
                        tiles(s, [ps[:, 2 * (k % 2)]], whole(n_hi, n_lo, META, TM), range(KD), True, True
                              ).then_inc(w_used[s], 1)
                for k in (12, 13):
                    s = take(k)
                    if k == 12:
                        pe.wait_ge(mx_dve, i * 12 + 4)
                    pe.wait_ge(mx_acc, i * 14 + (k + 1))
                    for m_ in range(2):
                        last = tiles(s, bank2((4 if k == 12 else 0) + 2 * m_), halved(xr_hi, xr_lo),
                                     range(2), True, True, 2 * m_)
                    last.then_inc(w_used[s], 1)
            st.leave(KD // 2)
            phase_end()

            pe.wait_ge(ln_dve, 1)
            nc.tensor.matmul(ps[:, 6], ones_d[:], n2["sum"][:, 0, 0:T], start=True, stop=True).then_inc(ln_pe, 1)
            pe.wait_ge(ln_dve, 1 + KD + 1)
            nc.tensor.matmul(ps[:, 7], ones_d[:], n2["sum"][:, 0, 0:T], start=True, stop=True).then_inc(ln_pe, 1)
            pe.wait_ge(ln_dve, 2 + 3 * KD)
            phase_end()

            with pe.Fori(0, KD) as i:
                st.enter(i, 2)
                s = take(0)
                pe.wait_ge(mg_dve, i * 3 + 1)
                tiles(s, [ps[:, 0]], whole(a_hi, a_lo), range(KD), True, True).then_inc(w_used[s], 1)
                s = take(1)
                tiles(s, [ps[:, 2]], whole(n_hi, n_lo), range(KD), True, True).then_inc(w_used[s], 1)
            st.leave(KD)
            pe.wait_ge(mg_dve, KD * 3 + 1)
            residual(RM, KD // 2, 1, whole(mg_hi, mg_lo), T)
            mean(NF2, T, n2["sum"][:, 0])
            phase_end()
            feed_forward(("f2a", "f2b", "f2c"), NF2, RD2, T)
            mean(NOUT, T, n2["sum"][:, 0])

        @block.scalar
        def _(act):
            st = Stream()
            over = [0]
            own = Own(act, own_s["act"])
            run = nc.scalar.activation

            def phase_end():
                over[0] += 1
                act.drain().then_inc(phase_over, 1)
                act.wait_ge(phase_over, 3 * over[0])

            def cut(k):
                s, use = st.slot(k)
                act.wait_ge(w_loaded[s], use * 16 + 16)
                act.wait_ge(w_used[s], use + 1)
                run(w_hi[:, s], w_raw[:, s], ACT.Copy).then_inc(hi_ready[s], 1)

            def after(k):
                st.wait_done(act, k)
                cut(k + 2)

            def root(N, acc, rt_):
                act.wait_ge(N["mean"], 1)
                run(rt_, acc, ACT.Sqrt, bias=eps[:]).then_inc(N["root"], 1)

            def norm_hi(N, hi, tmp, shift):
                for k in range(KD):
                    act.wait_ge(N["tmp"], k + 1)
                    run(hi(k), tmp(k), ACT.Identity, bias=shift(k)).then_inc(N["hi"], 1)

            def squares(R, src, sq):
                for k in range(KD):
                    if k:
                        act.wait_ge(R["add"], k)
                    run(sq, src(k), ACT.Square).then_inc(R["sq"], 1)

            def square_one(R, m_, src, sq, credit):
                act.wait_ge(R["res"], m_ + (1 + credit))
                act.wait_ge(R["add"], m_ + 2)
                run(sq, src, ACT.Square).then_inc(R["sq"], 1)

            for sem_ in (acc_free, ada_c, ft_acc, mx_acc):
                act.sem_inc(sem_, 2)
            for tag in ffn:
                act.sem_inc(ffn[tag]["gate"], 1)

            act.wait_ge(vec_in_s, 16)
            run(csil[:], vec[:, VEC["c"]:VEC["c"] + 2 * KD].rearrange("p (k n) -> p k n", n=2), ACT.Silu
                ).then_inc(small["act"], 1)
            act.wait_ge(small["act"], 1)
            run(c_hi[:], csil[:], ACT.Copy).then_inc(small["act"], 1)
            act.wait_ge(consts_set, 2)
            run(lbt[:, 1:3], lbt[:, 1:3], ACT.Exp).then_inc(small["act"], 1)
            act.wait_ge(consts_set, 3)
            run(rgc[:, 1], rgc[:, 0], ACT.Exp, scale=-1.0).then_inc(small["act"], 1)
            cut(0)
            cut(1)
            act.wait_ge(x_in_s, 16)
            squares(R0, lambda k: x0[:, k], st_sq[:])
            act.wait_ge(xc_in_s, 16)
            act.wait_ge(R0["add"], KD)
            squares(R0C, lambda k: xc[:, k], st_sq[:, 0:TC])
            with act.Fori(0, KD) as i:
                st.enter(i, 2)
                after(0)
                after(1)
            st.leave(KD)
            act.wait_ge(R0C["add"], KD)
            root(N0, ps[:, 6], st_sq[:])
            norm_hi(N0, lambda k: h_hi[:, k], lambda k: st_tmp[:, k % 2], lambda k: ada0[:, k, 0:1])
            act.wait_ge(N0["lo"], KD)
            root(N0C, ps[:, 6, 0:TC], st_sq[:, 0:TC])
            norm_hi(N0C, lambda k: hc_hi[:, k], lambda k: st_tmp[:, k % 2, 0:TC], lambda k: ada0[:, k, 1:2])
            phase_end()

            def act_head(i, j):
                def pe(n):
                    act.wait_ge(pe_scan, j * PE_SCAN + n)

                def dve(n):
                    act.wait_ge(dve_scan, j * DVE_SCAN + n)

                def stage(k):
                    if i is None:
                        return
                    after(k)
                    a, c = ps[:, k % 2], ps[:, 2 + k % 2]
                    if k == 0:
                        if j is not None:
                            pe(2)
                        run(q_st[:], a, ACT.Silu).then_inc(acc_free, 1)
                    elif k < 3:
                        if j is not None:
                            dve(2)
                        run(f_st[:, k - 1, TC:TA], a, ACT.Sigmoid)
                        run(f_st[:, k - 1, 0:TC], c[:, 0:TC], ACT.Sigmoid).then_inc(acc_free, 1)
                    elif k == 3:
                        if j is not None:
                            pe(5)
                        run(v_st[:, TC:TA], a, ACT.Copy)
                        run(v_st[:, 0:TC], c[:, 0:TC], ACT.Copy).then_inc(acc_free, 1)
                    elif k == 4:
                        if j is not None:
                            dve(1)
                        run(z_st[:], a, ACT.Silu).then_inc(acc_free, 1)
                    else:
                        run(row(ada1, i), c[:, 0:2], ACT.Identity, bias=col("ada_b1", i)).then_inc(acc_free, 1)

                def copy(n, dst, src):
                    if j is not None:
                        pe(n)
                        run(dst, src, ACT.Copy).then_inc(act_scan, 1)

                def squares_of_output():
                    if j is not None:
                        pe(17)
                        run(osq[:], ps[:, 7], ACT.Square).then_inc(act_scan, 1)

                def finish():
                    if j is not None:
                        pe(18)
                        run(rt[:], ps[:, 5], ACT.Sqrt, bias=eps[:]).then_inc(act_scan, 1)
                        dve(13)
                        run(row(y_hi, j), ytmp[:], ACT.Copy).then_inc(act_scan, 1)

                copy(1, V[:, CT:AT].rearrange("p t v -> p (t v)"), ps[:, 6])
                stage(0)
                copy(5, V[:, 0:CT].rearrange("p t v -> p (t v)"), ps[:, 6, 0:TC])
                stage(1)
                stage(2)
                kt = KT[:].rearrange("p t v -> p (t v)")
                copy(11, kt, ps[:, 6])
                copy(13, kt, ps[:, 6])
                stage(3)
                copy(15, kt[:, 0:2 * P], ps[:, 6, 0:2 * P])
                stage(4)
                squares_of_output()
                stage(5)
                finish()

            st.enter(0, 6)
            act_head(0, None)
            st.leave(1)
            with act.Fori(0, HEADS - 1) as j:
                st.enter(j, 6)
                act_head(j + 1, j)
            st.leave(HEADS - 1)
            act_head(None, HEADS - 1)
            phase_end()

            with act.Fori(0, KD) as i:
                st.enter(i, 4)
                after(0)
                run(row(ada0, i + 16), ps[:, 2, 0:2], ACT.Identity, bias=col("ada_b0", i + 16)).then_inc(ada_c, 1)
                after(1)
                after(2)
                square_one(RC, i, row(x1, i), n1["sq"][:, 0], 1)
                after(3)
                run(row(ada1, i + 16), ps[:, 3, 0:2], ACT.Identity, bias=col("ada_b1", i + 16)).then_inc(ada_c, 1)
            st.leave(KD)
            act.wait_ge(N1["sum"], 1)
            root(N1, ps[:, 6], n1["sq"][:, 0])
            norm_hi(N1, lambda k: g_hi[:, k], lambda k: n1["tmp"][:, k % 2], lambda k: ada1[:, k, 0:1])
            act.wait_ge(dft_in_s, 16)
            run(F_hi[:], F_raw[:], ACT.Copy).then_inc(dft_split["act"], 1)
            act.wait_ge(chan_in_s, 16)
            run(C_hi[:], C_raw[:], ACT.Copy).then_inc(dft_split["act"], 1)
            phase_end()

            def act_group(i, j):
                def pe(n):
                    act.wait_ge(pe_ft, j * 5 + n)

                def dve(n):
                    act.wait_ge(dve_ft, j * 8 + (n + 1))

                def stage(k):
                    if i is None:
                        return
                    if j is not None:
                        if k < 2:
                            pe(1)
                        else:
                            dve(5 + 2 * (k - 2))
                    if k < 2:
                        run(u_st[:, k], ps[:, k % 2], ACT.Copy).then_inc(ft_acc, 1)
                    else:
                        run(zf_st[:, k - 2], ps[:, k % 2], ACT.Silu).then_inc(ft_acc, 1)

                def hi(n, dst, src):
                    if j is not None:
                        pe(n)
                        run(dst, src, ACT.Copy).then_inc(act_ft, 1)

                def tail(m_):
                    if j is None:
                        return
                    pe(4 + m_)
                    run(o_sb[:], ps[:, 5 + 2 * m_, 0:256], ACT.Copy).then_inc(act_ft, 1)
                    dve(5 + 2 * m_)
                    run(row(y_hi, j * 2 + m_), yg[:], ACT.Copy).then_inc(act_ft, 1)

                hi(1, u_hi[:, 0], ps[:, 4])
                hi(1, u_hi[:, 1], ps[:, 5])
                if i is not None:
                    after(0)
                stage(0)
                hi(2, p_hi[:, 0], ps[:, 6])
                if i is not None:
                    after(1)
                stage(1)
                hi(3, p_hi[:, 1], ps[:, 7])
                if i is not None:
                    after(2)
                tail(0)
                stage(2)
                if i is not None:
                    after(3)
                tail(1)
                stage(3)

            st.enter(0, 4)
            act_group(0, None)
            st.leave(1)
            with act.Fori(0, GROUPS - 1) as j:
                st.enter(j, 4)
                act_group(j + 1, j)
            st.leave(GROUPS - 1)
            act_group(None, GROUPS - 1)

            def residual(R, trips, nb, src, sq, sums, ahead=True):
                def one(i):
                    for a in range(2):
                        for q in range(nb):
                            if ahead or not isinstance(i, int):
                                after(a * nb + q)
                        if sums:
                            square_one(R, i * 2 + a, src(i * 2 + a), sq, 2)
                if ahead:
                    with act.Fori(0, trips) as i:
                        st.enter(i, 2 * nb)
                        one(i)
                    st.leave(trips)
                else:
                    with act.Fori(0, trips - 1) as i:
                        st.enter(i, 2 * nb)
                        one(i)
                    st.leave(trips - 1)
                    one_last = trips - 1
                    for a in range(2):
                        if sums:
                            square_one(R, one_last * 2 + a, src(one_last * 2 + a), sq, 2)

            residual(RF, KD // 2, 2, lambda m_: row(x1, m_), n1["sq"][:, 0], True)
            act.wait_ge(NFIN["sum"], 1)
            root(NFIN, ps[:, 6], n1["sq"][:, 0])
            phase_end()
            for k in range(KD):
                act.wait_ge(RA["res"], k + 1)
                if k:
                    act.wait_ge(RA["add"], k)
                run(n2["sq"][:, 0], hb[:, k], ACT.Square).then_inc(RA["sq"], 1)

            def block_norm(N, n):
                act.wait_ge(N["sum"], 1)
                if n == TM:
                    root(N, ps[:, 6:8, 0:HALF], halves(n2["sq"][:, 0]))
                    norm_hi(N, lambda k: n_hi[:, k], lambda k: n2["tmp"][:, k % 2], lambda k: zero[:])
                else:
                    root(N, ps[:, 6], n2["sq"][:, 0, 0:T])
                    norm_hi(N, lambda k: n_hi[:, k, META:TM], lambda k: n2["tmp"][:, k % 2, 0:T],
                            lambda k: zero[:])

            def feed_forward(tags, last_R, n, last):
                c0 = TM - n
                for tag, count in zip(tags, FF_GROUPS):
                    S = ffn[tag]
                    with act.Fori(0, count) as i:
                        st.enter(i, 2)
                        after(0)
                        acc = ps[:, 0:2, 0:HALF] if n == TM else ps[:, 0]
                        dst = halves(sg[:]) if n == TM else sg[:, 0:n]
                        act.wait_ge(S["up"], i + 1)
                        run(dst, acc, ACT.Silu).then_inc(S["gate"], 1)
                        after(1)
                        act.wait_ge(S["up"], i + 2)
                        run(row(hid_hi, i)[:, c0:TM], hid[:, 0:n], ACT.Copy).then_inc(S["hi"], 1)
                    st.leave(count)
                    final = tag == tags[-1]
                    residual(last_R if final else RP[tag], KD // 2, 1,
                             lambda m_: row(hb, m_)[:, c0:TM], n2["sq"][:, 0, 0:n], final,
                             not (final and last))

            block_norm(NF1, TM)
            feed_forward(("f1a", "f1b", "f1c"), RD1, TM, False)
            block_norm(NMIX, TM)
            phase_end()

            with act.Fori(0, KD // 2) as i:
                st.enter(i, 14)
                own.enter(i, 2)

                def out_of(k, dst, func, bias):
                    n = TM if k < 6 else T
                    b0 = 2 * (k % 2)
                    acc = ps[:, b0:b0 + 2, 0:HALF] if n == TM else ps[:, b0]
                    run(halves(dst) if n == TM else dst, acc, func, bias=bias).then_inc(mx_acc, 1)

                def b_in(kind, a):
                    return col("b_in", i * 2 + (kind * KD + a))

                def dve(n):
                    act.wait_ge(mx_dve, i * 12 + n)

                for a in range(2):
                    after(a)
                    out_of(a, xpad[:, a, RW - 1:RW - 1 + TM], ACT.Identity, b_in(0, a))
                after(2)
                for a in range(2):
                    dve(1 + a)
                    run(xr_hi[:, a], xr[:, a], ACT.Copy).then_inc(mx_act, 1)
                out_of(2, gvs[:], ACT.Identity, b_in(2, 0))
                after(3)
                out_of(3, ggs[:], ACT.Sigmoid, b_in(3, 0))
                after(4)
                dve(5)
                out_of(4, gvs[:], ACT.Identity, b_in(2, 1))
                after(5)
                out_of(5, ggs[:], ACT.Sigmoid, b_in(3, 1))
                for a in range(2):
                    after(6 + a)
                    out_of(6 + a, yst[:, a], ACT.Gelu_apprx_tanh, b_in(1, a))
                for a in range(2):
                    for t in range(2):
                        after(8 + 2 * a + t)
                        out_of(8 + 2 * a + t, row(gate[:, t], i * 2 + a), ACT.Sigmoid, b_in(4 + t, a))
                after(12)
                for a in range(2):
                    last = run(halves(rr[:, a]), ps[:, 4 + 2 * a:6 + 2 * a, 0:HALF], ACT.Sigmoid,
                               bias=col("b_a", i * 2 + a))
                last.then_inc(mx_acc, 1)
                after(13)
                for a in range(2):
                    last = run(halves(ii[:, a]), ps[:, 2 * a:2 * a + 2, 0:HALF], ACT.Sigmoid,
                               bias=col("b_x", i * 2 + a))
                last.then_inc(mx_acc, 1)
                act.wait_ge(mx_acc, i * 14 + 16)
                for a in range(2):
                    own.link(run(pp[:, a], rr[:, a], ACT.Tanh, scale=rate(i * 2 + (KD + a))))
                    run(rr[:, a], rr[:, a], ACT.Exp, scale=rate(i * 2 + a)).then_inc(mx_act, 1)
                for a in range(2):
                    dve(7 + a)
                    run(pp[:, a], pp[:, a], ACT.Sqrt).then_inc(mx_act, 1)
                for a in range(2):
                    dve(9 + a)
                    run(row(a_hi, i * 2 + a), yst[:, a], ACT.Copy).then_inc(mx_act, 1)
            st.leave(KD // 2)
            own.leave(KD // 2)
            phase_end()

            act.wait_ge(ln_pe, 1)
            for k in range(KD):
                act.wait_ge(ln_dve, 2 + k)
                run(n2["sq"][:, 0, 0:T], cv[:, k], ACT.Square).then_inc(ln_act, 1)
            act.wait_ge(ln_dve, 2 + KD)
            act.wait_ge(ln_pe, 2)
            run(n2["sq"][:, 0, 0:T], ps[:, 7], ACT.Sqrt, bias=eps[:]).then_inc(ln_act, 1)
            for k in range(KD):
                act.wait_ge(ln_dve, 3 + KD + 2 * k)
                run(cv[:, k], cv[:, k], ACT.Silu, bias=col("ln_b", k)).then_inc(ln_act, 1)
                act.wait_ge(ln_act, KD + 2 + 2 * k)
                run(n_hi[:, k, 0:T], cv[:, k], ACT.Copy).then_inc(ln_act, 1)
            phase_end()

            with act.Fori(0, KD) as i:
                st.enter(i, 2)
                after(0)
                after(1)
                act.wait_ge(mg_dve, i * 3 + 3)
                run(row(mg_hi, i), mt[:, 0], ACT.Copy).then_inc(mg_act, 1)
            st.leave(KD)
            residual(RM, KD // 2, 1, lambda m_: row(hb, m_)[:, META:TM], n2["sq"][:, 0, 0:T], True)
            act.wait_ge(NF2["sum"], 1)
            phase_end()
            block_norm(NF2, T)
            feed_forward(("f2a", "f2b", "f2c"), RD2, T, True)
            act.wait_ge(NOUT["sum"], 1)
            root(NOUT, ps[:, 6], n2["sq"][:, 0, 0:T])

        @block.vector
        def _(dve):
            st = Stream()
            over = [0]
            own = Own(dve, own_s["dve"])
            v = nc.vector
            tt, ts, stt = v.tensor_tensor, v.tensor_scalar, v.scalar_tensor_tensor

            def phase_end():
                over[0] += 1
                dve.drain().then_inc(phase_over, 1)
                dve.wait_ge(phase_over, 3 * over[0])

            def cut(k):
                s, use = st.slot(k)
                dve.wait_ge(hi_ready[s], use + 1)
                tt(w_lo[:, s], w_raw[:, s], w_hi[:, s].bitcast(F32), ALU.subtract).then_inc(lo_ready[s], 1)

            def after(k):
                cut(k + 2)

            def sum_squares(R, n, acc, sq):
                for k in range(n):
                    dve.wait_ge(R["sq"], k + 1)
                    if k:
                        dve.wait_ge(R["add"], k)
                        tt(acc, acc, sq, ALU.add).then_inc(R["add"], 1)
                    else:
                        v.tensor_copy(acc, sq).then_inc(R["add"], 1)

            def norm_apply(N, src, gain, shift, tmp, rt_, hi, lo):
                dve.wait_ge(N["root"], 1)
                own.link(v.reciprocal(rt_, rt_))
                for k in range(KD + 1):
                    if k < KD:
                        if k > 1:
                            dve.wait_ge(N["lo"], k - 1)
                        stt(tmp(k), src(k), gain(k), rt_, ALU.mult, ALU.mult).then_inc(N["tmp"], 1)
                    if k:
                        dve.wait_ge(N["hi"], k)
                        stt(lo(k - 1), tmp(k - 1), shift(k - 1), hi(k - 1).bitcast(F32), ALU.add, ALU.subtract
                            ).then_inc(N["lo"], 1)

            def open_sums(R, acc, sq):
                v.memset(acc, 0.0).then_inc(R["add"], 1)
                v.memset(sq, 0.0).then_inc(R["sq"], 1)

            def add_square(R, m_, acc, sq):
                dve.wait_ge(R["sq"], m_ + 1)
                dve.wait_ge(R["add"], m_ + 1)
                tt(acc, acc, sq, ALU.add).then_inc(R["add"], 1)

            def close_sums(R, N, acc, sq):
                dve.wait_ge(R["sq"], KD + 1)
                dve.wait_ge(R["add"], KD + 1)
                tt(acc, acc, sq, ALU.add).then_inc(N["sum"], 1)

            for s in range(2):
                dve.sem_inc(lo_ready[s], 1)
            dve.sem_inc(RC["res"], 1)
            for R in (RF, RM, RD1, RD2, *RP.values()):
                dve.sem_inc(R["res"], 2)
            dve.sem_inc(dve_ft, 1)
            dve.sem_inc(mg_dve, 1)
            for tag in ffn:
                dve.sem_inc(ffn[tag]["up"], 1)
                dve.sem_inc(ffn[tag]["lo"], 1)

            v.memset(ones_d[:], 1.0 / D)
            v.memset(ones_h[:], 1.0 / P)
            v.memset(eps[:], EPS)
            v.memset(zero[:], 0.0).then_inc(consts_set, 1)
            dve.wait_ge(vec_in_s, 16)
            lb = vec[:, VEC["lb"]:VEC["lb"] + 4 * HEADS].rearrange("p (n c) -> p n c", n=2)
            own.link(tt(lbt[:, 0], lb[:, 0], lb[:, 1], ALU.max))
            tt(lbt[:, 1:3], lb, lbt[:, 0:1].broadcast_to([P, 2, 2 * HEADS]), ALU.subtract).then_inc(consts_set, 1)
            lam = vec[:, VEC["lam"]:VEC["lam"] + KD]
            own.link(ts(rgc[:, 0], lam, -1.0, None, ALU.mult))
            tt(rgc[:, 0], rgc[:, 0], lam, ALU.max).then_inc(consts_set, 1)
            dve.wait_ge(small["act"], 2)
            tt(c_lo[:], csil[:], c_hi[:].bitcast(F32), ALU.subtract).then_inc(consts_set, 1)
            cut(0)
            cut(1)
            dve.wait_ge(small["act"], 3)
            own.link(tt(lbt[:, 3], lbt[:, 1], lbt[:, 2], ALU.add))
            own.link(v.reciprocal(lbt[:, 3], lbt[:, 3]))
            own.link(tt(lbt[:, 4], lbt[:, 1], lbt[:, 3], ALU.mult))
            own.mark(ts(lbt[:, 5], lbt[:, 4], -1.0, 1.0, ALU.mult, ALU.add))
            dve.wait_ge(small["act"], 4)
            z, w, w2, p_ = rgc[:, 1], rgc[:, 2], rgc[:, 3], rgc[:, 4]
            own.link(ts(w, z, 2.0, None, ALU.add))
            own.link(v.reciprocal(w, w))
            own.link(tt(w, w, z, ALU.mult))
            own.link(tt(w2, w, w, ALU.mult))
            own.link(ts(p_, w2, 1.0 / 19, None, ALU.mult))
            for n in range(17, 1, -2):
                own.link(stt(p_, p_, 1.0 / n, w2, ALU.add, ALU.mult))
            own.link(stt(p_, p_, 1.0, w, ALU.add, ALU.mult))
            own.link(ts(rgc[:, 5], lam, -1.0, 0.0, ALU.mult, ALU.max))
            own.link(stt(p_, p_, 2.0, rgc[:, 5], ALU.mult, ALU.add))
            ts(rgc[:, 6], p_, -8.0, None, ALU.mult)
            own.mark(ts(rgc[:, 7], p_, 8.0, None, ALU.mult))
            sum_squares(R0, KD, st_sum[:, 0], st_sq[:])
            dve.wait_ge(R0["add"], KD)
            sum_squares(R0C, KD, st_sum[:, 1, 0:TC], st_sq[:, 0:TC])
            dve.wait_ge(R0C["add"], KD)
            dve.sem_inc(N0["sum"], 1)
            dve.sem_inc(N0C["sum"], 1)
            with dve.Fori(0, KD) as i:
                st.enter(i, 2)
                after(0)
                after(1)
            st.leave(KD)
            st.wait_done(dve, -2)
            st.wait_done(dve, -1)
            own.link(tt(ada0[:, 0:16], ps[:, 7, 0:32].rearrange("p (m n) -> p m n", n=2),
                        vec[:, VEC["ada_b0"]:VEC["ada_b0"] + 16].unsqueeze(2).broadcast_to([P, 16, 2]), ALU.add))
            g0 = vec[:, VEC["norm_g0"]:VEC["norm_g0"] + KD]
            for n in range(2):
                own.mark(stt(scale[:, n], ada0[:, 8:16, n:n + 1].rearrange("p k n -> p (k n)"), 1.0, g0,
                             ALU.add, ALU.mult))
            own.wait()
            norm_apply(N0, lambda k: x0[:, k], lambda k: scale[:, 0, k:k + 1], lambda k: ada0[:, k, 0:1],
                       lambda k: st_tmp[:, k % 2], st_sq[:], lambda k: h_hi[:, k], lambda k: h_lo[:, k])
            norm_apply(N0C, lambda k: xc[:, k], lambda k: scale[:, 1, k:k + 1], lambda k: ada0[:, k, 1:2],
                       lambda k: st_tmp[:, k % 2, 0:TC], st_sq[:, 0:TC], lambda k: hc_hi[:, k], lambda k: hc_lo[:, k])
            dve.wait_ge(const_in_s, 16)
            phase_end()

            def tree(l):
                if l == 0:
                    return f_st[:]
                at = TA - (TA >> (l - 1))
                return f_tree[:, :, at:at + (TA >> l)]

            def dve_head(i, j):
                def pe(n):
                    dve.wait_ge(pe_scan, j * PE_SCAN + n)

                def mine(n):
                    dve.wait_ge(dve_scan, j * DVE_SCAN + n)

                def next_block(k):
                    if i is not None:
                        after(k)

                def prepare():
                    dve.wait_ge(acc_free, j * 6 + 7)
                    for d in range(2):
                        own.mark(ts(f_st[:, d], f_st[:, d], lbt[:, 5, ds(j + d * HEADS, 1)],
                                    lbt[:, 4, ds(j + d * HEADS, 1)], ALU.mult, ALU.add))
                    own.wait()
                    own.mark(ts(K[:], f_st[:], -1.0, 1.0, ALU.mult, ALU.add))
                    tt(Q[:], q_st[:].unsqueeze(1).broadcast_to([P, 2, T]), f_st[:, :, TC:TA], ALU.mult)
                    v.tensor_copy(z_cur[:], z_st[:])
                    own.wait()
                    tt(ksum[:], K[:, 0, TC:TA], K[:, 1, TC:TA], ALU.add).then_inc(dve_scan, 1)

                def place(l, bank, signal=False):
                    last = v.copy_predicated(ST[:], masks[:, l].unsqueeze(1).broadcast_to([P, TT, P]),
                                             ps[:, bank].rearrange("p (t s) -> p t s", t=TT))
                    if signal:
                        last.then_inc(dve_scan, 1)
                    else:
                        own.mark(last)

                def merge(l):
                    n = 2 ** l
                    prev = tree(l).rearrange("p d (m h) -> p d m h", h=2)
                    if l == 0:
                        pe(2)
                    own.mark(tt(tree(l + 1), prev[:, :, :, 0], prev[:, :, :, 1], ALU.mult))
                    if l == 0:
                        place(LEVELS, 4)
                    own.wait()
                    pe((3, 4, 6, 7, 8, 9, 10)[l])
                    mine(1 + l)
                    for t, t0, size in ((Q, TC, T), (K, 0, TA)):
                        for d in range(2):
                            half = 1 - d if t is Q else d
                            part = t[:, d].rearrange("p (m h n) -> p m h n", h=2, n=n)[:, :, half]
                            by = prev[:, d, t0 // (2 * n):, 1 - half].unsqueeze(2).broadcast_to(
                                [P, size // (2 * n), n])
                            last = tt(part, part, by, ALU.mult)
                    last.then_inc(dve_scan, 1)
                    place(l, 5 - l % 2, l == LEVELS - 1)

                def passed(g_):
                    pe((12, 14, 16)[g_])
                    whole_tile = tree(LEVELS)
                    acc = ps[:, 4 + g_ % 2].rearrange("p (x c) -> p x c", c=P)
                    for x, n in enumerate(range(2 * g_, min(2 * g_ + 2, 5))):
                        if n == 0:
                            own.mark(v.tensor_copy(states[:, 0], acc[:, 0:2]))
                        else:
                            if x or g_ == 0:
                                own.wait()
                            for d in range(2):
                                tile_ = ORDER[d][n]
                                last = stt(states[:, n, d], states[:, n - 1, d], whole_tile[:, d, tile_:tile_ + 1],
                                           acc[:, 2 * x + d], ALU.mult, ALU.add)
                                if d == 1 and x == min(2, 5 - 2 * g_) - 1:
                                    last.then_inc(dve_scan, 1)
                                else:
                                    own.mark(last)

                def finish():
                    dve.wait_ge(act_scan, j * ACT_SCAN + 7)
                    own.link(v.reciprocal(rt[:], rt[:]))
                    own.link(stt(ytmp[:], ps[:, 7], col("hg_g", 0), rt[:], ALU.mult, ALU.mult))
                    tt(ytmp[:], ytmp[:], z_cur[:], ALU.mult).then_inc(dve_scan, 1)
                    dve.wait_ge(act_scan, j * ACT_SCAN + 8)
                    tt(row(y_lo, j), ytmp[:], row(y_hi, j).bitcast(F32), ALU.subtract).then_inc(dve_scan, 1)

                if j is None:
                    for k in range(6):
                        after(k)
                    return
                prepare()
                next_block(0)
                merge(0)
                merge(1)
                merge(2)
                next_block(1)
                merge(3)
                merge(4)
                merge(5)
                next_block(2)
                merge(6)
                passed(0)
                next_block(3)
                mine(10)
                passed(1)
                mine(11)
                passed(2)
                next_block(4)
                next_block(5)
                finish()

            st.enter(0, 6)
            dve_head(0, None)
            st.leave(1)
            with dve.Fori(0, HEADS - 1) as j:
                st.enter(j, 6)
                own.enter(j, PER["head"])
                dve_head(j + 1, j)
            st.leave(HEADS - 1)
            own.leave(HEADS - 1)
            dve_head(None, HEADS - 1)
            phase_end()

            dve.wait_ge(x1_in_s, 16)
            open_sums(RC, n1["sum"][:, 0], n1["sq"][:, 0])
            with dve.Fori(0, KD) as i:
                st.enter(i, 4)
                after(0)
                after(1)
                after(2)
                st.wait_done(dve, 2)
                dve.wait_ge(ada_c, i * 2 + 3)
                stt(row(x1, i), ps[:, 0], row(ada0, i + 16)[:, 0:1], row(x1, i), ALU.mult, ALU.add
                    ).then_inc(RC["res"], 1)
                add_square(RC, i, n1["sum"][:, 0], n1["sq"][:, 0])
                after(3)
            st.leave(KD)
            close_sums(RC, N1, n1["sum"][:, 0], n1["sq"][:, 0])
            dve.wait_ge(ada_c, 2 + 2 * KD)
            own.link(stt(scale[:, 2], ada1[:, 8:16, 0:1].rearrange("p k n -> p (k n)"), 1.0,
                         vec[:, VEC["norm_g1"]:VEC["norm_g1"] + KD], ALU.add, ALU.mult))
            norm_apply(N1, lambda k: x1[:, k], lambda k: scale[:, 2, k:k + 1], lambda k: ada1[:, k, 0:1],
                       lambda k: n1["tmp"][:, k % 2], n1["sq"][:, 0], lambda k: g_hi[:, k], lambda k: g_lo[:, k])
            dve.wait_ge(dft_split["act"], 1)
            tt(F_lo[:], F_raw[:], F_hi[:].bitcast(F32), ALU.subtract).then_inc(dft_split["dve"], 1)
            dve.wait_ge(dft_split["act"], 2)
            flat = "p a b c d -> p (a b c d)"
            tt(C_lo[:].rearrange(flat), C_raw[:].rearrange(flat), C_hi[:].rearrange(flat).bitcast(F32),
               ALU.subtract).then_inc(dft_split["dve"], 1)
            phase_end()

            def dve_group(i, j):
                def lo(n, dst, src, hi):
                    if j is not None:
                        dve.wait_ge(act_ft, j * 8 + n)
                        tt(dst, src, hi.bitcast(F32), ALU.subtract).then_inc(dve_ft, 1)

                def next_block(k):
                    if i is not None:
                        after(k)

                def mirror(m_):
                    if j is None:
                        return
                    e = ps[:, 4 + 2 * m_]
                    dve.wait_ge(act_ft, j * 8 + (5 + 2 * m_))
                    dve.wait_ge(ft_acc, j * 4 + 6)
                    tt(yf[:, 1:256], e[:, 1:256], o_sb[:, 1:256], ALU.subtract)
                    tt(yf[:, 511:256:-1], e[:, 1:256], o_sb[:, 1:256], ALU.add)
                    own.link(v.tensor_copy(yf[:, 0:512:256], e[:, 0:512:256]))
                    dve.wait_ge(dve_ft, j * 8 + (5 + 2 * m_))
                    tt(yg[:], yf[:], zf_st[:, m_], ALU.mult).then_inc(dve_ft, 1)
                    dve.wait_ge(act_ft, j * 8 + (6 + 2 * m_))
                    tt(row(y_lo, j * 2 + m_), yg[:], row(y_hi, j * 2 + m_).bitcast(F32), ALU.subtract
                       ).then_inc(dve_ft, 1)

                lo(1, u_lo[:, 0], ps[:, 4], u_hi[:, 0])
                lo(2, u_lo[:, 1], ps[:, 5], u_hi[:, 1])
                next_block(0)
                lo(3, p_lo[:, 0], ps[:, 6], p_hi[:, 0])
                next_block(1)
                lo(4, p_lo[:, 1], ps[:, 7], p_hi[:, 1])
                next_block(2)
                mirror(0)
                next_block(3)
                mirror(1)

            st.enter(0, 4)
            dve_group(0, None)
            st.leave(1)
            with dve.Fori(0, GROUPS - 1) as j:
                st.enter(j, 4)
                own.enter(j, 2)
                dve_group(j + 1, j)
            st.leave(GROUPS - 1)
            own.leave(GROUPS - 1)
            dve_group(None, GROUPS - 1)

            def residual(R, trips, nb, out_row, factor, n, sums, N=None, ahead=True):
                if sums:
                    open_sums(R, *sums)

                def one(i, cuts):
                    for a in range(2):
                        for q in range(nb):
                            if cuts:
                                after(a * nb + q)
                        st.wait_done(dve, a * nb + nb - 1)
                        r_ = out_row(i * 2 + a)
                        acc = ps[:, 2 * a:2 * a + 2, 0:HALF] if n == TM else ps[:, 2 * a]
                        r_ = halves(r_) if n == TM else r_
                        stt(r_, acc, factor(i * 2 + a), r_, ALU.mult, ALU.add).then_inc(R["res"], 1)
                        if sums:
                            add_square(R, i * 2 + a, *sums)

                n_loop = trips if ahead else trips - 1
                with dve.Fori(0, n_loop) as i:
                    st.enter(i, 2 * nb)
                    one(i, True)
                st.leave(n_loop)
                if not ahead:
                    st.enter(0, 2 * nb)
                    one(trips - 1, False)
                    st.leave(1)
                if sums:
                    close_sums(R, N, *sums)

            residual(RF, KD // 2, 2, lambda m_: row(x1, m_), lambda m_: row(ada1, m_ + 16)[:, 0:1], T,
                     (n1["sum"][:, 0], n1["sq"][:, 0]), NFIN)
            phase_end()
            dve.wait_ge(NFIN["root"], 1)
            own.link(v.reciprocal(n1["sq"][:, 0], n1["sq"][:, 0]))
            dve.wait_ge(meta_in_s, 16)
            for k in range(KD):
                stt(hb[:, k, META:TM], x1[:, k], col("final_g", k), n1["sq"][:, 0], ALU.mult, ALU.mult
                    ).then_inc(RA["res"], 1)
            sum_squares(RA, KD, n2["sum"][:, 0], n2["sq"][:, 0])
            dve.wait_ge(RA["add"], KD)
            dve.sem_inc(NF1["sum"], 1)

            def block_norm(N, name, n):
                c0 = TM - n
                norm_apply(N, lambda k: hb[:, k, c0:TM], lambda k: col(name, k), lambda k: zero[:],
                           lambda k: n2["tmp"][:, k % 2, 0:n], n2["sq"][:, 0, 0:n],
                           lambda k: n_hi[:, k, c0:TM], lambda k: n_lo[:, k, c0:TM])

            def feed_forward(tags, last_R, N, n, last):
                c0 = TM - n
                for tag, count in zip(tags, FF_GROUPS):
                    S = ffn[tag]
                    with dve.Fori(0, count) as i:
                        st.enter(i, 2)
                        after(0)
                        after(1)
                        st.wait_done(dve, 1)
                        dve.wait_ge(S["gate"], i + 2)
                        dve.wait_ge(S["lo"], i + 1)
                        acc = ps[:, 2:4, 0:HALF] if n == TM else ps[:, 2]
                        a, b_ = (halves(hid[:]), halves(sg[:])) if n == TM else (hid[:, 0:n], sg[:, 0:n])
                        tt(a, acc, b_, ALU.mult).then_inc(S["up"], 1)
                        dve.wait_ge(S["hi"], i + 1)
                        tt(row(hid_lo, i)[:, c0:TM], hid[:, 0:n], row(hid_hi, i)[:, c0:TM].bitcast(F32),
                           ALU.subtract).then_inc(S["lo"], 1)
                    st.leave(count)
                    final = tag == tags[-1]
                    sums = (n2["sum"][:, 0, 0:n], n2["sq"][:, 0, 0:n]) if final else None
                    residual(last_R if final else RP[tag], KD // 2, 1, lambda m_: row(hb, m_)[:, c0:TM],
                             lambda m_: 0.5, n, sums, N, not (final and last))

            block_norm(NF1, "ffn1_g", TM)
            feed_forward(("f1a", "f1b", "f1c"), RD1, NMIX, TM, False)
            block_norm(NMIX, "mix_g", TM)
            phase_end()

            own.mark(v.memset(vpad[:, 0:DW - 1], 0.0))
            own.link(v.memset(xpad[:, :, 0:RW - 1], 0.0))
            with dve.Fori(0, KD // 2) as i:
                st.enter(i, 14)
                own.enter(i, PER["mix"])

                def staged(k):
                    dve.wait_ge(mx_acc, i * 14 + (k + 3))

                def mine(n):
                    dve.wait_ge(mx_dve, i * 12 + n)

                def actv(n):
                    dve.wait_ge(mx_act, i * 8 + n)

                def tap(a, t):
                    dst = row(cv, i * 2 + a)
                    src = vpad[:, META + t:META + t + T]
                    w_ = col("dw", i * 2 + (t * KD + a))
                    if t == 0:
                        own.link(ts(dst, src, w_, col("dwb", i * 2 + a), ALU.mult, ALU.add))
                    else:
                        own.link(stt(dst, src, w_, dst, ALU.mult, ALU.add))

                def product(a):
                    staged(3 + 2 * a)
                    tt(vpad[:, DW - 1:DW - 1 + TM], gvs[:], ggs[:], ALU.mult).then_inc(mx_dve, 1)
                    mine(5 + a)

                after(0)
                after(1)
                for a in range(2):
                    staged(a)
                    for t in range(RW):
                        src = xpad[:, a, t:t + TM]
                        w_ = col("rw", i * 2 + (t * KD + a))
                        if t == 0:
                            own.link(ts(xr[:, a], src, w_, col("rb", i * 2 + a), ALU.mult, ALU.add))
                        elif t < RW - 1:
                            own.link(stt(xr[:, a], src, w_, xr[:, a], ALU.mult, ALU.add))
                        else:
                            stt(xr[:, a], src, w_, xr[:, a], ALU.mult, ALU.add).then_inc(mx_dve, 1)
                after(2)
                for a in range(2):
                    actv(1 + a)
                    tt(xr_lo[:, a], xr[:, a], xr_hi[:, a].bitcast(F32), ALU.subtract).then_inc(mx_dve, 1)
                after(3)
                product(0)
                taps = [(0, t) for t in range(DW)]
                for k, count in ((4, 5), (5, 5), (6, 6), (7, 6), (8, 7)):
                    for _ in range(count):
                        if taps:
                            tap(*taps.pop(0))
                    after(k)
                while taps:
                    tap(*taps.pop(0))
                product(1)
                taps = [(1, t) for t in range(DW)]
                for k, count in ((9, 6), (10, 7), (11, 7), (12, 6), (13, 5)):
                    after(k)
                    for _ in range(count):
                        tap(*taps.pop(0))
                for a in range(2):
                    actv(3 + a)
                    own.mark(tt(ii[:, a], ii[:, a], xr[:, a], ALU.mult))
                    own.link(ts(dd[:], pp[:, a], 1.0, None, ALU.add))
                    own.link(v.reciprocal(dd[:], dd[:]))
                    own.link(stt(pp[:, a], pp[:, a], 2.0, dd[:], ALU.mult, ALU.mult))
                    ts(pp[:, a], pp[:, a], 2.0 ** -100, None, ALU.max).then_inc(mx_dve, 1)
                for a in range(2):
                    actv(5 + a)
                    own.link(tt(ii[:, a], ii[:, a], pp[:, a], ALU.mult))
                    own.link(v.tensor_tensor_scan(pp[:, a], rr[:, a], ii[:, a], 0.0, ALU.mult, ALU.add))
                    tt(yst[:, a], yst[:, a], pp[:, a, META:TM], ALU.mult).then_inc(mx_dve, 1)
                for a in range(2):
                    actv(7 + a)
                    tt(row(a_lo, i * 2 + a), yst[:, a], row(a_hi, i * 2 + a).bitcast(F32), ALU.subtract
                       ).then_inc(mx_dve, 1)
            st.leave(KD // 2)
            own.leave(KD // 2)
            phase_end()

            lsum, lsq = n2["sum"][:, 0, 0:T], n2["sq"][:, 0, 0:T]
            for k in range(KD):
                if k == 0:
                    own.link(v.tensor_copy(lsum, cv[:, 0]))
                elif k < KD - 1:
                    own.link(tt(lsum, lsum, cv[:, k], ALU.add))
                else:
                    tt(lsum, lsum, cv[:, k], ALU.add).then_inc(ln_dve, 1)
            dve.wait_ge(ln_pe, 1)
            for k in range(KD):
                tt(cv[:, k], cv[:, k], ps[:, 6], ALU.subtract).then_inc(ln_dve, 1)
                dve.wait_ge(ln_act, k + 1)
                if k == 0:
                    own.link(v.tensor_copy(lsum, lsq))
                elif k < KD - 1:
                    own.link(tt(lsum, lsum, lsq, ALU.add))
                else:
                    tt(lsum, lsum, lsq, ALU.add).then_inc(ln_dve, 1)
            dve.wait_ge(ln_act, KD + 1)
            own.link(v.reciprocal(lsq, lsq))
            for k in range(KD):
                stt(cv[:, k], cv[:, k], col("ln_g", k), lsq, ALU.mult, ALU.mult).then_inc(ln_dve, 1)
                dve.wait_ge(ln_act, KD + 3 + 2 * k)
                tt(n_lo[:, k, 0:T], cv[:, k], n_hi[:, k, 0:T].bitcast(F32), ALU.subtract).then_inc(ln_dve, 1)
            phase_end()

            with dve.Fori(0, KD) as i:
                st.enter(i, 2)
                own.enter(i, 1)
                after(0)
                after(1)
                st.wait_done(dve, 0)
                dve.wait_ge(mg_dve, i * 3 + 1)
                own.mark(tt(mt[:, 0], ps[:, 0], row(gate[:, 0], i), ALU.mult))
                st.wait_done(dve, 1)
                stt(mt[:, 1], ps[:, 2], col("cpb", i), row(gate[:, 1], i), ALU.add, ALU.mult).then_inc(mg_dve, 1)
                dve.wait_ge(mg_dve, i * 3 + 2)
                tt(mt[:, 0], mt[:, 0], mt[:, 1], ALU.add).then_inc(mg_dve, 1)
                dve.wait_ge(mg_act, i + 1)
                tt(row(mg_lo, i), mt[:, 0], row(mg_hi, i).bitcast(F32), ALU.subtract).then_inc(mg_dve, 1)
            st.leave(KD)
            own.leave(KD)
            residual(RM, KD // 2, 1, lambda m_: row(hb, m_)[:, META:TM], lambda m_: 1.0, T,
                     (n2["sum"][:, 0, 0:T], n2["sq"][:, 0, 0:T]), NF2)
            phase_end()
            block_norm(NF2, "ffn2_g", T)
            feed_forward(("f2a", "f2b", "f2c"), RD2, NOUT, T, True)
            dve.wait_ge(NOUT["root"], 1)
            own.link(v.reciprocal(n2["sq"][:, 0, 0:T], n2["sq"][:, 0, 0:T]))
            for k in range(KD):
                stt(fin[:, k], hb[:, k, META:TM], col("out_g", k), n2["sq"][:, 0, 0:T], ALU.mult, ALU.mult
                    ).then_inc(NOUT["lo"], 1)


def _cols(a):
    return np.asarray(a).reshape(-1, P).T


def _blocks(w, ks=None):
    w = np.asarray(w)
    k, m = w.shape[0] // P, w.shape[1] // P
    tiles = w.reshape(k, P, m, P).transpose(2, 1, 0, 3)
    groups, at = [], 0
    for n in ks or (KD,) * (k // KD):
        part = tiles[:, :, at:at + n]
        if n < KD:
            part = np.concatenate([part, np.zeros((m, P, KD - n, P), w.dtype)], axis=2)
        groups.append(part.reshape(m, P, BLK))
        at += n
    return groups


def _stream(i):
    out = []
    a0, a1 = _blocks(i["ada_w"][0])[0], _blocks(i["ada_w"][1])[0]
    out += list(a0[:16])
    hg = _blocks(i["hg_w_in"][0])[0].reshape(5, HEADS, P, BLK)
    for h in range(HEADS):
        out += [*hg[:, h], a1[h]]
    wo = _blocks(i["hg_w_out"][0])
    for m in range(KD):
        out += [a0[16 + m], wo[0][m], wo[1][m], a1[16 + m]]
    fi = _blocks(i["ft_w_in"][0])[0].reshape(2, HEADS, P, BLK)
    for g in range(GROUPS):
        out += [fi[0, 2 * g], fi[0, 2 * g + 1], fi[1, 2 * g], fi[1, 2 * g + 1]]
    fo = _blocks(i["ft_w_out"][0])
    for m in range(KD):
        out += [fo[0][m], fo[1][m]]

    def feed_forward(name):
        gu, down = _blocks(i[name + "_w_gu_2"][0])[0], _blocks(i[name + "_w_down_2"][0], FF_GROUPS)
        blocks, at = [], 0
        for n, d in zip(FF_GROUPS, down):
            for j in range(at, at + n):
                blocks += [gu[j], gu[FT + j]]
            blocks += list(d)
            at += n
        return blocks

    out += feed_forward("ffn1")
    wi = _blocks(i["w_in_2"][0])[0].reshape(6, KD, P, BLK)
    heads = []
    for name in ("rg_w_a_2", "rg_w_x_2"):
        w = np.asarray(i[name][0]).reshape(4, 2, P, 2, P).transpose(0, 2, 3, 1, 4).reshape(4, P, 4 * P)
        heads.append(np.concatenate([w, np.zeros_like(w)], axis=2))
    for n in range(KD // 2):
        a, b = 2 * n, 2 * n + 1
        out += [wi[0, a], wi[0, b], wi[2, a], wi[3, a], wi[2, b], wi[3, b], wi[1, a], wi[1, b],
                wi[4, a], wi[5, a], wi[4, b], wi[5, b], heads[0][n], heads[1][n]]
    rn, cp = _blocks(i["rnn_w_proj_2"][0])[0], _blocks(i["conv_w_proj_2"][0])[0]
    for m in range(KD):
        out += [rn[m], cp[m]]
    out += list(_blocks(i["w_out_2"][0])[0])
    out += feed_forward("ffn2")
    return np.stack(out)


def _vectors(i):
    c = np.stack([_cols(i["c"][0]), _cols(i["c_ctx"])], axis=2).reshape(P, 2 * KD)
    lb = np.asarray(i["hg_lb_logits"]).reshape(2, 2, HEADS, P).transpose(3, 0, 1, 2).reshape(P, -1)
    parts = [c, _cols(i["ada_b"][0]), _cols(i["ada_b"][1]), _cols(i["norm_g"][0]), _cols(i["norm_g"][1]), lb,
             _cols(i["hg_norm_g"][0]), _cols(i["final_g"]), _cols(i["ffn1_norm_2"][0]), _cols(i["mix_norm_2"][0]),
             _cols(i["b_in_2"][0]), _cols(i["rnn_conv_w_2"][0]), _cols(i["rnn_conv_b_2"][0]),
             _cols(i["rg_b_a_2"][0]), _cols(i["rg_b_x_2"][0]), _cols(i["rg_lambda_2"][0]),
             _cols(i["conv_dw_w_2"][0]), _cols(i["conv_dw_b_2"][0]), _cols(i["conv_ln_g_2"][0]),
             _cols(i["conv_ln_b_2"][0]), _cols(i["conv_b_proj_2"][0]), _cols(i["ffn2_norm_2"][0]),
             _cols(i["final_norm_2"])]
    return np.ascontiguousarray(np.concatenate(parts, axis=1))


def _turned(a):
    a = np.asarray(a)
    return np.ascontiguousarray(a.reshape(a.shape[0], KD, P).transpose(2, 1, 0))


def _tables():
    s, t = np.arange(P)[:, None], np.arange(P)[None, :]
    masks = [(s // (2 * n) == t // (2 * n)) & (s // n != t // n) for n in (2 ** l for l in range(LEVELS))]
    masks = np.stack(masks + [s == t], axis=1).astype(np.int32)
    tok = np.arange(T)[:, None]
    seq = np.concatenate([np.cos(2 * np.pi * (tok * np.arange(257)[None] % T) / T),
                          np.sin(2 * np.pi * (tok * np.arange(1, 256)[None] % T) / T)], axis=1) / np.sqrt(T)
    seq = seq.reshape(TT, P, T).transpose(1, 0, 2).astype(np.float32)
    ch = np.arange(256)
    ang = 2 * np.pi * (ch[:, None] * ch[None] % 256) / 256
    chan = np.stack([np.cos(ang), np.sin(ang)]) / np.sqrt(256)
    chan = chan.reshape(2, 2, P, 2, P).transpose(2, 0, 1, 3, 4).astype(np.float32)
    return masks, np.eye(P, dtype=np.float32), np.ascontiguousarray(seq), np.ascontiguousarray(chan)


def kernel(**inputs):
    import concourse.bacc as _bacc
    from concourse.bass_utils import run_bass_kernel_spmd as _run

    nc = _bacc.Bacc("TRN2", target_bir_lowering=False, num_devices=1)
    i = {k: np.asarray(v) for k, v in inputs.items()}
    masks, ident, seq, chan = _tables()
    given = {"weights": _stream(i), "x": _turned(i["x"][0]), "ctx": _turned(i["ctx"][0]),
             "meta": _turned(i["meta_tokens_2"]), "vectors": _vectors(i), "masks": masks,
             "identity": ident, "seq_dft": seq, "chan_dft": chan}
    arrays, args = {}, []
    for name, a in given.items():
        arrays[f"in_{name}_dram"] = a
        args.append(nc.dram_tensor(f"in_{name}_dram", a.shape, mybir.dt.from_np(a.dtype), kind="ExternalInput").ap())
    args.append(nc.dram_tensor("out_0_dram", (P, KD, T), F32, kind="ExternalOutput").ap())
    program(nc, *args)
    r = _run(nc, [arrays], core_ids=[0])
    return np.ascontiguousarray(r.results[0]["out_0_dram"].transpose(2, 1, 0).reshape(1, T, D))
```

```python
from contextlib import ExitStack

import numpy as np

import concourse.bass as bass
from concourse import mybir

F32 = mybir.dt.float32
F32R = mybir.dt.float32r
I32 = mybir.dt.int32
ALU = mybir.AluOpType
ACT = mybir.ActivationFunctionType
ds = bass.ds

P = 128
D = 1024
KD = D // P
E = 2048
HEADS = E // P
T = 512
TT = T // P
TC = 256
CT = TC // P
TA = TC + T
AT = TA // P
GROUPS = 8
META = 16
TM = META + T
HALF = TM // 2
DFF = 2816
FT = DFF // P
FF_GROUPS = (8, 8, 6)
DW = 31
RW = 4
EPS = 1e-6
LEVELS = 7
BLK = KD * P
BF = 258

_sizes = [("c", 2 * KD), ("ada_b0", 16), ("gate_b", 16), ("ada_b1", 16), ("norm_g0", KD), ("norm_g1", KD),
          ("lb", 2 * 2 * HEADS), ("hg_g", 1), ("final_g", KD), ("ffn1_g", KD), ("mix_g", KD),
          ("b_in", 48), ("rw", RW * KD), ("rb", KD), ("b_a", KD), ("b_x", KD), ("lam", KD),
          ("dw", DW * KD), ("dwb", KD), ("ln_g", KD), ("ln_b", KD), ("cpb", KD), ("ffn2_g", KD),
          ("out_g", KD)]
VEC = {}
_at = 0
for _n, _s in _sizes:
    VEC[_n] = _at
    _at += _s
NVEC = _at


PER = {"head": 25, "mix": 72}

ORDER = ((0, 1, 2, 3, 4), (1, 0, 5, 4, 3))


class Own:

    def __init__(self, eng, sem):
        self.eng, self.sem, self.base, self.i, self.per, self.n = eng, sem, 0, 0, 0, 0

    def mark(self, instruction):
        instruction.then_inc(self.sem, 1)
        self.n += 1

    def wait(self):
        self.eng.wait_ge(self.sem, self.i * self.per + self.base + self.n)

    def link(self, instruction):
        self.mark(instruction)
        self.wait()

    def enter(self, i, per):
        self.base += self.n
        self.n, self.i, self.per = 0, i, per

    def leave(self, trips):
        assert self.n == self.per, f"{self.sem.name}: {self.n} signals an iteration, not {self.per}"
        self.base += trips * self.per
        self.n, self.i, self.per = 0, 0, 0


class Region:

    def __init__(self, nc, start):
        self.nc, self.at, self.start = nc, start, start

    def take(self, name, shape, dt=F32):
        size = int(np.prod(shape[1:])) * 4
        tensor = self.nc.alloc_sbuf_tensor_at(name, shape, dt, offset=self.at)
        self.at += (size + 31) // 32 * 32
        return tensor

    def over(self):
        return Region(self.nc, self.at)


def halves(ap):
    return ap.rearrange("p (a b) -> p a b", a=2)


def program(nc, wts, ada_in, gate_in, x_in, ctx_in, meta_in, vec_in, mask_in, ident_in, dft_in, chan_in, out):
    nblocks = wts.shape[0]
    with ExitStack() as top:
        def sem(name):
            return top.enter_context(nc.semaphore(name))

        g = Region(nc, (nc.sbuf_base + 63) // 64 * 64)
        w_raw = g.take("w_raw", [P, 2, BLK])
        w_hi = g.take("w_hi", [P, 2, BLK], F32R)
        w_lo = g.take("w_lo", [P, 2, BLK], F32R)
        vec = g.take("vec", [P, NVEC])
        ones_d = g.take("ones_d", [P, P])
        ones_h = g.take("ones_h", [P, P])
        ident = g.take("ident", [P, P])
        eps = g.take("eps", [P, 1])
        zero = g.take("zero", [P, 1])
        tiny = g.take("tiny", [P, 1])
        ada0 = g.take("ada0", [P, 16, 2])
        ada1 = g.take("ada1", [P, 16, 2])
        gates = g.take("gates", [P, 16, 2])
        scale = g.take("scale", [P, 3, KD])
        csil = g.take("csil", [P, KD, 2])
        c_hi = g.take("c_hi", [P, KD, 2], F32R)
        c_lo = g.take("c_lo", [P, KD, 2], F32R)
        lbt = g.take("lbt", [P, 6, 2 * HEADS])
        rgc = g.take("rgc", [P, 8, KD])
        r = g.over()
        x0 = r.take("x0", [P, KD, T])
        xc = r.take("xc", [P, KD, TC])
        st_sum, st_sq = r.take("st_sum", [P, 2, T]), r.take("st_sq", [P, T])
        st_tmp, st_tmpc = r.take("st_tmp", [P, 2, T]), r.take("st_tmpc", [P, 3, TC])
        r_tail = r.over()
        r = g.over()
        y_hi = r.take("y_hi", [P, HEADS, T], F32R)
        y_lo = r.take("y_lo", [P, HEADS, T], F32R)
        h = r.over()
        h_hi, h_lo = h.take("h_hi", [P, KD, T], F32R), h.take("h_lo", [P, KD, T], F32R)
        hc_hi, hc_lo = h.take("hc_hi", [P, KD, TC], F32R), h.take("hc_lo", [P, KD, TC], F32R)
        h_tail = h.over()
        q_st = h.take("q_st", [P, T])
        f_st = h.take("f_st", [P, 2, TA])
        v_st = h.take("v_st", [P, TA])
        z_st = h.take("z_st", [P, T])
        z_cur = h.take("z_cur", [P, T])
        Q = h.take("Q", [P, 2, T])
        K = h.take("K", [P, 2, TA])
        ksum = h.take("ksum", [P, T])
        f_tree = h.take("f_tree", [P, 2, TA])
        V = h.take("V", [P, AT, P])
        KT = h.take("KT", [P, 4, P])
        ST = h.take("ST", [P, TT, P])
        states = h.take("states", [P, 5, 2, P])
        osq, rt, ytmp = h.take("osq", [P, T]), h.take("rt", [P, T]), h.take("ytmp", [P, T])
        masks = h.take("masks", [P, LEVELS + 1, P], I32)
        gate_raw = h.take("gate_raw", [P, BLK])
        ada_raw = (r_tail.take("ada_raw0", [P, 6, BLK]), h_tail.take("ada_raw1", [P, 10, BLK]))
        f = r.over()
        x1 = f.take("x1", [P, KD, T])
        n1 = {k: f.take(f"n1_{k}", [P, 2 if k == "tmp" else 1, T]) for k in ("sum", "sq", "tmp")}
        g_hi, g_lo = f.take("g_hi", [P, KD, T], F32R), f.take("g_lo", [P, KD, T], F32R)
        F_hi = f.take("F_hi", [P, TT, T], F32R)
        F_lo = f.take("F_lo", [P, TT, T], F32R)
        C_hi = f.take("C_hi", [P, 2, 2, 2, P], F32R)
        C_lo = f.take("C_lo", [P, 2, 2, 2, P], F32R)
        raw = f.over()
        F_raw, C_raw = raw.take("F_raw", [P, TT, T]), raw.take("C_raw", [P, 2, 2, 2, P])
        u_st, zf_st = f.take("u_st", [P, 2, T]), f.take("zf_st", [P, 2, T])
        u_hi, u_lo = f.take("u_hi", [P, 2, T], F32R), f.take("u_lo", [P, 2, T], F32R)
        p_hi, p_lo = f.take("p_hi", [P, 2, T], F32R), f.take("p_lo", [P, 2, T], F32R)
        o_sb, yf, yg = f.take("o_sb", [P, 256]), f.take("yf", [P, T]), f.take("yg", [P, T])
        b = g.over()
        hb = b.take("hb", [P, KD, TM])
        n2 = {k: b.take(f"n2_{k}", [P, 2 if k == "tmp" else 1, TM]) for k in ("sum", "sq", "tmp")}
        n_hi, n_lo = b.take("n_hi", [P, KD, TM], F32R), b.take("n_lo", [P, KD, TM], F32R)
        assert b.at <= r.at
        m = b.over()
        hid_hi, hid_lo = m.take("hid_hi", [P, 8, TM], F32R), m.take("hid_lo", [P, 8, TM], F32R)
        sg, hid = m.take("sg", [P, TM]), m.take("hid", [P, TM])
        m = b.over()
        a_hi, a_lo = m.take("a_hi", [P, KD, T], F32R), m.take("a_lo", [P, KD, T], F32R)
        gate = m.take("gate", [P, 2, KD, T])
        mk = m.over()
        cv = mk.take("cv", [P, KD, T])
        gvs, ggs = mk.take("gvs", [P, TM]), mk.take("ggs", [P, TM])
        vpad = mk.take("vpad", [P, DW - 1 + TM])
        xpad = mk.take("xpad", [P, 2, RW - 1 + TM + 1])
        xr = mk.take("xr", [P, 2, TM])
        xr_hi, xr_lo = mk.take("xr_hi", [P, 2, TM], F32R), mk.take("xr_lo", [P, 2, TM], F32R)
        yst = mk.take("yst", [P, 2, T])
        rr, ii = mk.take("rr", [P, 2, TM]), mk.take("ii", [P, 2, TM])
        pp = mk.take("pp", [P, 2, TM])
        m = m.over()
        mg_hi, mg_lo = m.take("mg_hi", [P, KD, T], F32R), m.take("mg_lo", [P, KD, T], F32R)
        mt, centred_sq = m.take("mt", [P, 2, T]), m.take("centred_sq", [P, KD, T])
        m = b.over()
        fin = m.take("fin", [P, KD, T])

        ps = top.enter_context(nc.psum_tensor("ps", [P, 8, T], F32))

        w_loaded = [sem(f"w_loaded{s}") for s in range(2)]
        hi_ready = [sem(f"hi_ready{s}") for s in range(2)]
        lo_ready = [sem(f"lo_ready{s}") for s in range(2)]
        w_used = [sem(f"w_used{s}") for s in range(2)]
        phase_over = sem("phase_over")
        vec_in_s, x_in_s, xc_in_s, const_in_s, dft_in_s, chan_in_s, x1_in_s, meta_in_s, out_s = [
            sem(n) for n in ("vec_loaded", "x_loaded", "ctx_loaded", "const_loaded", "dft_loaded",
                             "chan_loaded", "x1_loaded", "meta_loaded", "out_stored")]
        ident_in_s = sem("ident_loaded")
        ADA_LOADS = [(ada_raw[0][:, 0:3], 0, 3), (ada_raw[0][:, 3:6], 3, 6), (ada_raw[1][:, 0:3], 6, 9),
                     (ada_raw[1][:, 3:6], 9, 12), (ada_raw[1][:, 6:8], 12, 14), (ada_raw[1][:, 8:10], 14, 16)]
        ada_loaded = [sem(f"ada_loaded{n}") for n in range(len(ADA_LOADS))]
        gate_loaded, gate_used = sem("gate_loaded"), sem("gate_used")
        consts_set = sem("consts_set")
        small = {e: sem(f"small_{e}") for e in ("act", "dve")}
        own_s = {e: sem(f"own_{e}") for e in ("act", "dve")}
        ada_done = sem("ada_done")
        acc_free = sem("acc_free")
        pe_scan, act_scan, dve_scan = sem("pe_scan"), sem("act_scan"), sem("dve_scan")
        PE_SCAN, ACT_SCAN, DVE_SCAN = 18, 7, 11
        gates_ready = sem("gates_ready")
        y_ready, y_hi_ready = sem("y_ready"), sem("y_hi_ready")
        z_taken = sem("z_taken")

        def residual_sems(tag):
            return {k: sem(f"{tag}_{k}") for k in ("res", "sq", "add")}

        def norm_sems(tag):
            return {k: sem(f"{tag}_{k}") for k in ("sum", "mean", "root", "tmp", "hi", "lo")}

        N0, N0C, N1, NFIN, NF1, NMIX, NF2, NOUT = [
            norm_sems(t) for t in ("n0", "n0c", "n1", "nfin", "nf1", "nmix", "nf2", "nout")]
        R0, R0C, RC, RF, RA, RD1, RM, RD2 = [
            residual_sems(t) for t in ("r0", "r0c", "rc", "rf", "ra", "rd1", "rm", "rd2")]
        ft_acc, pe_ft, act_ft, dve_ft = sem("ft_acc"), sem("pe_ft"), sem("act_ft"), sem("dve_ft")
        dft_split = {e: sem(f"dft_split_{e}") for e in ("act", "dve")}
        ffn = {}
        for f_ in ("f1", "f2"):
            sems = {k: sem(f"{f_}_{k}") for k in ("gate", "up", "hi", "lo")}
            ffn |= {f"{f_}{c}": (sems, n_ * 8) for n_, c in enumerate("abc")}
        RP = {t: {"res": sem(f"{t}_res")} for t in ("f1a", "f1b", "f2a", "f2b")}
        mx_acc, mx_act, mx_dve = sem("mx_acc"), sem("mx_act"), sem("mx_dve")
        ln_pe, ln_act, ln_dve = sem("ln_pe"), sem("ln_act"), sem("ln_dve")
        ln_norm, ln_silu, ln_hi, ln_lo = [sem(f"ln_{n}") for n in ("norm", "silu", "hi", "lo")]
        YA = {"res": sem("projection_read")}
        mg_sum, mg_hi_s, mg_lo_s = sem("mg_sum"), sem("mg_hi_done"), sem("mg_lo_done")

        def col(name, j, n=1):
            return vec[:, ds(VEC[name] + j, n)]

        def row(t, j):
            return t[:, j] if isinstance(j, int) else t[:, ds(j, 1)].rearrange("p a n -> p (a n)")

        def rate(j):
            return rgc[:, 6:8].rearrange("p a k -> p (a k)")[:, ds(j, 1)]

        class Stream:

            def __init__(self):
                self.base, self.i, self.per = 0, 0, 0

            def enter(self, i, per):
                self.i, self.per = i, per

            def leave(self, trips):
                self.base += trips * self.per
                self.i = self.per = 0

            def slot(self, k):
                return k % 2, self.i * (self.per // 2) + (self.base // 2 + k // 2)

            def wait_done(self, eng, k):
                s, use = self.slot(k)
                eng.wait_ge(w_used[s], use + 2)

        block = top.enter_context(nc.Block())

        @block.sync
        def _(sp):
            sp.dma_start(vec[:], vec_in).then_inc(vec_in_s, 16)
            sp.dma_start(x0[:], x_in).then_inc(x_in_s, 16)
            for n, (dst, a, b_) in enumerate(ADA_LOADS):
                sp.dma_start(dst, ada_in[a:b_].rearrange("b p n -> p b n")).then_inc(ada_loaded[n], 16)
            with sp.Fori(0, nblocks // 2) as i:
                for s in range(2):
                    sp.wait_ge(lo_ready[s], i + 1)
                    sp.dma_start(w_raw[:, s], wts[ds(i * 2 + s, 1)].rearrange("a p n -> p (a n)")
                                 ).then_inc(w_loaded[s], 16)

        @block.gpsimd
        def _(pool):
            pool.dma_start(xc[:], ctx_in).then_inc(xc_in_s, 16)
            pool.dma_start(masks[:], mask_in).then_inc(const_in_s, 16)
            pool.dma_start(ident[:], ident_in).then_inc(ident_in_s, 16)
            with pool.Fori(0, HEADS) as i:
                pool.wait_ge(gate_used, i + 1)
                pool.dma_start(gate_raw[:], gate_in[ds(i, 1)].rearrange("a p n -> p (a n)")
                               ).then_inc(gate_loaded, 16)
            pool.wait_ge(w_used[1], 3 * HEADS + 1)
            pool.dma_start(x1[:], x_in).then_inc(x1_in_s, 16)
            pool.wait_ge(phase_over, 3 * 1)
            pool.dma_start(F_raw[:], dft_in).then_inc(dft_in_s, 16)
            pool.dma_start(C_raw[:], chan_in).then_inc(chan_in_s, 16)
            pool.wait_ge(phase_over, 3 * 3)
            pool.dma_start(hb[:, :, 0:META], meta_in).then_inc(meta_in_s, 16)
            pool.wait_ge(NOUT["lo"], KD)
            pool.dma_start(out, fin[:]).then_inc(out_s, 16)
            pool.wait_ge(out_s, 16)

        @block.tensor
        def _(pe):
            st = Stream()
            over = [0]

            def phase_end():
                over[0] += 1
                pe.drain().then_inc(phase_over, 1)
                pe.wait_ge(phase_over, 3 * over[0])

            def three(outs, whi, wlo, xhi, xlo, start, stop):
                for n, (w, x) in enumerate(((whi, xhi), (whi, xlo), (wlo, xhi))):
                    for o, xp in zip(outs, x):
                        last = nc.tensor.matmul(o, w, xp, start=start and n == 0,
                                                stop=stop and n == 2)
                return last

            def take(k):
                s, use = st.slot(k)
                pe.wait_ge(lo_ready[s], use + 2)
                return s

            def tiles(s, outs, xs, ks, start, stop, first=0):
                for n, k in enumerate(ks):
                    c = slice((first + n) * P, (first + n + 1) * P)
                    last = three(outs, w_hi[:, s, c], w_lo[:, s, c], *xs(k),
                                 start=start and n == 0, stop=stop and n == len(ks) - 1)
                return last

            def whole(hi, lo, a=0, b=T):
                return lambda k: ([hi[:, k, a:b]], [lo[:, k, a:b]])

            def halved(hi, lo):
                return lambda k: ([hi[:, k, 0:HALF], hi[:, k, HALF:TM]],
                                  [lo[:, k, 0:HALF], lo[:, k, HALF:TM]])

            def bank2(b):
                return [ps[:, b, 0:HALF], ps[:, b + 1, 0:HALF]]

            def mean(N, n, src):
                pe.wait_ge(N["sum"], 1)
                if n == TM:
                    for q in range(2):
                        last = nc.tensor.matmul(ps[:, 6 + q, 0:HALF], ones_d[:], src[:, q * HALF:(q + 1) * HALF],
                                                start=True, stop=True)
                else:
                    last = nc.tensor.matmul(ps[:, 6, 0:n], ones_d[:], src[:, 0:n], start=True, stop=True)
                last.then_inc(N["mean"], 1)

            pe.sem_inc(w_used[0], 1)
            pe.sem_inc(w_used[1], 1)
            pe.sem_inc(gate_used, 1)

            pe.wait_ge(consts_set, 4)
            for n, (raw_, a, b_) in enumerate(ADA_LOADS):
                pe.wait_ge(ada_loaded[n], 16)
                for m_ in range(a, b_):
                    for k in range(KD):
                        last = nc.tensor.matmul(ps[:, 7, 2 * m_:2 * m_ + 2], raw_[:, m_ - a, k * P:(k + 1) * P],
                                                csil[:, k], start=k == 0, stop=k == KD - 1)
                if n == 4:
                    mean(N0, T, st_sum[:, 0])
            last.then_inc(ada_done, 1)
            pe.wait_ge(N0["root"], 1)
            mean(N0C, TC, st_sum[:, 1])
            pe.wait_ge(ident_in_s, 16)

            def tile(t):
                return slice(t * P, (t + 1) * P)

            def halves_of(ap, n, half):
                return ap.rearrange("p (m h n) -> p m h n", h=2, n=n)[:, :, half]

            def as_cut(N, xs):
                def of(k):
                    pe.wait_ge(N["lo"], k + 1)
                    return xs(k)
                return of

            def pe_head(i, j):
                def free(k):
                    pe.wait_ge(acc_free, i * 6 + (k + 1))

                def project(k, part):
                    if i is None:
                        return
                    a, c = k % 2, 2 + k % 2
                    if part == "a":
                        s = take(k)
                        free(k)
                        xs = whole(h_hi, h_lo)
                        tiles(s, [ps[:, a]], as_cut(N0, xs) if j is None and k == 0 else xs, range(4), True, False)
                    elif part == "b":
                        xs = whole(h_hi, h_lo)
                        last = tiles(k % 2, [ps[:, a]], as_cut(N0, xs) if j is None and k == 0 else xs,
                                     range(4, 8), False, True, 4)
                        if k in (0, 4):
                            last.then_inc(w_used[k % 2], 1)
                    elif part == "c":
                        xs = whole(hc_hi, hc_lo, 0, TC)
                        tiles(k % 2, [ps[:, c, 0:TC]], as_cut(N0C, xs) if j is None and k == 1 else xs,
                              range(8), True, True
                              ).then_inc(w_used[k % 2], 1)
                    else:
                        free(k)
                        pe.wait_ge(gate_loaded, i * 16 + 16)
                        for n in range(KD):
                            last = nc.tensor.matmul(ps[:, c, 2:4], gate_raw[:, n * P:(n + 1) * P], csil[:, n],
                                                    start=n == 0, stop=n == KD - 1)
                        last.then_inc(gate_used, 1)
                        s = take(k)
                        tiles(s, [ps[:, c, 0:2]], whole(c_hi, c_lo, 0, 2), range(8), True, True
                              ).then_inc(w_used[s], 1)

                def dve(n):
                    pe.wait_ge(dve_scan, j * DVE_SCAN + n)

                def act(n):
                    pe.wait_ge(act_scan, (j + 1) * ACT_SCAN + n)

                def turn_v(ts):
                    if j is None:
                        return
                    if len(ts) == TT:
                        pe.wait_ge(acc_free, j * 6 + 6)
                    else:
                        act(1)
                    for n, t in enumerate(ts):
                        last = nc.tensor.transpose(ps[:, 6, tile(n)], v_st[:, tile(t)], ident[:])
                    last.then_inc(pe_scan, 1)

                def diagonal():
                    if j is None:
                        return
                    pe.wait_ge(gates_ready, j + 1)
                    for t in range(TT):
                        last = nc.tensor.matmul(ps[:, 4, tile(t)], ksum[:, tile(t)], q_st[:, tile(t)],
                                                start=True, stop=True)
                    last.then_inc(pe_scan, 1)

                def level(l):
                    if j is None:
                        return
                    if l == 0:
                        pe.wait_ge(act_scan, j * ACT_SCAN + 7)
                    else:
                        dve(l)
                    for t in range(TT):
                        for d in range(2):
                            last = nc.tensor.matmul(
                                halves_of(ps[:, 5 - l % 2, tile(t)], 2 ** l, 1 - d),
                                K[:, d, tile(CT + t)], halves_of(Q[:, d, tile(t)], 2 ** l, 1 - d),
                                start=True, stop=True)
                    last.then_inc(pe_scan, 1)

                def steps(g_):
                    return [(n, d) for n in range(2 * g_, min(2 * g_ + 2, 5)) for d in range(2)]

                def turn_k(g_):
                    if j is None:
                        return
                    dve(7)
                    act(2 + g_)
                    for x, (n, d) in enumerate(steps(g_)):
                        last = nc.tensor.transpose(ps[:, 6, tile(x)], K[:, d, tile(ORDER[d][n])], ident[:])
                    last.then_inc(pe_scan, 1)

                def outer(g_):
                    if j is None:
                        return
                    act(3 + g_)
                    dve((7, 8, 9)[g_])
                    for x, (n, d) in enumerate(steps(g_)):
                        last = nc.tensor.matmul(ps[:, 4 + g_ % 2, tile(x)], KT[:, x], V[:, ORDER[d][n]],
                                                start=True, stop=True)
                    last.then_inc(pe_scan, 1)

                def output():
                    if j is None:
                        return
                    dve(11)
                    for t in range(TT):
                        o = ps[:, 7, tile(t)]
                        nc.tensor.matmul(o, V[:, CT + t], ST[:, t], start=True, stop=False)
                        nc.tensor.matmul(o, states[:, 1 + t, 0], Q[:, 0, tile(t)], start=False, stop=False)
                        last = nc.tensor.matmul(o, states[:, 4 - t, 1], Q[:, 1, tile(t)], start=False, stop=True)
                    last.then_inc(pe_scan, 1)

                def norm():
                    if j is None:
                        return
                    act(6)
                    nc.tensor.matmul(ps[:, 5], ones_h[:], osq[:], start=True, stop=True).then_inc(pe_scan, 1)

                project(0, "a"); turn_v(range(CT, AT)); project(0, "b"); diagonal(); level(0)
                project(1, "a"); level(1); turn_v(range(CT)); project(1, "b"); level(2)
                project(1, "c"); level(3); project(2, "a"); level(4); project(2, "b"); level(5)
                project(2, "c"); level(6); project(3, "a"); turn_k(0); project(3, "b"); outer(0)
                turn_k(1); project(3, "c"); outer(1); turn_k(2); project(4, "a"); outer(2)
                project(4, "b"); output(); project(5, "ada"); norm()

            st.enter(0, 6)
            pe_head(0, None)
            st.leave(1)
            with pe.Fori(0, HEADS - 1) as j:
                st.enter(j, 6)
                pe_head(j + 1, j)
            st.leave(HEADS - 1)
            pe_head(None, HEADS - 1)
            pe.wait_ge(dve_scan, HEADS * DVE_SCAN)
            phase_end()

            def residual(R, trips, nb, xs, n, nk=KD, done=0):
                with pe.Fori(0, trips) as i:
                    st.enter(i, 2 * nb)
                    for a in range(2):
                        o = bank2(2 * a) if n == TM else [ps[:, 2 * a]]
                        for q in range(nb):
                            s = take(a * nb + q)
                            if q == 0:
                                pe.wait_ge(R["res"], i * 2 + (done + a + 1))
                            tiles(s, o, xs, range(q * KD, q * KD + nk), q == 0, q == nb - 1
                                  ).then_inc(w_used[s], 1)
                st.leave(trips)

            residual(RC, KD // 2, 2, whole(y_hi, y_lo), T)
            mean(N1, T, n1["sum"][:, 0])
            pe.wait_ge(N1["lo"], KD)
            pe.wait_ge(dft_split["dve"], 2)
            phase_end()

            def pe_group(i, j):
                def project(k):
                    if i is None:
                        return
                    s = take(k)
                    pe.wait_ge(ft_acc, i * 4 + (k + 1))
                    tiles(s, [ps[:, k % 2]], whole(g_hi, g_lo), range(8), True, True).then_inc(w_used[s], 1)

                def turn():
                    if j is None:
                        return
                    pe.wait_ge(ft_acc, j * 4 + 4)
                    pe.wait_ge(dve_ft, j * 8 + 1)
                    for a in range(2):
                        for t in range(TT):
                            last = nc.tensor.transpose(ps[:, 4 + a, tile(t)], u_st[:, a, tile(t)], ident[:])
                    last.then_inc(pe_ft, 1)

                def over_tokens(a):
                    if j is None:
                        return
                    pe.wait_ge(dve_ft, j * 8 + (2 + a))
                    for t in range(TT):
                        last = three([ps[:, 6 + a]], u_hi[:, a, tile(t)], u_lo[:, a, tile(t)],
                                     [F_hi[:, t]], [F_lo[:, t]], t == 0, t == TT - 1)
                    last.then_inc(pe_ft, 1)

                def over_channels(m_):
                    if j is None:
                        return
                    pe.wait_ge(dve_ft, j * 8 + 5)
                    for part, c0, n in ((0, 0, BF), (1, 256, 256)):
                        for kk in range(2):
                            last = three([ps[:, 4 + 2 * m_ + part, 0:n]], C_hi[:, part, kk, m_],
                                         C_lo[:, part, kk, m_], [p_hi[:, kk, c0:c0 + n]],
                                         [p_lo[:, kk, c0:c0 + n]], kk == 0, kk == 1)
                    last.then_inc(pe_ft, 1)

                turn(); project(0); over_tokens(0); project(1); over_tokens(1)
                project(2); over_channels(0); project(3); over_channels(1)

            st.enter(0, 4)
            pe_group(0, None)
            st.leave(1)
            with pe.Fori(0, GROUPS - 1) as j:
                st.enter(j, 4)
                pe_group(j + 1, j)
            st.leave(GROUPS - 1)
            pe_group(None, GROUPS - 1)
            pe.wait_ge(dve_ft, GROUPS * 8 + 1)

            residual(RF, KD // 2, 2, whole(y_hi, y_lo), T)
            mean(NFIN, T, n1["sum"][:, 0])
            phase_end()
            mean(NF1, TM, n2["sum"][:, 0])

            def feed_forward(tags, N, last_tag, n):
                inner = halved(n_hi, n_lo) if n == TM else whole(n_hi, n_lo, META, TM)
                xs = as_cut(N, inner)
                hs = halved(hid_hi, hid_lo) if n == TM else whole(hid_hi, hid_lo, META, TM)
                for tag, count in zip(tags, FF_GROUPS):
                    S, before = ffn[tag]
                    with pe.Fori(0, count) as i:
                        st.enter(i, 2)
                        for k, reader in ((0, "gate"), (1, "up")):
                            s = take(k)
                            pe.wait_ge(S[reader], i + (before + 1))
                            o = bank2(2 * k) if n == TM else [ps[:, 2 * k]]
                            tiles(s, o, xs if k == 0 else inner, range(KD), True, True).then_inc(w_used[s], 1)
                    st.leave(count)
                    pe.wait_ge(S["lo"], before + count + 1)
                    R = RP.get(tag, last_tag)
                    residual(R, KD // 2, 1, hs, n, count)
                    pe.wait_ge(R["res"], KD + 2)

            feed_forward(("f1a", "f1b", "f1c"), NF1, RD1, TM)
            mean(NMIX, TM, n2["sum"][:, 0])
            pe.wait_ge(NMIX["lo"], KD)
            phase_end()

            with pe.Fori(0, KD // 2) as i:
                st.enter(i, 14)
                for k in range(12):
                    s = take(k)
                    pe.wait_ge(mx_acc, i * 14 + (k + 1 if k else 2))
                    if k < 6:
                        tiles(s, bank2(2 * (k % 2)), halved(n_hi, n_lo), range(KD), True, True
                              ).then_inc(w_used[s], 1)
                    else:
                        tiles(s, [ps[:, 2 * (k % 2)]], whole(n_hi, n_lo, META, TM), range(KD), True, True
                              ).then_inc(w_used[s], 1)
                for k in (12, 13):
                    s = take(k)
                    if k == 12:
                        pe.wait_ge(mx_dve, i * 12 + 4)
                    pe.wait_ge(mx_acc, i * 14 + (k + 1))
                    for m_ in range(2):
                        last = tiles(s, bank2((4 if k == 12 else 0) + 2 * m_), halved(xr_hi, xr_lo),
                                     range(2), True, True, 2 * m_)
                    last.then_inc(w_used[s], 1)
            st.leave(KD // 2)
            pe.wait_ge(mx_dve, (KD // 2 - 1) * 12 + 7)
            pe.wait_ge(mx_acc, KD // 2 * 14 + 1)
            for k in range(KD):
                last = nc.tensor.matmul(ps[:, 6], ones_d[:], cv[:, k], start=k == 0, stop=k == KD - 1)
            last.then_inc(ln_pe, 1)
            phase_end()

            residual(YA, 2, 1, whole(a_hi, a_lo), T)
            for k in range(KD):
                pe.wait_ge(ln_act, k + 1)
                last = nc.tensor.matmul(ps[:, 7], ones_d[:], centred_sq[:, k], start=k == 0, stop=k == KD - 1)
            last.then_inc(ln_pe, 1)
            residual(YA, 2, 1, whole(a_hi, a_lo), T, done=4)
            residual(YA, KD // 2, 1, as_cut({"lo": ln_lo}, whole(n_hi, n_lo)), T, done=8)
            pe.wait_ge(YA["res"], 2 * KD + 2)
            residual(RM, KD // 2, 1, as_cut({"lo": mg_lo_s}, whole(mg_hi, mg_lo)), T)
            mean(NF2, T, n2["sum"][:, 0])
            phase_end()
            feed_forward(("f2a", "f2b", "f2c"), NF2, RD2, T)
            mean(NOUT, T, n2["sum"][:, 0])

        @block.scalar
        def _(act):
            st = Stream()
            over = [0]
            own = Own(act, own_s["act"])
            run = nc.scalar.activation

            def phase_end():
                over[0] += 1
                act.drain().then_inc(phase_over, 1)
                act.wait_ge(phase_over, 3 * over[0])

            def cut(k):
                s, use = st.slot(k)
                act.wait_ge(w_loaded[s], use * 16 + 16)
                act.wait_ge(w_used[s], use + 1)
                run(w_hi[:, s], w_raw[:, s], ACT.Copy).then_inc(hi_ready[s], 1)

            def after(k):
                st.wait_done(act, k)
                cut(k + 2)

            def root(N, acc, rt_):
                act.wait_ge(N["mean"], 1)
                run(rt_, acc, ACT.Sqrt, bias=eps[:]).then_inc(N["root"], 1)

            def norm_hi(N, hi, tmp, shift):
                for k in range(KD):
                    act.wait_ge(N["tmp"], k + 1)
                    run(hi(k), tmp(k), ACT.Identity, bias=shift(k)).then_inc(N["hi"], 1)

            def squares(R, src, sq):
                for k in range(KD):
                    if k:
                        act.wait_ge(R["add"], k)
                    run(sq, src(k), ACT.Square).then_inc(R["sq"], 1)

            def square_one(R, m_, src, sq, credit):
                act.wait_ge(R["res"], m_ + (1 + credit))
                act.wait_ge(R["add"], m_ + 2)
                run(sq, src, ACT.Square).then_inc(R["sq"], 1)

            for sem_ in (acc_free, ft_acc, mx_acc):
                act.sem_inc(sem_, 2)
            act.sem_inc(act_scan, ACT_SCAN)
            for tag in ("f1a", "f2a"):
                act.sem_inc(ffn[tag][0]["gate"], 1)

            act.wait_ge(vec_in_s, 16)
            run(csil[:], vec[:, VEC["c"]:VEC["c"] + 2 * KD].rearrange("p (k n) -> p k n", n=2), ACT.Silu
                ).then_inc(small["act"], 1)
            act.wait_ge(small["act"], 1)
            run(c_hi[:], csil[:], ACT.Copy).then_inc(small["act"], 1)
            act.wait_ge(consts_set, 2)
            run(lbt[:, 1:3], lbt[:, 1:3], ACT.Exp).then_inc(small["act"], 1)
            act.wait_ge(consts_set, 3)
            run(rgc[:, 1], rgc[:, 0], ACT.Exp, scale=-1.0).then_inc(small["act"], 1)
            act.wait_ge(x_in_s, 16)
            squares(R0, lambda k: x0[:, k], st_sq[:])
            act.wait_ge(xc_in_s, 16)
            act.wait_ge(R0["add"], KD)
            squares(R0C, lambda k: xc[:, k], st_sq[:, 0:TC])
            act.wait_ge(R0C["add"], KD)
            cut(0)
            cut(1)
            root(N0, ps[:, 6], st_sq[:])
            norm_hi(N0, lambda k: h_hi[:, k], lambda k: st_tmp[:, k % 2], lambda k: ada0[:, k, 0:1])
            root(N0C, ps[:, 6, 0:TC], st_tmpc[:, 2])
            norm_hi(N0C, lambda k: hc_hi[:, k], lambda k: st_tmpc[:, k % 2], lambda k: ada0[:, k, 1:2])

            def act_head(i, j, f):
                def pe(n):
                    act.wait_ge(pe_scan, j * PE_SCAN + n)

                def dve(n):
                    act.wait_ge(dve_scan, j * DVE_SCAN + n)

                def stage(k):
                    if i is None:
                        return
                    after(k)
                    a, c = ps[:, k % 2], ps[:, 2 + k % 2]
                    if k == 0:
                        if j is not None:
                            pe(2)
                        run(q_st[:], a, ACT.Silu).then_inc(acc_free, 1)
                    elif k < 3:
                        if j is not None:
                            dve(1)
                        run(f_st[:, k - 1, TC:TA], a, ACT.Sigmoid)
                        run(f_st[:, k - 1, 0:TC], c[:, 0:TC], ACT.Sigmoid).then_inc(acc_free, 1)
                    elif k == 3:
                        if j is not None:
                            pe(5)
                        run(v_st[:, TC:TA], a, ACT.Copy)
                        run(v_st[:, 0:TC], c[:, 0:TC], ACT.Copy).then_inc(acc_free, 1)
                    elif k == 4:
                        if j is not None:
                            act.wait_ge(z_taken, j + 1)
                        run(z_st[:], a, ACT.Silu).then_inc(acc_free, 1)
                    else:
                        run(row(ada1, i), c[:, 0:2], ACT.Identity, bias=col("ada_b1", i))
                        run(row(gates, i), c[:, 2:4], ACT.Identity, bias=col("gate_b", i)).then_inc(acc_free, 1)

                def copy(n, dst, src):
                    if j is not None:
                        pe(n)
                        run(dst, src, ACT.Copy).then_inc(act_scan, 1)

                def squares_of_output():
                    if j is not None:
                        pe(17)
                        run(osq[:], ps[:, 7], ACT.Square).then_inc(act_scan, 1)

                def root_of_output():
                    if j is not None:
                        pe(18)
                        run(rt[:], ps[:, 5], ACT.Sqrt, bias=eps[:]).then_inc(act_scan, 1)

                def cut_output():
                    if f is not None:
                        act.wait_ge(y_ready, f + 1)
                        run(row(y_hi, f), ytmp[:], ACT.Copy).then_inc(y_hi_ready, 1)

                copy(1, V[:, CT:AT].rearrange("p t v -> p (t v)"), ps[:, 6])
                stage(0)
                copy(5, V[:, 0:CT].rearrange("p t v -> p (t v)"), ps[:, 6, 0:TC])
                stage(1)
                stage(2)
                kt = KT[:].rearrange("p t v -> p (t v)")
                copy(11, kt, ps[:, 6])
                copy(13, kt, ps[:, 6])
                stage(3)
                copy(15, kt[:, 0:2 * P], ps[:, 6, 0:2 * P])
                cut_output()
                stage(4)
                squares_of_output()
                stage(5)
                root_of_output()

            st.enter(0, 6)
            act_head(0, None, None)
            st.leave(1)
            st.enter(0, 6)
            act_head(1, 0, None)
            st.leave(1)
            with act.Fori(0, HEADS - 2) as f:
                st.enter(f, 6)
                act_head(f + 2, f + 1, f)
            st.leave(HEADS - 2)
            act_head(None, HEADS - 1, HEADS - 2)
            act_head(None, None, HEADS - 1)
            phase_end()

            def residual(R, trips, nb, src, sq, sums, ahead=True):
                def one(i):
                    for a in range(2):
                        for q in range(nb):
                            if ahead or not isinstance(i, int):
                                after(a * nb + q)
                        if sums:
                            square_one(R, i * 2 + a, src(i * 2 + a), sq, 2)
                if ahead:
                    with act.Fori(0, trips) as i:
                        st.enter(i, 2 * nb)
                        one(i)
                    st.leave(trips)
                else:
                    with act.Fori(0, trips - 1) as i:
                        st.enter(i, 2 * nb)
                        one(i)
                    st.leave(trips - 1)
                    one_last = trips - 1
                    for a in range(2):
                        if sums:
                            square_one(R, one_last * 2 + a, src(one_last * 2 + a), sq, 2)

            residual(RC, KD // 2, 2, lambda m_: row(x1, m_), n1["sq"][:, 0], True)
            act.wait_ge(N1["sum"], 1)
            root(N1, ps[:, 6], n1["sq"][:, 0])
            norm_hi(N1, lambda k: g_hi[:, k], lambda k: n1["tmp"][:, k % 2], lambda k: ada1[:, k, 0:1])
            act.wait_ge(dft_in_s, 16)
            run(F_hi[:], F_raw[:], ACT.Copy).then_inc(dft_split["act"], 1)
            act.wait_ge(chan_in_s, 16)
            run(C_hi[:], C_raw[:], ACT.Copy).then_inc(dft_split["act"], 1)
            phase_end()

            def act_group(i, j):
                def pe(n):
                    act.wait_ge(pe_ft, j * 5 + n)

                def dve(n):
                    act.wait_ge(dve_ft, j * 8 + (n + 1))

                def stage(k):
                    if i is None:
                        return
                    if j is not None:
                        if k < 2:
                            pe(1)
                        else:
                            dve(5 + 2 * (k - 2))
                    if k < 2:
                        run(u_st[:, k], ps[:, k % 2], ACT.Copy).then_inc(ft_acc, 1)
                    else:
                        run(zf_st[:, k - 2], ps[:, k % 2], ACT.Silu).then_inc(ft_acc, 1)

                def hi(n, dst, src):
                    if j is not None:
                        pe(n)
                        run(dst, src, ACT.Copy).then_inc(act_ft, 1)

                def tail(m_):
                    if j is None:
                        return
                    pe(4 + m_)
                    run(o_sb[:], ps[:, 5 + 2 * m_, 0:256], ACT.Copy).then_inc(act_ft, 1)
                    dve(5 + 2 * m_)
                    run(row(y_hi, j * 2 + m_), yg[:], ACT.Copy).then_inc(act_ft, 1)

                hi(1, u_hi[:, 0], ps[:, 4])
                hi(1, u_hi[:, 1], ps[:, 5])
                if i is not None:
                    after(0)
                stage(0)
                hi(2, p_hi[:, 0], ps[:, 6])
                if i is not None:
                    after(1)
                stage(1)
                hi(3, p_hi[:, 1], ps[:, 7])
                if i is not None:
                    after(2)
                tail(0)
                stage(2)
                if i is not None:
                    after(3)
                tail(1)
                stage(3)

            st.enter(0, 4)
            act_group(0, None)
            st.leave(1)
            with act.Fori(0, GROUPS - 1) as j:
                st.enter(j, 4)
                act_group(j + 1, j)
            st.leave(GROUPS - 1)
            act_group(None, GROUPS - 1)

            residual(RF, KD // 2, 2, lambda m_: row(x1, m_), n1["sq"][:, 0], True)
            act.wait_ge(NFIN["sum"], 1)
            root(NFIN, ps[:, 6], n1["sq"][:, 0])
            phase_end()
            for k in range(KD):
                act.wait_ge(RA["res"], k + 1)
                if k:
                    act.wait_ge(RA["add"], k)
                run(n2["sq"][:, 0], hb[:, k], ACT.Square).then_inc(RA["sq"], 1)

            def block_norm(N, n):
                act.wait_ge(N["sum"], 1)
                if n == TM:
                    root(N, ps[:, 6:8, 0:HALF], halves(n2["sq"][:, 0]))
                    norm_hi(N, lambda k: n_hi[:, k], lambda k: n2["tmp"][:, k % 2], lambda k: zero[:])
                else:
                    root(N, ps[:, 6], n2["sq"][:, 0, 0:T])
                    norm_hi(N, lambda k: n_hi[:, k, META:TM], lambda k: n2["tmp"][:, k % 2, 0:T],
                            lambda k: zero[:])

            def feed_forward(tags, last_R, n, last):
                c0 = TM - n
                for tag, count in zip(tags, FF_GROUPS):
                    S, before = ffn[tag]
                    with act.Fori(0, count) as i:
                        st.enter(i, 2)
                        after(0)
                        acc = ps[:, 0:2, 0:HALF] if n == TM else ps[:, 0]
                        dst = halves(sg[:]) if n == TM else sg[:, 0:n]
                        act.wait_ge(S["up"], i + (before + 1))
                        run(dst, acc, ACT.Silu).then_inc(S["gate"], 1)
                        after(1)
                        act.wait_ge(S["up"], i + (before + 2))
                        run(row(hid_hi, i)[:, c0:TM], hid[:, 0:n], ACT.Copy).then_inc(S["hi"], 1)
                    st.leave(count)
                    final = tag == tags[-1]
                    residual(last_R if final else RP[tag], KD // 2, 1,
                             lambda m_: row(hb, m_)[:, c0:TM], n2["sq"][:, 0, 0:n], final,
                             not (final and last))

            block_norm(NF1, TM)
            feed_forward(("f1a", "f1b", "f1c"), RD1, TM, False)
            block_norm(NMIX, TM)
            phase_end()

            with act.Fori(0, KD // 2) as i:
                st.enter(i, 14)
                own.enter(i, 4)

                def out_of(k, dst, func, bias):
                    n = TM if k < 6 else T
                    b0 = 2 * (k % 2)
                    acc = ps[:, b0:b0 + 2, 0:HALF] if n == TM else ps[:, b0]
                    run(halves(dst) if n == TM else dst, acc, func, bias=bias).then_inc(mx_acc, 1)

                def b_in(kind, a):
                    return col("b_in", i * 2 + (kind * KD + a))

                def dve(n):
                    act.wait_ge(mx_dve, i * 12 + n)

                for a in range(2):
                    after(a)
                    out_of(a, xpad[:, a, RW - 1:RW - 1 + TM], ACT.Identity, b_in(0, a))
                after(2)
                for a in range(2):
                    dve(1 + a)
                    run(xr_hi[:, a], xr[:, a], ACT.Copy).then_inc(mx_act, 1)
                out_of(2, gvs[:], ACT.Identity, b_in(2, 0))
                after(3)
                out_of(3, ggs[:], ACT.Sigmoid, b_in(3, 0))
                after(4)
                dve(5)
                out_of(4, gvs[:], ACT.Identity, b_in(2, 1))
                after(5)
                out_of(5, ggs[:], ACT.Sigmoid, b_in(3, 1))
                for a in range(2):
                    after(6 + a)
                    out_of(6 + a, yst[:, a], ACT.Gelu_apprx_tanh, b_in(1, a))
                for a in range(2):
                    for t in range(2):
                        after(8 + 2 * a + t)
                        out_of(8 + 2 * a + t, row(gate[:, t], i * 2 + a), ACT.Sigmoid, b_in(4 + t, a))
                after(12)
                for a in range(2):
                    last = run(halves(rr[:, a]), ps[:, 4 + 2 * a:6 + 2 * a, 0:HALF], ACT.Sigmoid,
                               bias=col("b_a", i * 2 + a))
                last.then_inc(mx_acc, 1)
                after(13)
                for a in range(2):
                    last = run(halves(ii[:, a]), ps[:, 2 * a:2 * a + 2, 0:HALF], ACT.Sigmoid,
                               bias=col("b_x", i * 2 + a))
                last.then_inc(mx_acc, 1)
                act.wait_ge(mx_acc, i * 14 + 16)
                dve(6)
                for a in range(2):
                    own.link(run(pp[:, a], rr[:, a], ACT.Tanh, scale=rate(i * 2 + (KD + a))))
                    own.link(run(rr[:, a], rr[:, a], ACT.Exp, scale=rate(i * 2 + a)))
                    run((gvs, ggs)[a][:], rr[:, a], ACT.Square).then_inc(mx_act, 1)
                for a in range(2):
                    dve(7 + a)
                    run(pp[:, a], pp[:, a], ACT.Sqrt, bias=tiny[:]).then_inc(mx_act, 1)
                for a in range(2):
                    dve(9 + a)
                    run(row(a_hi, i * 2 + a), yst[:, a], ACT.Copy).then_inc(mx_act, 1)
            st.leave(KD // 2)
            own.leave(KD // 2)
            phase_end()

            with act.Fori(0, 2) as i:
                st.enter(i, 2)
                for a in range(2):
                    after(a)
                    for n in (2 * a, 2 * a + 1):
                        act.wait_ge(ln_dve, i * 4 + (n + 1))
                        run(row(centred_sq, i * 4 + n), row(cv, i * 4 + n), ACT.Square).then_inc(ln_act, 1)
            st.leave(2)
            act.wait_ge(ln_pe, 2)
            run(n2["sq"][:, 0, 0:T], ps[:, 7], ACT.Sqrt, bias=eps[:]).then_inc(ln_act, 1)
            with act.Fori(0, 2) as i:
                st.enter(i, 2)
                for a in range(2):
                    after(a)
                    for n in (2 * a, 2 * a + 1):
                        act.wait_ge(ln_norm, i * 4 + (n + 1))
                        run(row(cv, i * 4 + n), row(cv, i * 4 + n), ACT.Silu, bias=col("ln_b", i * 4 + n)
                            ).then_inc(ln_silu, 1)
                        act.wait_ge(ln_silu, i * 4 + (n + 1))
                        run(row(n_hi, i * 4 + n)[:, 0:T], row(cv, i * 4 + n), ACT.Copy).then_inc(ln_hi, 1)
            st.leave(2)
            with act.Fori(0, KD // 2) as i:
                st.enter(i, 2)
                for a in range(2):
                    after(a)
                    act.wait_ge(mg_sum, i * 2 + (a + 1))
                    run(row(mg_hi, i * 2 + a), mt[:, a], ACT.Copy).then_inc(mg_hi_s, 1)
            st.leave(KD // 2)
            residual(RM, KD // 2, 1, lambda m_: row(hb, m_)[:, META:TM], n2["sq"][:, 0, 0:T], True)
            act.wait_ge(NF2["sum"], 1)
            phase_end()
            block_norm(NF2, T)
            feed_forward(("f2a", "f2b", "f2c"), RD2, T, True)
            act.wait_ge(NOUT["sum"], 1)
            root(NOUT, ps[:, 6], n2["sq"][:, 0, 0:T])

        @block.vector
        def _(dve):
            st = Stream()
            over = [0]
            own = Own(dve, own_s["dve"])
            v = nc.vector
            tt, ts, stt = v.tensor_tensor, v.tensor_scalar, v.scalar_tensor_tensor

            def phase_end():
                over[0] += 1
                dve.drain().then_inc(phase_over, 1)
                dve.wait_ge(phase_over, 3 * over[0])

            def cut(k):
                s, use = st.slot(k)
                dve.wait_ge(hi_ready[s], use + 1)
                tt(w_lo[:, s], w_raw[:, s], w_hi[:, s].bitcast(F32), ALU.subtract).then_inc(lo_ready[s], 1)

            def after(k):
                cut(k + 2)

            def sum_squares(R, n, acc, sq):
                for k in range(n):
                    dve.wait_ge(R["sq"], k + 1)
                    if k:
                        dve.wait_ge(R["add"], k)
                        tt(acc, acc, sq, ALU.add).then_inc(R["add"], 1)
                    else:
                        v.tensor_copy(acc, sq).then_inc(R["add"], 1)

            def norm_apply(N, src, gain, shift, tmp, rt_, hi, lo):
                dve.wait_ge(N["root"], 1)
                own.link(v.reciprocal(rt_, rt_))
                for k in range(KD + 1):
                    if k < KD:
                        if k > 1:
                            dve.wait_ge(N["lo"], k - 1)
                        stt(tmp(k), src(k), gain(k), rt_, ALU.mult, ALU.mult).then_inc(N["tmp"], 1)
                    if k:
                        dve.wait_ge(N["hi"], k)
                        stt(lo(k - 1), tmp(k - 1), shift(k - 1), hi(k - 1).bitcast(F32), ALU.add, ALU.subtract
                            ).then_inc(N["lo"], 1)

            def open_sums(R, acc, sq):
                v.memset(acc, 0.0).then_inc(R["add"], 1)
                v.memset(sq, 0.0).then_inc(R["sq"], 1)

            def add_square(R, m_, acc, sq):
                dve.wait_ge(R["sq"], m_ + 1)
                dve.wait_ge(R["add"], m_ + 1)
                tt(acc, acc, sq, ALU.add).then_inc(R["add"], 1)

            def close_sums(R, N, acc, sq):
                dve.wait_ge(R["sq"], KD + 1)
                dve.wait_ge(R["add"], KD + 1)
                tt(acc, acc, sq, ALU.add).then_inc(N["sum"], 1)

            for s in range(2):
                dve.sem_inc(lo_ready[s], 1)
            for R in (RC, RF, RM, RD1, RD2, *RP.values()):
                dve.sem_inc(R["res"], 2)
            dve.sem_inc(dve_ft, 1)
            dve.sem_inc(YA["res"], 2)
            for tag in ("f1a", "f2a"):
                dve.sem_inc(ffn[tag][0]["up"], 1)
                dve.sem_inc(ffn[tag][0]["lo"], 1)

            v.memset(ones_d[:], 1.0 / D)
            v.memset(ones_h[:], 1.0 / P)
            v.memset(eps[:], EPS)
            v.memset(tiny[:], 2.0 ** -100)
            v.memset(zero[:], 0.0).then_inc(consts_set, 1)
            dve.wait_ge(vec_in_s, 16)
            lb = vec[:, VEC["lb"]:VEC["lb"] + 4 * HEADS].rearrange("p (n c) -> p n c", n=2)
            own.link(tt(lbt[:, 0], lb[:, 0], lb[:, 1], ALU.max))
            tt(lbt[:, 1:3], lb, lbt[:, 0:1].broadcast_to([P, 2, 2 * HEADS]), ALU.subtract).then_inc(consts_set, 1)
            lam = vec[:, VEC["lam"]:VEC["lam"] + KD]
            own.link(ts(rgc[:, 0], lam, -1.0, None, ALU.mult))
            tt(rgc[:, 0], rgc[:, 0], lam, ALU.max).then_inc(consts_set, 1)
            dve.wait_ge(small["act"], 2)
            tt(c_lo[:], csil[:], c_hi[:].bitcast(F32), ALU.subtract).then_inc(consts_set, 1)
            dve.wait_ge(small["act"], 3)
            own.link(tt(lbt[:, 3], lbt[:, 1], lbt[:, 2], ALU.add))
            own.link(v.reciprocal(lbt[:, 3], lbt[:, 3]))
            own.link(tt(lbt[:, 4], lbt[:, 1], lbt[:, 3], ALU.mult))
            own.mark(ts(lbt[:, 5], lbt[:, 4], -1.0, 1.0, ALU.mult, ALU.add))
            dve.wait_ge(small["act"], 4)
            z, w, w2, p_ = rgc[:, 1], rgc[:, 2], rgc[:, 3], rgc[:, 4]
            own.link(ts(w, z, 2.0, None, ALU.add))
            own.link(v.reciprocal(w, w))
            own.link(tt(w, w, z, ALU.mult))
            own.link(tt(w2, w, w, ALU.mult))
            own.link(ts(p_, w2, 1.0 / 19, None, ALU.mult))
            for n in range(17, 1, -2):
                own.link(stt(p_, p_, 1.0 / n, w2, ALU.add, ALU.mult))
            own.link(stt(p_, p_, 1.0, w, ALU.add, ALU.mult))
            own.link(ts(rgc[:, 5], lam, -1.0, 0.0, ALU.mult, ALU.max))
            own.link(stt(p_, p_, 2.0, rgc[:, 5], ALU.mult, ALU.add))
            ts(rgc[:, 6], p_, -8.0, None, ALU.mult)
            own.mark(ts(rgc[:, 7], p_, 8.0, None, ALU.mult))
            sum_squares(R0, KD, st_sum[:, 0], st_sq[:])
            dve.wait_ge(R0["add"], KD)
            dve.sem_inc(N0["sum"], 1)
            sum_squares(R0C, KD, st_sum[:, 1, 0:TC], st_sq[:, 0:TC])
            dve.wait_ge(R0C["add"], KD)
            dve.sem_inc(N0C["sum"], 1)
            cut(0)
            cut(1)
            dve.wait_ge(ada_done, 1)
            own.link(tt(ada0[:, 0:16], ps[:, 7, 0:32].rearrange("p (m n) -> p m n", n=2),
                        vec[:, VEC["ada_b0"]:VEC["ada_b0"] + 16].unsqueeze(2).broadcast_to([P, 16, 2]), ALU.add))
            g0 = vec[:, VEC["norm_g0"]:VEC["norm_g0"] + KD]
            for n in range(2):
                own.mark(stt(scale[:, n], ada0[:, 8:16, n:n + 1].rearrange("p k n -> p (k n)"), 1.0, g0,
                             ALU.add, ALU.mult))
            own.wait()
            norm_apply(N0, lambda k: x0[:, k], lambda k: scale[:, 0, k:k + 1], lambda k: ada0[:, k, 0:1],
                       lambda k: st_tmp[:, k % 2], st_sq[:], lambda k: h_hi[:, k], lambda k: h_lo[:, k])
            norm_apply(N0C, lambda k: xc[:, k], lambda k: scale[:, 1, k:k + 1], lambda k: ada0[:, k, 1:2],
                       lambda k: st_tmpc[:, k % 2], st_tmpc[:, 2], lambda k: hc_hi[:, k], lambda k: hc_lo[:, k])
            dve.wait_ge(const_in_s, 16)

            def tree(l):
                if l == 0:
                    return f_st[:]
                at = TA - (TA >> (l - 1))
                return f_tree[:, :, at:at + (TA >> l)]

            def dve_head(i, j, f):
                def pe(n):
                    dve.wait_ge(pe_scan, j * PE_SCAN + n)

                def mine(n):
                    dve.wait_ge(dve_scan, j * DVE_SCAN + n)

                def next_block(k):
                    if i is not None:
                        after(k)

                def prepare():
                    if i is None:
                        return
                    dve.wait_ge(acc_free, i * 6 + 7)
                    if j is not None:
                        mine(11)
                        pe(17)
                    for d in range(2):
                        own.mark(ts(f_st[:, d], f_st[:, d], lbt[:, 5, ds(i + d * HEADS, 1)],
                                    lbt[:, 4, ds(i + d * HEADS, 1)], ALU.mult, ALU.add))
                    own.wait()
                    own.mark(ts(K[:], f_st[:], -1.0, 1.0, ALU.mult, ALU.add))
                    tt(Q[:], q_st[:].unsqueeze(1).broadcast_to([P, 2, T]), f_st[:, :, TC:TA], ALU.mult)
                    own.wait()
                    tt(ksum[:], K[:, 0, TC:TA], K[:, 1, TC:TA], ALU.add).then_inc(gates_ready, 1)

                def place(l, bank, signal=False):
                    last = v.copy_predicated(ST[:], masks[:, l].unsqueeze(1).broadcast_to([P, TT, P]),
                                             ps[:, bank].rearrange("p (t s) -> p t s", t=TT))
                    if signal:
                        last.then_inc(dve_scan, 1)
                    else:
                        own.mark(last)

                def merge(l):
                    n = 2 ** l
                    prev = tree(l).rearrange("p d (m h) -> p d m h", h=2)
                    if l == 0:
                        dve.wait_ge(gates_ready, j + 1)
                        pe(2)
                    own.mark(tt(tree(l + 1), prev[:, :, :, 0], prev[:, :, :, 1], ALU.mult))
                    if l == 0:
                        place(LEVELS, 4)
                    own.wait()
                    pe((3, 4, 6, 7, 8, 9, 10)[l])
                    if l:
                        mine(l)
                    for t, t0, size in ((Q, TC, T), (K, 0, TA)):
                        for d in range(2):
                            half = 1 - d if t is Q else d
                            part = t[:, d].rearrange("p (m h n) -> p m h n", h=2, n=n)[:, :, half]
                            by = prev[:, d, t0 // (2 * n):, 1 - half].unsqueeze(2).broadcast_to(
                                [P, size // (2 * n), n])
                            last = tt(part, part, by, ALU.mult)
                    last.then_inc(dve_scan, 1)
                    place(l, 5 - l % 2, l == LEVELS - 1)

                def passed(g_):
                    pe((12, 14, 16)[g_])
                    whole_tile = tree(LEVELS)
                    acc = ps[:, 4 + g_ % 2].rearrange("p (x c) -> p x c", c=P)
                    for x, n in enumerate(range(2 * g_, min(2 * g_ + 2, 5))):
                        if n == 0:
                            own.mark(v.tensor_copy(states[:, 0], acc[:, 0:2]))
                        else:
                            if x or g_ == 0:
                                own.wait()
                            for d in range(2):
                                tile_ = ORDER[d][n]
                                last = stt(states[:, n, d], states[:, n - 1, d], whole_tile[:, d, tile_:tile_ + 1],
                                           acc[:, 2 * x + d], ALU.mult, ALU.add)
                                if d == 1 and x == min(2, 5 - 2 * g_) - 1:
                                    last.then_inc(dve_scan, 1)
                                else:
                                    own.mark(last)

                def invert_root():
                    if f is not None:
                        dve.wait_ge(act_scan, (f + 1) * ACT_SCAN + 7)
                        own.link(v.reciprocal(rt[:], rt[:]))

                def gate_output():
                    if f is not None:
                        own.link(stt(ytmp[:], ps[:, 7], col("hg_g", 0), rt[:], ALU.mult, ALU.mult))
                        tt(ytmp[:], ytmp[:], z_cur[:], ALU.mult).then_inc(y_ready, 1)

                def cut_output():
                    if f is not None:
                        dve.wait_ge(y_hi_ready, f + 1)
                        tt(row(y_lo, f), ytmp[:], row(y_hi, f).bitcast(F32), ALU.subtract)

                def take_z():
                    if j is not None:
                        v.tensor_copy(z_cur[:], z_st[:]).then_inc(z_taken, 1)

                if j is None:
                    if i is not None:
                        for k in range(6):
                            after(k)
                        prepare()
                    invert_root()
                    gate_output()
                    cut_output()
                    return
                next_block(0)
                merge(0)
                merge(1)
                merge(2)
                next_block(1)
                merge(3)
                merge(4)
                merge(5)
                next_block(2)
                merge(6)
                invert_root()
                passed(0)
                gate_output()
                next_block(3)
                mine(9)
                passed(1)
                cut_output()
                take_z()
                mine(10)
                passed(2)
                next_block(4)
                prepare()
                next_block(5)

            st.enter(0, 6)
            dve_head(0, None, None)
            st.leave(1)
            st.enter(0, 6)
            dve_head(1, 0, None)
            st.leave(1)
            with dve.Fori(0, HEADS - 2) as f:
                st.enter(f, 6)
                own.enter(f, PER["head"])
                dve_head(f + 2, f + 1, f)
            st.leave(HEADS - 2)
            own.leave(HEADS - 2)
            dve_head(None, HEADS - 1, HEADS - 2)
            dve_head(None, None, HEADS - 1)
            phase_end()

            def residual(R, trips, nb, out_row, factor, n, sums, N=None, ahead=True):
                if sums:
                    open_sums(R, *sums)

                def one(i, cuts):
                    for a in range(2):
                        for q in range(nb):
                            if cuts:
                                after(a * nb + q)
                        st.wait_done(dve, a * nb + nb - 1)
                        r_ = out_row(i * 2 + a)
                        acc = ps[:, 2 * a:2 * a + 2, 0:HALF] if n == TM else ps[:, 2 * a]
                        r_ = halves(r_) if n == TM else r_
                        stt(r_, acc, factor(i * 2 + a), r_, ALU.mult, ALU.add).then_inc(R["res"], 1)
                        if sums:
                            add_square(R, i * 2 + a, *sums)

                n_loop = trips if ahead else trips - 1
                with dve.Fori(0, n_loop) as i:
                    st.enter(i, 2 * nb)
                    one(i, True)
                st.leave(n_loop)
                if not ahead:
                    st.enter(0, 2 * nb)
                    one(trips - 1, False)
                    st.leave(1)
                if sums:
                    close_sums(R, N, *sums)

            dve.wait_ge(x1_in_s, 16)
            residual(RC, KD // 2, 2, lambda m_: row(x1, m_), lambda m_: row(gates, m_)[:, 0:1], T,
                     (n1["sum"][:, 0], n1["sq"][:, 0]), N1)
            own.link(stt(scale[:, 2], ada1[:, 8:16, 0:1].rearrange("p k n -> p (k n)"), 1.0,
                         vec[:, VEC["norm_g1"]:VEC["norm_g1"] + KD], ALU.add, ALU.mult))
            norm_apply(N1, lambda k: x1[:, k], lambda k: scale[:, 2, k:k + 1], lambda k: ada1[:, k, 0:1],
                       lambda k: n1["tmp"][:, k % 2], n1["sq"][:, 0], lambda k: g_hi[:, k], lambda k: g_lo[:, k])
            dve.wait_ge(dft_split["act"], 1)
            tt(F_lo[:], F_raw[:], F_hi[:].bitcast(F32), ALU.subtract).then_inc(dft_split["dve"], 1)
            dve.wait_ge(dft_split["act"], 2)
            flat = "p a b c d -> p (a b c d)"
            tt(C_lo[:].rearrange(flat), C_raw[:].rearrange(flat), C_hi[:].rearrange(flat).bitcast(F32),
               ALU.subtract).then_inc(dft_split["dve"], 1)
            phase_end()

            def dve_group(i, j):
                def lo(n, dst, src, hi):
                    if j is not None:
                        dve.wait_ge(act_ft, j * 8 + n)
                        tt(dst, src, hi.bitcast(F32), ALU.subtract).then_inc(dve_ft, 1)

                def next_block(k):
                    if i is not None:
                        after(k)

                def mirror(m_):
                    if j is None:
                        return
                    e = ps[:, 4 + 2 * m_]
                    dve.wait_ge(act_ft, j * 8 + (5 + 2 * m_))
                    dve.wait_ge(ft_acc, j * 4 + 6)
                    tt(yf[:, 1:256], e[:, 1:256], o_sb[:, 1:256], ALU.subtract)
                    tt(yf[:, 511:256:-1], e[:, 1:256], o_sb[:, 1:256], ALU.add)
                    own.link(v.tensor_copy(yf[:, 0:512:256], e[:, 0:512:256]))
                    dve.wait_ge(dve_ft, j * 8 + (5 + 2 * m_))
                    tt(yg[:], yf[:], zf_st[:, m_], ALU.mult).then_inc(dve_ft, 1)
                    dve.wait_ge(act_ft, j * 8 + (6 + 2 * m_))
                    tt(row(y_lo, j * 2 + m_), yg[:], row(y_hi, j * 2 + m_).bitcast(F32), ALU.subtract
                       ).then_inc(dve_ft, 1)

                lo(1, u_lo[:, 0], ps[:, 4], u_hi[:, 0])
                lo(2, u_lo[:, 1], ps[:, 5], u_hi[:, 1])
                next_block(0)
                lo(3, p_lo[:, 0], ps[:, 6], p_hi[:, 0])
                next_block(1)
                lo(4, p_lo[:, 1], ps[:, 7], p_hi[:, 1])
                next_block(2)
                mirror(0)
                next_block(3)
                mirror(1)

            st.enter(0, 4)
            dve_group(0, None)
            st.leave(1)
            with dve.Fori(0, GROUPS - 1) as j:
                st.enter(j, 4)
                own.enter(j, 2)
                dve_group(j + 1, j)
            st.leave(GROUPS - 1)
            own.leave(GROUPS - 1)
            dve_group(None, GROUPS - 1)

            residual(RF, KD // 2, 2, lambda m_: row(x1, m_), lambda m_: row(gates, m_ + KD)[:, 0:1], T,
                     (n1["sum"][:, 0], n1["sq"][:, 0]), NFIN)
            phase_end()
            dve.wait_ge(NFIN["root"], 1)
            own.link(v.reciprocal(n1["sq"][:, 0], n1["sq"][:, 0]))
            dve.wait_ge(meta_in_s, 16)
            for k in range(KD):
                stt(hb[:, k, META:TM], x1[:, k], col("final_g", k), n1["sq"][:, 0], ALU.mult, ALU.mult
                    ).then_inc(RA["res"], 1)
            sum_squares(RA, KD, n2["sum"][:, 0], n2["sq"][:, 0])
            dve.wait_ge(RA["add"], KD)
            dve.sem_inc(NF1["sum"], 1)

            def block_norm(N, name, n):
                c0 = TM - n
                norm_apply(N, lambda k: hb[:, k, c0:TM], lambda k: col(name, k), lambda k: zero[:],
                           lambda k: n2["tmp"][:, k % 2, 0:n], n2["sq"][:, 0, 0:n],
                           lambda k: n_hi[:, k, c0:TM], lambda k: n_lo[:, k, c0:TM])

            def feed_forward(tags, last_R, N, n, last):
                c0 = TM - n
                for tag, count in zip(tags, FF_GROUPS):
                    S, before = ffn[tag]
                    with dve.Fori(0, count) as i:
                        st.enter(i, 2)
                        after(0)
                        after(1)
                        st.wait_done(dve, 1)
                        dve.wait_ge(S["gate"], i + (before + 2))
                        dve.wait_ge(S["lo"], i + (before + 1))
                        acc = ps[:, 2:4, 0:HALF] if n == TM else ps[:, 2]
                        a, b_ = (halves(hid[:]), halves(sg[:])) if n == TM else (hid[:, 0:n], sg[:, 0:n])
                        tt(a, acc, b_, ALU.mult).then_inc(S["up"], 1)
                        dve.wait_ge(S["hi"], i + (before + 1))
                        tt(row(hid_lo, i)[:, c0:TM], hid[:, 0:n], row(hid_hi, i)[:, c0:TM].bitcast(F32),
                           ALU.subtract).then_inc(S["lo"], 1)
                    st.leave(count)
                    final = tag == tags[-1]
                    sums = (n2["sum"][:, 0, 0:n], n2["sq"][:, 0, 0:n]) if final else None
                    residual(last_R if final else RP[tag], KD // 2, 1, lambda m_: row(hb, m_)[:, c0:TM],
                             lambda m_: 0.5, n, sums, N, not (final and last))

            block_norm(NF1, "ffn1_g", TM)
            feed_forward(("f1a", "f1b", "f1c"), RD1, NMIX, TM, False)
            block_norm(NMIX, "mix_g", TM)
            phase_end()

            own.mark(v.memset(vpad[:, 0:DW - 1], 0.0))
            own.link(v.memset(xpad[:, :, 0:RW - 1], 0.0))
            with dve.Fori(0, KD // 2) as i:
                st.enter(i, 14)
                own.enter(i, PER["mix"])

                def staged(k):
                    dve.wait_ge(mx_acc, i * 14 + (k + 3))

                def mine(n):
                    dve.wait_ge(mx_dve, i * 12 + n)

                def actv(n):
                    dve.wait_ge(mx_act, i * 8 + n)

                def tap(a, t):
                    dst = row(cv, i * 2 + a)
                    src = vpad[:, META + t:META + t + T]
                    w_ = col("dw", i * 2 + (t * KD + a))
                    if t == 0:
                        own.link(ts(dst, src, w_, col("dwb", i * 2 + a), ALU.mult, ALU.add))
                    else:
                        own.link(stt(dst, src, w_, dst, ALU.mult, ALU.add))

                def product(a):
                    staged(3 + 2 * a)
                    tt(vpad[:, DW - 1:DW - 1 + TM], gvs[:], ggs[:], ALU.mult).then_inc(mx_dve, 1)
                    mine(5 + a)

                after(0)
                after(1)
                for a in range(2):
                    staged(a)
                    for t in range(RW):
                        src = xpad[:, a, t:t + TM]
                        w_ = col("rw", i * 2 + (t * KD + a))
                        if t == 0:
                            own.link(ts(xr[:, a], src, w_, col("rb", i * 2 + a), ALU.mult, ALU.add))
                        elif t < RW - 1:
                            own.link(stt(xr[:, a], src, w_, xr[:, a], ALU.mult, ALU.add))
                        else:
                            stt(xr[:, a], src, w_, xr[:, a], ALU.mult, ALU.add).then_inc(mx_dve, 1)
                after(2)
                for a in range(2):
                    actv(1 + a)
                    tt(xr_lo[:, a], xr[:, a], xr_hi[:, a].bitcast(F32), ALU.subtract).then_inc(mx_dve, 1)
                after(3)
                product(0)
                taps = [(0, t) for t in range(DW)]
                for k, count in ((4, 5), (5, 5), (6, 6), (7, 6), (8, 7)):
                    for _ in range(count):
                        if taps:
                            tap(*taps.pop(0))
                    after(k)
                while taps:
                    tap(*taps.pop(0))
                product(1)
                taps = [(1, t) for t in range(DW)]
                for k, count in ((9, 6), (10, 7), (11, 7), (12, 6), (13, 5)):
                    after(k)
                    for _ in range(count):
                        tap(*taps.pop(0))
                for a in range(2):
                    actv(3 + a)
                    tt(ii[:, a], ii[:, a], xr[:, a], ALU.mult)
                    stt(pp[:, a], (gvs, ggs)[a][:], 1.0, pp[:, a], ALU.add, ALU.mult).then_inc(mx_dve, 1)
                for a in range(2):
                    actv(5 + a)
                    own.link(tt(ii[:, a], ii[:, a], pp[:, a], ALU.mult))
                    own.link(v.tensor_tensor_scan(pp[:, a], rr[:, a], ii[:, a], 0.0, ALU.mult, ALU.add))
                    tt(yst[:, a], yst[:, a], pp[:, a, META:TM], ALU.mult).then_inc(mx_dve, 1)
                for a in range(2):
                    actv(7 + a)
                    tt(row(a_lo, i * 2 + a), yst[:, a], row(a_hi, i * 2 + a).bitcast(F32), ALU.subtract
                       ).then_inc(mx_dve, 1)
            st.leave(KD // 2)
            own.leave(KD // 2)
            phase_end()

            lroot = n2["sq"][:, 0, 0:T]

            def gated(i, a, done):
                m_ = i * 2 + (a + done)
                after(a)
                st.wait_done(dve, a)
                tt(row(gate[:, 0], m_), ps[:, 2 * a], row(gate[:, 0], m_), ALU.mult).then_inc(YA["res"], 1)

            dve.wait_ge(ln_pe, 1)
            with dve.Fori(0, 2) as i:
                st.enter(i, 2)
                for a in range(2):
                    for n in (2 * a, 2 * a + 1):
                        tile_ = row(cv, i * 4 + n)
                        tt(tile_, tile_, ps[:, 6], ALU.subtract).then_inc(ln_dve, 1)
                    gated(i, a, 0)
            st.leave(2)
            dve.wait_ge(ln_act, KD + 1)
            own.link(v.reciprocal(lroot, lroot))
            with dve.Fori(0, 2) as i:
                st.enter(i, 2)
                for a in range(2):
                    gated(i, a, 4)
                    for n in (2 * a, 2 * a + 1):
                        stt(row(cv, i * 4 + n), row(cv, i * 4 + n), col("ln_g", i * 4 + n), lroot,
                            ALU.mult, ALU.mult).then_inc(ln_norm, 1)
                    for n in (2 * a, 2 * a + 1):
                        dve.wait_ge(ln_hi, i * 4 + (n + 1))
                        tt(row(n_lo, i * 4 + n)[:, 0:T], row(cv, i * 4 + n),
                           row(n_hi, i * 4 + n)[:, 0:T].bitcast(F32), ALU.subtract).then_inc(ln_lo, 1)
            st.leave(2)

            with dve.Fori(0, KD // 2) as i:
                st.enter(i, 2)
                for a in range(2):
                    m_ = i * 2 + a
                    after(a)
                    st.wait_done(dve, a)
                    stt(mt[:, a], ps[:, 2 * a], col("cpb", m_), row(gate[:, 1], m_), ALU.add, ALU.mult
                        ).then_inc(YA["res"], 1)
                    dve.wait_ge(YA["res"], i * 2 + (a + KD + 3))
                    tt(mt[:, a], mt[:, a], row(gate[:, 0], m_), ALU.add).then_inc(mg_sum, 1)
                    dve.wait_ge(mg_hi_s, m_ + 1)
                    tt(row(mg_lo, m_), mt[:, a], row(mg_hi, m_).bitcast(F32), ALU.subtract).then_inc(mg_lo_s, 1)
            st.leave(KD // 2)
            residual(RM, KD // 2, 1, lambda m_: row(hb, m_)[:, META:TM], lambda m_: 1.0, T,
                     (n2["sum"][:, 0, 0:T], n2["sq"][:, 0, 0:T]), NF2)
            phase_end()
            block_norm(NF2, "ffn2_g", T)
            feed_forward(("f2a", "f2b", "f2c"), RD2, NOUT, T, True)
            dve.wait_ge(NOUT["root"], 1)
            own.link(v.reciprocal(n2["sq"][:, 0, 0:T], n2["sq"][:, 0, 0:T]))
            for k in range(KD):
                stt(fin[:, k], hb[:, k, META:TM], col("out_g", k), n2["sq"][:, 0, 0:T], ALU.mult, ALU.mult
                    ).then_inc(NOUT["lo"], 1)


def _cols(a):
    return np.asarray(a).reshape(-1, P).T


def _blocks(w, ks=None):
    w = np.asarray(w)
    k, m = w.shape[0] // P, w.shape[1] // P
    tiles = w.reshape(k, P, m, P).transpose(2, 1, 0, 3)
    groups, at = [], 0
    for n in ks or (KD,) * (k // KD):
        part = tiles[:, :, at:at + n]
        if n < KD:
            part = np.concatenate([part, np.zeros((m, P, KD - n, P), w.dtype)], axis=2)
        groups.append(part.reshape(m, P, BLK))
        at += n
    return groups


def _stream(i):
    out = []
    a1 = _blocks(i["ada_w"][1])[0]
    hg = _blocks(i["hg_w_in"][0])[0].reshape(5, HEADS, P, BLK)
    for h in range(HEADS):
        out += [*hg[:, h], a1[h]]
    wo = _blocks(i["hg_w_out"][0])
    for m in range(KD):
        out += [wo[0][m], wo[1][m]]
    fi = _blocks(i["ft_w_in"][0])[0].reshape(2, HEADS, P, BLK)
    for g in range(GROUPS):
        out += [fi[0, 2 * g], fi[0, 2 * g + 1], fi[1, 2 * g], fi[1, 2 * g + 1]]
    fo = _blocks(i["ft_w_out"][0])
    for m in range(KD):
        out += [fo[0][m], fo[1][m]]

    def feed_forward(name):
        gu, down = _blocks(i[name + "_w_gu_2"][0])[0], _blocks(i[name + "_w_down_2"][0], FF_GROUPS)
        blocks, at = [], 0
        for n, d in zip(FF_GROUPS, down):
            for j in range(at, at + n):
                blocks += [gu[j], gu[FT + j]]
            blocks += list(d)
            at += n
        return blocks

    out += feed_forward("ffn1")
    wi = _blocks(i["w_in_2"][0])[0].reshape(6, KD, P, BLK)
    heads = []
    for name in ("rg_w_a_2", "rg_w_x_2"):
        w = np.asarray(i[name][0]).reshape(4, 2, P, 2, P).transpose(0, 2, 3, 1, 4).reshape(4, P, 4 * P)
        heads.append(np.concatenate([w, np.zeros_like(w)], axis=2))
    for n in range(KD // 2):
        a, b = 2 * n, 2 * n + 1
        out += [wi[0, a], wi[0, b], wi[2, a], wi[3, a], wi[2, b], wi[3, b], wi[1, a], wi[1, b],
                wi[4, a], wi[5, a], wi[4, b], wi[5, b], heads[0][n], heads[1][n]]
    rn, cp = _blocks(i["rnn_w_proj_2"][0])[0], _blocks(i["conv_w_proj_2"][0])[0]
    out += [*rn, *cp]
    out += list(_blocks(i["w_out_2"][0])[0])
    out += feed_forward("ffn2")
    return np.stack(out)


def _ada(i):
    a0, a1 = _blocks(i["ada_w"][0])[0], _blocks(i["ada_w"][1])[0]
    return np.ascontiguousarray(a0[:16]), np.concatenate([a0[16:], a1[16:]])


def _vectors(i):
    c = np.stack([_cols(i["c"][0]), _cols(i["c_ctx"])], axis=2).reshape(P, 2 * KD)
    lb = np.asarray(i["hg_lb_logits"]).reshape(2, 2, HEADS, P).transpose(3, 0, 1, 2).reshape(P, -1)
    b0, b1 = _cols(i["ada_b"][0]), _cols(i["ada_b"][1])
    parts = [c, b0[:, :16], b0[:, 16:], b1[:, 16:], b1[:, :16], _cols(i["norm_g"][0]), _cols(i["norm_g"][1]), lb,
             _cols(i["hg_norm_g"][0]), _cols(i["final_g"]), _cols(i["ffn1_norm_2"][0]), _cols(i["mix_norm_2"][0]),
             _cols(i["b_in_2"][0]), _cols(i["rnn_conv_w_2"][0]), _cols(i["rnn_conv_b_2"][0]),
             _cols(i["rg_b_a_2"][0]), _cols(i["rg_b_x_2"][0]), _cols(i["rg_lambda_2"][0]),
             _cols(i["conv_dw_w_2"][0]), _cols(i["conv_dw_b_2"][0]), _cols(i["conv_ln_g_2"][0]),
             _cols(i["conv_ln_b_2"][0]), _cols(i["conv_b_proj_2"][0]), _cols(i["ffn2_norm_2"][0]),
             _cols(i["final_norm_2"])]
    return np.ascontiguousarray(np.concatenate(parts, axis=1))


def _turned(a):
    a = np.asarray(a)
    return np.ascontiguousarray(a.reshape(a.shape[0], KD, P).transpose(2, 1, 0))


def _tables():
    s, t = np.arange(P)[:, None], np.arange(P)[None, :]
    masks = [(s // (2 * n) == t // (2 * n)) & (s // n != t // n) for n in (2 ** l for l in range(LEVELS))]
    masks = np.stack(masks + [s == t], axis=1).astype(np.int32)
    tok = np.arange(T)[:, None]
    seq = np.concatenate([np.cos(2 * np.pi * (tok * np.arange(257)[None] % T) / T),
                          np.sin(2 * np.pi * (tok * np.arange(1, 256)[None] % T) / T)], axis=1) / np.sqrt(T)
    seq = seq.reshape(TT, P, T).transpose(1, 0, 2).astype(np.float32)
    ch = np.arange(256)
    ang = 2 * np.pi * (ch[:, None] * ch[None] % 256) / 256
    chan = np.stack([np.cos(ang), np.sin(ang)]) / np.sqrt(256)
    chan = chan.reshape(2, 2, P, 2, P).transpose(2, 0, 1, 3, 4).astype(np.float32)
    return masks, np.eye(P, dtype=np.float32), np.ascontiguousarray(seq), np.ascontiguousarray(chan)


def kernel(**inputs):
    import concourse.bacc as _bacc
    from concourse.bass_utils import run_bass_kernel_spmd as _run

    nc = _bacc.Bacc("TRN2", target_bir_lowering=False, num_devices=1)
    i = {k: np.asarray(v) for k, v in inputs.items()}
    masks, ident, seq, chan = _tables()
    given = {"weights": _stream(i), "ada_weights": _ada(i)[0], "gate_weights": _ada(i)[1], "x": _turned(i["x"][0]), "ctx": _turned(i["ctx"][0]),
             "meta": _turned(i["meta_tokens_2"]), "vectors": _vectors(i), "masks": masks,
             "identity": ident, "seq_dft": seq, "chan_dft": chan}
    arrays, args = {}, []
    for name, a in given.items():
        arrays[f"in_{name}_dram"] = a
        args.append(nc.dram_tensor(f"in_{name}_dram", a.shape, mybir.dt.from_np(a.dtype), kind="ExternalInput").ap())
    args.append(nc.dram_tensor("out_0_dram", (P, KD, T), F32, kind="ExternalOutput").ap())
    program(nc, *args)
    r = _run(nc, [arrays], core_ids=[0])
    return np.ascontiguousarray(r.results[0]["out_0_dram"].transpose(2, 1, 0).reshape(1, T, D))
```

```python
from contextlib import ExitStack

import numpy as np

import concourse.bass as bass
from concourse import mybir

F32 = mybir.dt.float32
F32R = mybir.dt.float32r
I32 = mybir.dt.int32
ALU = mybir.AluOpType
ACT = mybir.ActivationFunctionType
ds = bass.ds

P = 128
D = 1024
KD = D // P
E = 2048
HEADS = E // P
T = 512
TT = T // P
TC = 256
CT = TC // P
TA = TC + T
AT = TA // P
GROUPS = 8
META = 16
TM = META + T
HALF = TM // 2
DFF = 2816
FT = DFF // P
FF_GROUPS = (8, 8, 6)
DW = 31
RW = 4
EARLY = 4
EPS = 1e-6
LEVELS = 7
BLK = KD * P
BF = 258

_sizes = [("c", 2 * KD), ("ada_b0", 16), ("gate_b", 16), ("ada_b1", 16), ("norm_g0", KD), ("norm_g1", KD),
          ("lb", 2 * 2 * HEADS), ("hg_g", 1), ("final_g", KD), ("ffn1_g", KD), ("mix_g", KD),
          ("b_in", 48), ("rw", RW * KD), ("rb", KD), ("b_a", KD), ("b_x", KD), ("lam", KD),
          ("dw", DW * KD), ("dwb", KD), ("ln_g", KD), ("ln_b", KD), ("cpb", KD), ("ffn2_g", KD),
          ("out_g", KD)]
VEC = {}
_at = 0
for _n, _s in _sizes:
    VEC[_n] = _at
    _at += _s
NVEC = _at


PER = {"head": 25, "mix": 74}

WIDE = (0, 1, 2, 3, 4, 5, 7, 8, 10, 11, 12, 13)
RG_A, RG_X = 6, 9

ORDER = ((0, 1, 2, 3, 4), (1, 0, 5, 4, 3))


class Own:

    def __init__(self, eng, sem):
        self.eng, self.sem, self.base, self.i, self.per, self.n = eng, sem, 0, 0, 0, 0

    def mark(self, instruction):
        instruction.then_inc(self.sem, 1)
        self.n += 1

    def wait(self, lag=0):
        self.eng.wait_ge(self.sem, self.i * self.per + self.base + self.n - lag)

    def link(self, instruction):
        self.mark(instruction)
        self.wait()

    def enter(self, i, per):
        self.base += self.n
        self.n, self.i, self.per = 0, i, per

    def leave(self, trips):
        assert self.n == self.per, f"{self.sem.name}: {self.n} signals an iteration, not {self.per}"
        self.base += trips * self.per
        self.n, self.i, self.per = 0, 0, 0


class Region:

    def __init__(self, nc, start):
        self.nc, self.at, self.start = nc, start, start

    def take(self, name, shape, dt=F32):
        size = int(np.prod(shape[1:])) * 4
        tensor = self.nc.alloc_sbuf_tensor_at(name, shape, dt, offset=self.at)
        self.at += (size + 31) // 32 * 32
        return tensor

    def over(self):
        return Region(self.nc, self.at)


def halves(ap):
    return ap.rearrange("p (a b) -> p a b", a=2)


def program(nc, wts, ada_in, gate_in, x_in, ctx_in, meta_in, vec_in, mask_in, ident_in, dft_in, chan_in, out):
    nblocks = wts.shape[0]
    with ExitStack() as top:
        def sem(name):
            return top.enter_context(nc.semaphore(name))

        g = Region(nc, (nc.sbuf_base + 63) // 64 * 64)
        w_raw = g.take("w_raw", [P, 2, BLK])
        w_hi = g.take("w_hi", [P, 2, BLK], F32R)
        w_lo = g.take("w_lo", [P, 2, BLK], F32R)
        vec = g.take("vec", [P, NVEC])
        ones_d = g.take("ones_d", [P, P])
        ones_h = g.take("ones_h", [P, P])
        ident = g.take("ident", [P, P])
        eps = g.take("eps", [P, 1])
        zero = g.take("zero", [P, 1])
        tiny = g.take("tiny", [P, 1])
        unused = g.take("unused", [P, 1])
        ada0 = g.take("ada0", [P, 16, 2])
        ada1 = g.take("ada1", [P, 16, 2])
        gates = g.take("gates", [P, 16, 2])
        scale = g.take("scale", [P, 3, KD])
        csil = g.take("csil", [P, KD, 2])
        c_hi = g.take("c_hi", [P, KD, 2], F32R)
        c_lo = g.take("c_lo", [P, KD, 2], F32R)
        lbt = g.take("lbt", [P, 6, 2 * HEADS])
        rgc = g.take("rgc", [P, 8, KD])
        r = g.over()
        x0 = r.take("x0", [P, KD, T])
        xc = r.take("xc", [P, KD, TC])
        st_sum, st_sq = r.take("st_sum", [P, 2, T]), r.take("st_sq", [P, T])
        st_tmp, st_tmpc = r.take("st_tmp", [P, 2, T]), r.take("st_tmpc", [P, 3, TC])
        r_tail = r.over()
        r = g.over()
        y_hi = r.take("y_hi", [P, HEADS, T], F32R)
        y_lo = r.take("y_lo", [P, HEADS, T], F32R)
        h = r.over()
        h_hi, h_lo = h.take("h_hi", [P, KD, T], F32R), h.take("h_lo", [P, KD, T], F32R)
        hc_hi, hc_lo = h.take("hc_hi", [P, KD, TC], F32R), h.take("hc_lo", [P, KD, TC], F32R)
        h_tail = h.over()
        q_st = h.take("q_st", [P, T])
        f_st = h.take("f_st", [P, 2, TA])
        v_st = h.take("v_st", [P, TA])
        z_st = h.take("z_st", [P, T])
        z_cur = h.take("z_cur", [P, T])
        Q = h.take("Q", [P, 2, T])
        K = h.take("K", [P, 2, TA])
        ksum = h.take("ksum", [P, T])
        f_tree = h.take("f_tree", [P, 2, TA])
        V = h.take("V", [P, AT, P])
        KT = h.take("KT", [P, 4, P])
        ST = h.take("ST", [P, TT, P])
        states = h.take("states", [P, 5, 2, P])
        osq, rt, ytmp = h.take("osq", [P, T]), h.take("rt", [P, T]), h.take("ytmp", [P, T])
        masks = h.take("masks", [P, LEVELS + 1, P], I32)
        gate_raw = h.take("gate_raw", [P, BLK])
        ada_raw = (r_tail.take("ada_raw0", [P, 4, BLK]), h_tail.take("ada_raw1", [P, 12, BLK]))
        ada_row = r_tail.take("ada_row", [2, 4, T])
        f = r.over()
        x1 = f.take("x1", [P, KD, T])
        n1 = {k: f.take(f"n1_{k}", [P, 2 if k == "tmp" else 1, T]) for k in ("sum", "sq", "tmp")}
        g_hi, g_lo = f.take("g_hi", [P, KD, T], F32R), f.take("g_lo", [P, KD, T], F32R)
        F_hi = f.take("F_hi", [P, TT, T], F32R)
        F_lo = f.take("F_lo", [P, TT, T], F32R)
        C_hi = f.take("C_hi", [P, 2, 2, 2, P], F32R)
        C_lo = f.take("C_lo", [P, 2, 2, 2, P], F32R)
        raw = f.over()
        F_raw, C_raw = raw.take("F_raw", [P, TT, T]), raw.take("C_raw", [P, 2, 2, 2, P])
        u_st, zf_st = f.take("u_st", [P, 2, T]), f.take("zf_st", [P, 2, T])
        u_hi, u_lo = f.take("u_hi", [P, 2, T], F32R), f.take("u_lo", [P, 2, T], F32R)
        p_hi, p_lo = f.take("p_hi", [P, 2, T], F32R), f.take("p_lo", [P, 2, T], F32R)
        o_sb, yf, yg = f.take("o_sb", [P, 256]), f.take("yf", [P, T]), f.take("yg", [P, T])
        b = g.over()
        hb = b.take("hb", [P, KD, TM])
        n2 = {k: b.take(f"n2_{k}", [P, 2 if k == "tmp" else 1, TM]) for k in ("sum", "sq", "tmp")}
        squares8 = b.over().take("squares8", [P, KD, TM])
        n_hi, n_lo = b.take("n_hi", [P, KD, TM], F32R), b.take("n_lo", [P, KD, TM], F32R)
        assert b.at <= r.at
        m = b.over()
        hid_hi, hid_lo = m.take("hid_hi", [P, 8, TM], F32R), m.take("hid_lo", [P, 8, TM], F32R)
        sg, hid = m.take("sg", [P, TM]), m.take("hid", [P, TM])
        m = b.over()
        a_hi, a_lo = m.take("a_hi", [P, KD, T], F32R), m.take("a_lo", [P, KD, T], F32R)
        gate = m.take("gate", [P, 2, KD, T])
        mk = m.over()
        cv = mk.take("cv", [P, KD, T])
        gvs, ggs = mk.take("gvs", [P, TM]), mk.take("ggs", [P, TM])
        vpad = mk.take("vpad", [P, DW - 1 + TM])
        xpad = mk.take("xpad", [P, 2, RW - 1 + TM + 1])
        xr = mk.take("xr", [P, 2, TM])
        xr_hi, xr_lo = mk.take("xr_hi", [P, 2, TM], F32R), mk.take("xr_lo", [P, 2, TM], F32R)
        yst = mk.take("yst", [P, 2, T])
        rr, ii = mk.take("rr", [P, 2, TM]), mk.take("ii", [P, 2, TM])
        pp, odd_taps = mk.take("pp", [P, 2, TM]), n2["tmp"][:, 1, 0:T]
        m = m.over()
        mg_hi, mg_lo = m.take("mg_hi", [P, KD, T], F32R), m.take("mg_lo", [P, KD, T], F32R)
        mt, centred_sq = m.take("mt", [P, 2, T]), m.take("centred_sq", [P, KD, T])
        m = b.over()
        fin = m.take("fin", [P, KD, T])

        ps = top.enter_context(nc.psum_tensor("ps", [P, 8, T], F32))

        w_loaded = [sem(f"w_loaded{s}") for s in range(2)]
        hi_ready = [sem(f"hi_ready{s}") for s in range(2)]
        lo_ready = [sem(f"lo_ready{s}") for s in range(2)]
        w_used = [sem(f"w_used{s}") for s in range(2)]
        phase_over = sem("phase_over")
        vec_in_s, x_in_s, xc_in_s, const_in_s, dft_in_s, chan_in_s, x1_in_s, meta_in_s, out_s = [
            sem(n) for n in ("vec_loaded", "x_loaded", "ctx_loaded", "const_loaded", "dft_loaded",
                             "chan_loaded", "x1_loaded", "meta_loaded", "out_stored")]
        ident_in_s = sem("ident_loaded")
        ADA_LOADS = [(ada_raw[0][:], 0, 4), (ada_raw[1][:, 0:4], 4, 8), (ada_raw[1][:, 4:8], 8, 12),
                     (ada_raw[1][:, 8:12], 12, 16)]
        ada_part = sem("ada_part")
        ada_loaded = [sem(f"ada_loaded{n}") for n in range(len(ADA_LOADS))]
        gate_loaded, gate_used = sem("gate_loaded"), sem("gate_used")
        consts_set = sem("consts_set")
        small = {e: sem(f"small_{e}") for e in ("act", "dve")}
        own_s = {e: sem(f"own_{e}") for e in ("act", "dve")}
        ada_done, ada_copied = sem("ada_done"), sem("ada_copied")
        acc_free = sem("acc_free")
        pe_scan, act_scan, dve_scan = sem("pe_scan"), sem("act_scan"), sem("dve_scan")
        PE_SCAN, ACT_SCAN, DVE_SCAN = 18, 7, 11
        gates_ready = sem("gates_ready")
        y_ready, y_hi_ready = sem("y_ready"), sem("y_hi_ready")
        y_cut = sem("y_cut")
        z_taken = sem("z_taken")

        def residual_sems(tag):
            return {k: sem(f"{tag}_{k}") for k in ("res", "sq", "add")}

        def norm_sems(tag):
            return {k: sem(f"{tag}_{k}") for k in ("sum", "mean", "root", "tmp", "hi", "lo")}

        N0, N0C, N1, NFIN, NF1, NMIX, NF2, NOUT = [
            norm_sems(t) for t in ("n0", "n0c", "n1", "nfin", "nf1", "nmix", "nf2", "nout")]
        R0, R0C, RC, RF, RA, RD1, RM, RD2 = [
            residual_sems(t) for t in ("r0", "r0c", "rc", "rf", "ra", "rd1", "rm", "rd2")]
        ft_acc, pe_ft, act_ft, dve_ft = sem("ft_acc"), sem("pe_ft"), sem("act_ft"), sem("dve_ft")
        dft_split = {e: sem(f"dft_split_{e}") for e in ("act", "dve")}
        ffn = {}
        for f_ in ("f1", "f2"):
            sems = {k: sem(f"{f_}_{k}") for k in ("gate", "up", "hi", "lo")}
            ffn |= {f"{f_}{c}": (sems, n_ * 8) for n_, c in enumerate("abc")}
        RP = {t: {"res": sem(f"{t}_res")} for t in ("f1a", "f1b", "f2a", "f2b")}
        mx_acc, mx_act, mx_dve = sem("mx_acc"), sem("mx_act"), sem("mx_dve")
        ln_pe, ln_act, ln_dve = sem("ln_pe"), sem("ln_act"), sem("ln_dve")
        ln_norm, ln_silu, ln_hi, ln_lo = [sem(f"ln_{n}") for n in ("norm", "silu", "hi", "lo")]
        conv_done = sem("conv_done")
        YA = {"res": sem("projection_read")}
        mg_sum, mg_hi_s, mg_lo_s = sem("mg_sum"), sem("mg_hi_done"), sem("mg_lo_done")

        def col(name, j, n=1):
            return vec[:, ds(VEC[name] + j, n)]

        def row(t, j):
            return t[:, j] if isinstance(j, int) else t[:, ds(j, 1)].rearrange("p a n -> p (a n)")

        def rate(j):
            return rgc[:, 6:8].rearrange("p a k -> p (a k)")[:, ds(j, 1)]

        class Stream:

            def __init__(self):
                self.base, self.i, self.per = 0, 0, 0

            def enter(self, i, per):
                self.i, self.per = i, per

            def leave(self, trips):
                self.base += trips * self.per
                self.i = self.per = 0

            def slot(self, k):
                return k % 2, self.i * (self.per // 2) + (self.base // 2 + k // 2)

            def wait_done(self, eng, k):
                s, use = self.slot(k)
                eng.wait_ge(w_used[s], use + 2)

        block = top.enter_context(nc.Block())

        @block.sync
        def _(sp):
            sp.dma_start(vec[:], vec_in).then_inc(vec_in_s, 16)
            sp.dma_start(x0[:], x_in).then_inc(x_in_s, 16)
            for n, (dst, a, b_) in enumerate(ADA_LOADS):
                sp.dma_start(dst, ada_in[a:b_].rearrange("b p n -> p b n")).then_inc(ada_loaded[n], 16)
            with sp.Fori(0, nblocks // 2) as i:
                for s in range(2):
                    sp.wait_ge(lo_ready[s], i + 1)
                    sp.dma_start(w_raw[:, s], wts[ds(i * 2 + s, 1)].rearrange("a p n -> p (a n)")
                                 ).then_inc(w_loaded[s], 16)

        @block.gpsimd
        def _(pool):
            pool.dma_start(xc[:], ctx_in).then_inc(xc_in_s, 16)
            pool.dma_start(masks[:], mask_in).then_inc(const_in_s, 16)
            pool.dma_start(ident[:], ident_in).then_inc(ident_in_s, 16)
            with pool.Fori(0, HEADS) as i:
                pool.wait_ge(gate_used, i + 1)
                pool.dma_start(gate_raw[:], gate_in[ds(i, 1)].rearrange("a p n -> p (a n)")
                               ).then_inc(gate_loaded, 16)
            pool.wait_ge(w_used[1], 3 * HEADS + 1)
            pool.dma_start(x1[:], x_in).then_inc(x1_in_s, 16)
            pool.wait_ge(y_cut, HEADS)
            pool.dma_start(F_raw[:], dft_in).then_inc(dft_in_s, 16)
            pool.dma_start(C_raw[:], chan_in).then_inc(chan_in_s, 16)
            pool.wait_ge(NFIN["mean"], 1)
            pool.dma_start(hb[:, :, 0:META], meta_in).then_inc(meta_in_s, 16)
            pool.wait_ge(NOUT["lo"], KD)
            pool.dma_start(out, fin[:]).then_inc(out_s, 16)
            pool.wait_ge(out_s, 16)

        @block.tensor
        def _(pe):
            st = Stream()
            over = [0]

            def phase_end():
                over[0] += 1
                pe.drain().then_inc(phase_over, 1)
                pe.wait_ge(phase_over, 3 * over[0])

            def three(outs, whi, wlo, xhi, xlo, start, stop):
                for n, (w, x) in enumerate(((whi, xhi), (whi, xlo), (wlo, xhi))):
                    for o, xp in zip(outs, x):
                        last = nc.tensor.matmul(o, w, xp, start=start and n == 0,
                                                stop=stop and n == 2)
                return last

            def take(k):
                s, use = st.slot(k)
                pe.wait_ge(lo_ready[s], use + 2)
                return s

            def tiles(s, outs, xs, ks, start, stop, first=0):
                for n, k in enumerate(ks):
                    c = slice((first + n) * P, (first + n + 1) * P)
                    last = three(outs, w_hi[:, s, c], w_lo[:, s, c], *xs(k),
                                 start=start and n == 0, stop=stop and n == len(ks) - 1)
                return last

            def whole(hi, lo, a=0, b=T):
                return lambda k: ([hi[:, k, a:b]], [lo[:, k, a:b]])

            def halved(hi, lo):
                return lambda k: ([hi[:, k, 0:HALF], hi[:, k, HALF:TM]],
                                  [lo[:, k, 0:HALF], lo[:, k, HALF:TM]])

            def bank2(b):
                return [ps[:, b, 0:HALF], ps[:, b + 1, 0:HALF]]

            def mean(N, n, src):
                pe.wait_ge(N["sum"], 1)
                if n == TM:
                    for q in range(2):
                        last = nc.tensor.matmul(ps[:, 6 + q, 0:HALF], ones_d[:], src[:, q * HALF:(q + 1) * HALF],
                                                start=True, stop=True)
                else:
                    last = nc.tensor.matmul(ps[:, 6, 0:n], ones_d[:], src[:, 0:n], start=True, stop=True)
                last.then_inc(N["mean"], 1)

            def tile_cols(t):
                return slice(t * P, (t + 1) * P)

            pe.sem_inc(w_used[0], 1)
            pe.sem_inc(w_used[1], 1)
            pe.sem_inc(gate_used, 1)

            pe.wait_ge(consts_set, 4)
            for n, (raw_, a, b_) in enumerate(ADA_LOADS):
                if n == 3:
                    mean(N0, T, st_sum[:, 0])
                pe.wait_ge(ada_loaded[n], 16)
                for k in range(KD):
                    last = nc.tensor.matmul(ps[0:2, n], csil[:, k], raw_[:, :, k * P:(k + 1) * P],
                                            start=k == 0, stop=k == KD - 1)
                last.then_inc(ada_part, 1)
            pe.wait_ge(ident_in_s, 16)
            pe.wait_ge(ada_copied, 1)
            for m_ in range(16):
                last = nc.tensor.transpose(ps[:, 7, 2 * m_:2 * m_ + 2], ada_row[:, m_ // 4, tile_cols(m_ % 4)],
                                           ident[0:2, 0:2])
            last.then_inc(ada_done, 1)
            pe.wait_ge(N0["root"], 1)
            mean(N0C, TC, st_sum[:, 1])

            def tile(t):
                return slice(t * P, (t + 1) * P)

            def halves_of(ap, n, half):
                return ap.rearrange("p (m h n) -> p m h n", h=2, n=n)[:, :, half]

            def as_cut(N, xs, earlier=0):
                def of(k):
                    pe.wait_ge(N["lo"], k + 1 + earlier)
                    return xs(k)
                return of

            def pe_head(i, j):
                def free(k):
                    pe.wait_ge(acc_free, i * 6 + (k + 1))

                def begin_output(k, part):
                    xs = whole(y_hi, y_lo)
                    if part == "a":
                        s = take(k)
                        pe.wait_ge(acc_free, HEADS * 6 + 2)
                        tiles(s, [ps[:, k]], xs, range(4), True, False)
                    elif part == "b":
                        tiles(k % 2, [ps[:, k]], xs, range(4, 8), False, False, 4).then_inc(w_used[k % 2], 1)

                def project(k, part):
                    if i is None:
                        if k < EARLY:
                            begin_output(k, part)
                        return
                    a, c = k % 2, 2 + k % 2
                    if part == "a":
                        s = take(k)
                        free(k)
                        xs = whole(h_hi, h_lo)
                        tiles(s, [ps[:, a]], as_cut(N0, xs) if j is None and k == 0 else xs, range(4), True, False)
                    elif part == "b":
                        xs = whole(h_hi, h_lo)
                        last = tiles(k % 2, [ps[:, a]], as_cut(N0, xs) if j is None and k == 0 else xs,
                                     range(4, 8), False, True, 4)
                        if k in (0, 4):
                            last.then_inc(w_used[k % 2], 1)
                    elif part == "c":
                        xs = whole(hc_hi, hc_lo, 0, TC)
                        tiles(k % 2, [ps[:, c, 0:TC]], as_cut(N0C, xs) if j is None and k == 1 else xs,
                              range(8), True, True
                              ).then_inc(w_used[k % 2], 1)
                    else:
                        free(k)
                        pe.wait_ge(gate_loaded, i * 16 + 16)
                        for n in range(KD):
                            last = nc.tensor.matmul(ps[:, c, 2:4], gate_raw[:, n * P:(n + 1) * P], csil[:, n],
                                                    start=n == 0, stop=n == KD - 1)
                        last.then_inc(gate_used, 1)
                        s = take(k)
                        tiles(s, [ps[:, c, 0:2]], whole(c_hi, c_lo, 0, 2), range(8), True, True
                              ).then_inc(w_used[s], 1)

                def dve(n):
                    pe.wait_ge(dve_scan, j * DVE_SCAN + n)

                def act(n):
                    pe.wait_ge(act_scan, (j + 1) * ACT_SCAN + n)

                def turn_v(ts):
                    if j is None:
                        return
                    if len(ts) == TT:
                        pe.wait_ge(acc_free, j * 6 + 6)
                    else:
                        act(1)
                    for n, t in enumerate(ts):
                        last = nc.tensor.transpose(ps[:, 6, tile(n)], v_st[:, tile(t)], ident[:])
                    last.then_inc(pe_scan, 1)

                def diagonal():
                    if j is None:
                        return
                    pe.wait_ge(gates_ready, j + 1)
                    for t in range(TT):
                        last = nc.tensor.matmul(ps[:, 4, tile(t)], ksum[:, tile(t)], q_st[:, tile(t)],
                                                start=True, stop=True)
                    last.then_inc(pe_scan, 1)

                def level(l):
                    if j is None:
                        return
                    if l == 0:
                        pe.wait_ge(act_scan, j * ACT_SCAN + 7)
                    else:
                        dve(l)
                    for t in range(TT):
                        for d in range(2):
                            last = nc.tensor.matmul(
                                halves_of(ps[:, 5 - l % 2, tile(t)], 2 ** l, 1 - d),
                                K[:, d, tile(CT + t)], halves_of(Q[:, d, tile(t)], 2 ** l, 1 - d),
                                start=True, stop=True)
                    last.then_inc(pe_scan, 1)

                def steps(g_):
                    return [(n, d) for n in range(2 * g_, min(2 * g_ + 2, 5)) for d in range(2)]

                def turn_k(g_):
                    if j is None:
                        return
                    dve(7)
                    act(2 + g_)
                    for x, (n, d) in enumerate(steps(g_)):
                        last = nc.tensor.transpose(ps[:, 6, tile(x)], K[:, d, tile(ORDER[d][n])], ident[:])
                    last.then_inc(pe_scan, 1)

                def outer(g_):
                    if j is None:
                        return
                    act(3 + g_)
                    dve((7, 8, 9)[g_])
                    for x, (n, d) in enumerate(steps(g_)):
                        last = nc.tensor.matmul(ps[:, 4 + g_ % 2, tile(x)], KT[:, x], V[:, ORDER[d][n]],
                                                start=True, stop=True)
                    last.then_inc(pe_scan, 1)

                def output():
                    if j is None:
                        return
                    dve(11)
                    for t in range(TT):
                        o = ps[:, 7, tile(t)]
                        nc.tensor.matmul(o, V[:, CT + t], ST[:, t], start=True, stop=False)
                        nc.tensor.matmul(o, states[:, 1 + t, 0], Q[:, 0, tile(t)], start=False, stop=False)
                        last = nc.tensor.matmul(o, states[:, 4 - t, 1], Q[:, 1, tile(t)], start=False, stop=True)
                    last.then_inc(pe_scan, 1)

                def norm():
                    if j is None:
                        return
                    act(6)
                    nc.tensor.matmul(ps[:, 5], ones_h[:], osq[:], start=True, stop=True).then_inc(pe_scan, 1)

                project(0, "a"); turn_v(range(CT, AT)); project(0, "b"); diagonal(); level(0)
                project(1, "a"); level(1); turn_v(range(CT)); project(1, "b"); level(2)
                project(1, "c"); level(3); project(2, "a"); level(4); project(2, "b"); level(5)
                project(2, "c"); level(6); project(3, "a"); turn_k(0); project(3, "b"); outer(0)
                turn_k(1); project(3, "c"); outer(1); turn_k(2); project(4, "a"); outer(2)
                project(4, "b"); output(); project(5, "ada"); norm()

            st.enter(0, 6)
            pe_head(0, None)
            st.leave(1)
            with pe.Fori(0, HEADS - 1) as j:
                st.enter(j, 6)
                pe_head(j + 1, j)
            st.leave(HEADS - 1)
            st.enter(0, EARLY)
            pe_head(None, HEADS - 1)
            st.leave(1)

            def residual(R, trips, nb, xs, n, nk=KD, done=0):
                with pe.Fori(0, trips) as i:
                    st.enter(i, 2 * nb)
                    for a in range(2):
                        o = bank2(2 * a) if n == TM else [ps[:, 2 * a]]
                        for q in range(nb):
                            s = take(a * nb + q)
                            if q == 0:
                                pe.wait_ge(R["res"], i * 2 + (done + a + 1))
                            tiles(s, o, xs, range(q * KD, q * KD + nk), q == 0, q == nb - 1
                                  ).then_inc(w_used[s], 1)
                st.leave(trips)

            st.enter(0, EARLY)
            for k in range(EARLY):
                s = take(k)
                tiles(s, [ps[:, k]], as_cut({"lo": y_cut}, whole(y_hi, y_lo)), range(8, 16), False, True
                      ).then_inc(w_used[s], 1)
            st.leave(1)
            residual(RC, (KD - EARLY) // 2, 2, whole(y_hi, y_lo), T, done=EARLY)
            mean(N1, T, n1["sum"][:, 0])

            def pe_group(i, j):
                def project(k):
                    if i is None:
                        return
                    s = take(k)
                    pe.wait_ge(ft_acc, i * 4 + (k + 1))
                    xs = whole(g_hi, g_lo)
                    tiles(s, [ps[:, k % 2]], as_cut(N1, xs) if j is None and k == 0 else xs, range(8), True, True
                          ).then_inc(w_used[s], 1)

                def turn():
                    if j is None:
                        return
                    pe.wait_ge(ft_acc, j * 4 + 4)
                    pe.wait_ge(dve_ft, j * 8 + 1)
                    for a in range(2):
                        for t in range(TT):
                            last = nc.tensor.transpose(ps[:, 4 + a, tile(t)], u_st[:, a, tile(t)], ident[:])
                    last.then_inc(pe_ft, 1)

                def over_tokens(a):
                    if j is None:
                        return
                    pe.wait_ge(dft_split["dve"], 1)
                    pe.wait_ge(dve_ft, j * 8 + (2 + a))
                    for t in range(TT):
                        last = three([ps[:, 6 + a]], u_hi[:, a, tile(t)], u_lo[:, a, tile(t)],
                                     [F_hi[:, t]], [F_lo[:, t]], t == 0, t == TT - 1)
                    last.then_inc(pe_ft, 1)

                def over_channels(m_):
                    if j is None:
                        return
                    pe.wait_ge(dft_split["dve"], 2)
                    pe.wait_ge(dve_ft, j * 8 + 5)
                    for part, c0, n in ((0, 0, BF), (1, 256, 256)):
                        for kk in range(2):
                            last = three([ps[:, 4 + 2 * m_ + part, 0:n]], C_hi[:, part, kk, m_],
                                         C_lo[:, part, kk, m_], [p_hi[:, kk, c0:c0 + n]],
                                         [p_lo[:, kk, c0:c0 + n]], kk == 0, kk == 1)
                    last.then_inc(pe_ft, 1)

                project(0); turn(); project(1); over_tokens(0); over_tokens(1)
                project(2); over_channels(0); project(3); over_channels(1)

            st.enter(0, 4)
            pe_group(0, None)
            st.leave(1)
            with pe.Fori(0, GROUPS - 1) as j:
                st.enter(j, 4)
                pe_group(j + 1, j)
            st.leave(GROUPS - 1)
            pe_group(None, GROUPS - 1)
            pe.wait_ge(dve_ft, GROUPS * 8 + 1)

            residual(RF, KD // 2, 2, whole(y_hi, y_lo), T)
            mean(NFIN, T, n1["sum"][:, 0])
            for k in range(KD):
                pe.wait_ge(RA["sq"], k + 1)
                for q in range(2):
                    last = nc.tensor.matmul(ps[:, 6 + q, 0:HALF], ones_d[:], squares8[:, k, q * HALF:(q + 1) * HALF],
                                            start=k == 0, stop=k == KD - 1)
            last.then_inc(NF1["mean"], 1)

            def feed_forward(tags, N, last_tag, n):
                inner = halved(n_hi, n_lo) if n == TM else whole(n_hi, n_lo, META, TM)
                xs = as_cut(N, inner)
                hs = halved(hid_hi, hid_lo) if n == TM else whole(hid_hi, hid_lo, META, TM)
                for tag, count in zip(tags, FF_GROUPS):
                    S, before = ffn[tag]
                    with pe.Fori(0, count) as i:
                        st.enter(i, 2)
                        for k, reader in ((0, "gate"), (1, "up")):
                            s = take(k)
                            if k and before:
                                pe.wait_ge(before_R["res"], KD + 2)
                            pe.wait_ge(S[reader], i + (before + 1))
                            o = bank2(2 * k) if n == TM else [ps[:, 2 * k]]
                            tiles(s, o, xs if k == 0 else inner, range(KD), True, True).then_inc(w_used[s], 1)
                    st.leave(count)
                    R = RP.get(tag, last_tag)
                    pe.wait_ge(S["gate"], before + count + 1)
                    residual(R, KD // 2, 1, as_cut(S, hs, before + 1), n, count)
                    pe.wait_ge(R["res"], KD + (2 if tag == tags[-1] else 1))
                    before_R = R

            feed_forward(("f1a", "f1b", "f1c"), NF1, RD1, TM)
            mean(NMIX, TM, n2["sum"][:, 0])

            with pe.Fori(0, KD // 2) as i:
                st.enter(i, 14)
                for k in range(14):
                    s = take(k)
                    if k in WIDE:
                        p_ = WIDE.index(k)
                        pe.wait_ge(mx_acc, i * 14 + 3 + (WIDE[p_ - 2] if p_ > 1 else WIDE[p_ - 2] - 14))
                        xs = halved(n_hi, n_lo) if k < 6 else whole(n_hi, n_lo, META, TM)
                        o = bank2(2 * (p_ % 2)) if k < 6 else [ps[:, 2 * (p_ % 2)]]
                        tiles(s, o, xs if k else as_cut(NMIX, xs), range(KD), True, True).then_inc(w_used[s], 1)
                        continue
                    if k == RG_A:
                        pe.wait_ge(mx_dve, i * 12 + 5)
                    else:
                        pe.wait_ge(mx_acc, i * 14 + (RG_A + 3))
                    for m_ in range(2):
                        last = tiles(s, bank2(4 + 2 * m_), halved(xr_hi, xr_lo), range(2), True, True, 2 * m_)
                    last.then_inc(w_used[s], 1)
            st.leave(KD // 2)
            pe.wait_ge(mx_dve, KD // 2 * 12)
            pe.wait_ge(mx_acc, KD // 2 * 14 + 2)
            residual(YA, 2, 1, whole(a_hi, a_lo), T)
            for k in range(KD):
                if k == KD - 1:
                    pe.wait_ge(conv_done, 1)
                last = nc.tensor.matmul(ps[:, 6], ones_d[:], cv[:, k], start=k == 0, stop=k == KD - 1)
            last.then_inc(ln_pe, 1)
            residual(YA, 1, 1, whole(a_hi, a_lo), T, done=4)
            for k in range(KD):
                pe.wait_ge(ln_act, k + 1)
                last = nc.tensor.matmul(ps[:, 7], ones_d[:], centred_sq[:, k], start=k == 0, stop=k == KD - 1)
            last.then_inc(ln_pe, 1)
            residual(YA, 1, 1, whole(a_hi, a_lo), T, done=6)
            residual(YA, KD // 2, 1, as_cut({"lo": ln_lo}, whole(n_hi, n_lo)), T, done=8)
            pe.wait_ge(YA["res"], 2 * KD + 2)
            residual(RM, KD // 2, 1, as_cut({"lo": mg_lo_s}, whole(mg_hi, mg_lo)), T)
            mean(NF2, T, n2["sum"][:, 0])
            phase_end()
            feed_forward(("f2a", "f2b", "f2c"), NF2, RD2, T)
            mean(NOUT, T, n2["sum"][:, 0])

        @block.scalar
        def _(act):
            st = Stream()
            over = [0]
            own = Own(act, own_s["act"])
            run = nc.scalar.activation

            def phase_end():
                over[0] += 1
                act.drain().then_inc(phase_over, 1)
                act.wait_ge(phase_over, 3 * over[0])

            def cut(k):
                s, use = st.slot(k)
                act.wait_ge(w_loaded[s], use * 16 + 16)
                act.wait_ge(w_used[s], use + 1)
                run(w_hi[:, s], w_raw[:, s], ACT.Copy).then_inc(hi_ready[s], 1)

            def after(k):
                st.wait_done(act, k)
                cut(k + 2)

            def fetch_root():
                run(unused[:], eps[:], ACT.Sqrt)

            def root(N, acc, rt_):
                act.wait_ge(N["mean"], 1)
                run(rt_, acc, ACT.Sqrt, bias=eps[:]).then_inc(N["root"], 1)

            def norm_hi(N, hi, tmp, shift):
                for k in range(KD):
                    act.wait_ge(N["tmp"], k + 1)
                    run(hi(k), tmp(k), ACT.Identity, bias=shift(k)).then_inc(N["hi"], 1)

            def squares(R, src, sq):
                for k in range(KD):
                    if k:
                        act.wait_ge(R["add"], k)
                    run(sq, src(k), ACT.Square).then_inc(R["sq"], 1)

            def square_one(R, m_, src, sq, credit):
                act.wait_ge(R["res"], m_ + (1 + credit))
                act.wait_ge(R["add"], m_ + 2)
                run(sq, src, ACT.Square).then_inc(R["sq"], 1)

            for sem_ in (acc_free, ft_acc, mx_acc):
                act.sem_inc(sem_, 2)
            act.sem_inc(act_scan, ACT_SCAN)
            for tag in ("f1a", "f2a"):
                act.sem_inc(ffn[tag][0]["gate"], 1)

            act.wait_ge(vec_in_s, 16)
            run(csil[:], vec[:, VEC["c"]:VEC["c"] + 2 * KD].rearrange("p (k n) -> p k n", n=2), ACT.Silu
                ).then_inc(small["act"], 1)
            act.wait_ge(small["act"], 1)
            run(c_hi[:], csil[:], ACT.Copy).then_inc(small["act"], 1)
            act.wait_ge(consts_set, 2)
            run(lbt[:, 1:3], lbt[:, 1:3], ACT.Exp).then_inc(small["act"], 1)
            act.wait_ge(consts_set, 3)
            run(rgc[:, 1], rgc[:, 0], ACT.Exp, scale=-1.0).then_inc(small["act"], 1)
            act.wait_ge(x_in_s, 16)
            squares(R0, lambda k: x0[:, k], st_sq[:])
            act.wait_ge(xc_in_s, 16)
            act.wait_ge(R0["add"], KD)
            squares(R0C, lambda k: xc[:, k], st_sq[:, 0:TC])
            act.wait_ge(R0C["add"], KD)
            root(N0, ps[:, 6], st_sq[:])
            cut(0)
            cut(1)
            norm_hi(N0, lambda k: h_hi[:, k], lambda k: st_tmp[:, k % 2], lambda k: ada0[:, k, 0:1])
            root(N0C, ps[:, 6, 0:TC], st_tmpc[:, 2])
            norm_hi(N0C, lambda k: hc_hi[:, k], lambda k: st_tmpc[:, k % 2], lambda k: ada0[:, k, 1:2])

            def act_head(i, j, f):
                def pe(n):
                    act.wait_ge(pe_scan, j * PE_SCAN + n)

                def dve(n):
                    act.wait_ge(dve_scan, j * DVE_SCAN + n)

                def stage(k):
                    if i is None:
                        if j is not None and k < EARLY:
                            after(k)
                        return
                    after(k)
                    a, c = ps[:, k % 2], ps[:, 2 + k % 2]
                    if k == 0:
                        if j is not None:
                            pe(2)
                        run(q_st[:], a, ACT.Silu).then_inc(acc_free, 1)
                    elif k < 3:
                        if j is not None:
                            dve(1)
                        run(f_st[:, k - 1, TC:TA], a, ACT.Sigmoid)
                        run(f_st[:, k - 1, 0:TC], c[:, 0:TC], ACT.Sigmoid).then_inc(acc_free, 1)
                    elif k == 3:
                        if j is not None:
                            pe(5)
                        run(v_st[:, TC:TA], a, ACT.Copy)
                        run(v_st[:, 0:TC], c[:, 0:TC], ACT.Copy).then_inc(acc_free, 1)
                    elif k == 4:
                        if j is not None:
                            act.wait_ge(z_taken, j + 1)
                        run(z_st[:], a, ACT.Silu).then_inc(acc_free, 1)
                    else:
                        run(row(ada1, i), c[:, 0:2], ACT.Identity, bias=col("ada_b1", i))
                        run(row(gates, i), c[:, 2:4], ACT.Identity, bias=col("gate_b", i)).then_inc(acc_free, 1)

                def copy(n, dst, src):
                    if j is not None:
                        pe(n)
                        run(dst, src, ACT.Copy).then_inc(act_scan, 1)

                def squares_of_output():
                    if j is not None:
                        pe(17)
                        run(osq[:], ps[:, 7], ACT.Square).then_inc(act_scan, 1)

                def root_of_output():
                    if j is not None:
                        pe(18)
                        run(rt[:], ps[:, 5], ACT.Sqrt, bias=eps[:]).then_inc(act_scan, 1)

                def cut_output():
                    if f is not None:
                        act.wait_ge(y_ready, f + 1)
                        run(row(y_hi, f), ytmp[:], ACT.Copy).then_inc(y_hi_ready, 1)

                copy(1, V[:, CT:AT].rearrange("p t v -> p (t v)"), ps[:, 6])
                stage(0)
                copy(5, V[:, 0:CT].rearrange("p t v -> p (t v)"), ps[:, 6, 0:TC])
                stage(1)
                stage(2)
                kt = KT[:].rearrange("p t v -> p (t v)")
                copy(11, kt, ps[:, 6])
                copy(13, kt, ps[:, 6])
                stage(3)
                copy(15, kt[:, 0:2 * P], ps[:, 6, 0:2 * P])
                cut_output()
                stage(4)
                squares_of_output()
                stage(5)
                root_of_output()

            st.enter(0, 6)
            act_head(0, None, None)
            st.leave(1)
            st.enter(0, 6)
            act_head(1, 0, None)
            st.leave(1)
            with act.Fori(0, HEADS - 2) as f:
                st.enter(f, 6)
                act_head(f + 2, f + 1, f)
            st.leave(HEADS - 2)
            st.enter(0, EARLY)
            act_head(None, HEADS - 1, HEADS - 2)
            st.leave(1)
            act_head(None, None, HEADS - 1)

            def residual(R, trips, nb, src, sq, sums, ahead=True, done=0):
                def one(i):
                    for a in range(2):
                        for q in range(nb):
                            if ahead or not isinstance(i, int):
                                after(a * nb + q)
                        if sums:
                            square_one(R, i * 2 + (a + done), src(i * 2 + (a + done)), sq, 2)
                if ahead:
                    with act.Fori(0, trips) as i:
                        st.enter(i, 2 * nb)
                        one(i)
                    st.leave(trips)
                else:
                    with act.Fori(0, trips - 1) as i:
                        st.enter(i, 2 * nb)
                        one(i)
                    st.leave(trips - 1)
                    one_last = trips - 1
                    for a in range(2):
                        if sums:
                            square_one(R, one_last * 2 + a, src(one_last * 2 + a), sq, 2)

            st.enter(0, EARLY)
            for k in range(EARLY):
                after(k)
                square_one(RC, k, x1[:, k], n1["sq"][:, 0], 2)
            st.leave(1)
            residual(RC, (KD - EARLY) // 2, 2, lambda m_: row(x1, m_), n1["sq"][:, 0], True, done=EARLY)
            fetch_root()
            act.wait_ge(N1["sum"], 1)
            root(N1, ps[:, 6], n1["sq"][:, 0])
            norm_hi(N1, lambda k: g_hi[:, k], lambda k: n1["tmp"][:, k % 2], lambda k: ada1[:, k, 0:1])
            act.wait_ge(dft_in_s, 16)
            run(F_hi[:], F_raw[:], ACT.Copy).then_inc(dft_split["act"], 1)
            act.wait_ge(chan_in_s, 16)
            run(C_hi[:], C_raw[:], ACT.Copy).then_inc(dft_split["act"], 1)
            act.wait_ge(dft_split["dve"], 2)

            def act_group(i, j):
                def pe(n):
                    act.wait_ge(pe_ft, j * 5 + n)

                def dve(n):
                    act.wait_ge(dve_ft, j * 8 + (n + 1))

                def stage(k):
                    if i is None:
                        return
                    if j is not None:
                        if k < 2:
                            pe(1)
                        else:
                            dve(5 + 2 * (k - 2))
                    if k < 2:
                        run(u_st[:, k], ps[:, k % 2], ACT.Copy).then_inc(ft_acc, 1)
                    else:
                        run(zf_st[:, k - 2], ps[:, k % 2], ACT.Silu).then_inc(ft_acc, 1)

                def hi(n, dst, src):
                    if j is not None:
                        pe(n)
                        run(dst, src, ACT.Copy).then_inc(act_ft, 1)

                def tail(m_):
                    if j is None:
                        return
                    pe(4 + m_)
                    run(o_sb[:], ps[:, 5 + 2 * m_, 0:256], ACT.Copy).then_inc(act_ft, 1)
                    dve(5 + 2 * m_)
                    run(row(y_hi, j * 2 + m_), yg[:], ACT.Copy).then_inc(act_ft, 1)

                if i is not None:
                    after(0)
                hi(1, u_hi[:, 0], ps[:, 4])
                hi(1, u_hi[:, 1], ps[:, 5])
                stage(0)
                if i is not None:
                    after(1)
                stage(1)
                hi(2, p_hi[:, 0], ps[:, 6])
                hi(3, p_hi[:, 1], ps[:, 7])
                if i is not None:
                    after(2)
                tail(0)
                stage(2)
                if i is not None:
                    after(3)
                tail(1)
                stage(3)

            st.enter(0, 4)
            act_group(0, None)
            st.leave(1)
            with act.Fori(0, GROUPS - 1) as j:
                st.enter(j, 4)
                act_group(j + 1, j)
            st.leave(GROUPS - 1)
            act_group(None, GROUPS - 1)

            residual(RF, KD // 2, 2, lambda m_: row(x1, m_), n1["sq"][:, 0], True)
            fetch_root()
            act.wait_ge(NFIN["sum"], 1)
            root(NFIN, ps[:, 6], n1["sq"][:, 0])
            act.wait_ge(meta_in_s, 16)
            for k in range(KD):
                act.wait_ge(RA["res"], k + 1)
                run(squares8[:, k], hb[:, k], ACT.Square).then_inc(RA["sq"], 1)

            def block_norm(N, n):
                fetch_root()
                act.wait_ge(N["sum"], 1)
                if n == TM:
                    root(N, ps[:, 6:8, 0:HALF], halves(n2["sq"][:, 0]))
                    norm_hi(N, lambda k: n_hi[:, k], lambda k: n2["tmp"][:, k % 2], lambda k: zero[:])
                else:
                    root(N, ps[:, 6], n2["sq"][:, 0, 0:T])
                    norm_hi(N, lambda k: n_hi[:, k, META:TM], lambda k: n2["tmp"][:, k % 2, 0:T],
                            lambda k: zero[:])

            def feed_forward(tags, last_R, n, last):
                c0 = TM - n
                for tag, count in zip(tags, FF_GROUPS):
                    S, before = ffn[tag]
                    with act.Fori(0, count) as i:
                        st.enter(i, 2)
                        after(0)
                        acc = ps[:, 0:2, 0:HALF] if n == TM else ps[:, 0]
                        dst = halves(sg[:]) if n == TM else sg[:, 0:n]
                        act.wait_ge(S["up"], i + (before + 1))
                        run(dst, acc, ACT.Silu).then_inc(S["gate"], 1)
                        after(1)
                        act.wait_ge(S["up"], i + (before + 2))
                        run(row(hid_hi, i)[:, c0:TM], hid[:, 0:n], ACT.Copy).then_inc(S["hi"], 1)
                    st.leave(count)
                    final = tag == tags[-1]
                    residual(last_R if final else RP[tag], KD // 2, 1,
                             lambda m_: row(hb, m_)[:, c0:TM], n2["sq"][:, 0, 0:n], final,
                             not (final and last))

            block_norm(NF1, TM)
            feed_forward(("f1a", "f1b", "f1c"), RD1, TM, False)
            block_norm(NMIX, TM)

            with act.Fori(0, KD // 2) as i:
                st.enter(i, 14)
                own.enter(i, 4)

                def out_of(k, dst, func, bias):
                    n = TM if k < 6 else T
                    b0 = 2 * (WIDE.index(k) % 2)
                    acc = ps[:, b0:b0 + 2, 0:HALF] if n == TM else ps[:, b0]
                    run(halves(dst) if n == TM else dst, acc, func, bias=bias).then_inc(mx_acc, 1)

                def heads_out(dst, bias):
                    for a in range(2):
                        last = run(halves(dst[:, a]), ps[:, 4 + 2 * a:6 + 2 * a, 0:HALF], ACT.Sigmoid,
                                   bias=col(bias, i * 2 + a))
                    last.then_inc(mx_acc, 1)

                def b_in(kind, a):
                    return col("b_in", i * 2 + (kind * KD + a))

                def dve(n):
                    act.wait_ge(mx_dve, i * 12 + n)

                after(0)
                out_of(0, gvs[:], ACT.Identity, b_in(2, 0))
                after(1)
                out_of(1, ggs[:], ACT.Sigmoid, b_in(3, 0))
                for a in range(2):
                    after(2 + a)
                    out_of(2 + a, xpad[:, a, RW - 1:RW - 1 + TM], ACT.Identity, b_in(0, a))
                after(4)
                dve(1)
                out_of(4, gvs[:], ACT.Identity, b_in(2, 1))
                for a in range(2):
                    dve(2 + a)
                    run(xr_hi[:, a], xr[:, a], ACT.Copy).then_inc(mx_act, 1)
                after(5)
                out_of(5, ggs[:], ACT.Sigmoid, b_in(3, 1))
                after(RG_A)
                heads_out(rr, "b_a")
                for a in range(2):
                    after(7 + a)
                    out_of(7 + a, yst[:, a], ACT.Gelu_apprx_tanh, b_in(1, a))
                after(RG_X)
                heads_out(ii, "b_x")
                after(10)
                out_of(10, row(gate[:, 0], i * 2), ACT.Sigmoid, b_in(4, 0))
                act.wait_ge(mx_acc, i * 14 + (RG_X + 3))
                dve(6)
                for a in range(2):
                    own.link(run(pp[:, a], rr[:, a], ACT.Tanh, scale=rate(i * 2 + (KD + a))))
                    own.link(run(rr[:, a], rr[:, a], ACT.Exp, scale=rate(i * 2 + a)))
                    run((gvs, ggs)[a][:], rr[:, a], ACT.Square).then_inc(mx_act, 1)
                after(11)
                out_of(11, row(gate[:, 1], i * 2), ACT.Sigmoid, b_in(5, 0))
                for a in range(2):
                    dve(7 + a)
                    run(pp[:, a], pp[:, a], ACT.Sqrt, bias=tiny[:]).then_inc(mx_act, 1)
                after(12)
                out_of(12, row(gate[:, 0], i * 2 + 1), ACT.Sigmoid, b_in(4, 1))
                for a in range(2):
                    dve(9 + a)
                    run(row(a_hi, i * 2 + a), yst[:, a], ACT.Copy).then_inc(mx_act, 1)
                after(13)
                out_of(13, row(gate[:, 1], i * 2 + 1), ACT.Sigmoid, b_in(5, 1))
            st.leave(KD // 2)
            own.leave(KD // 2)

            with act.Fori(0, 2) as i:
                st.enter(i, 2)
                after(0)
                after(1)
            st.leave(2)
            for k in range(KD):
                act.wait_ge(ln_dve, k + 1)
                run(centred_sq[:, k], cv[:, k], ACT.Square).then_inc(ln_act, 1)
            st.enter(0, 2)
            after(0)
            after(1)
            st.leave(1)
            fetch_root()
            act.wait_ge(ln_pe, 2)
            run(n2["sq"][:, 0, 0:T], ps[:, 7], ACT.Sqrt, bias=eps[:]).then_inc(ln_act, 1)
            st.enter(0, 2)
            for a in range(2):
                after(a)
                for k in range(4 * a, 4 * a + 4):
                    act.wait_ge(ln_norm, k + 1)
                    run(cv[:, k], cv[:, k], ACT.Silu, bias=col("ln_b", k)).then_inc(ln_silu, 1)
                    act.wait_ge(ln_silu, k + 1)
                    run(n_hi[:, k, 0:T], cv[:, k], ACT.Copy).then_inc(ln_hi, 1)
            st.leave(1)
            with act.Fori(0, KD // 2) as i:
                st.enter(i, 2)
                for a in range(2):
                    after(a)
                    act.wait_ge(mg_sum, i * 2 + (a + 1))
                    run(row(mg_hi, i * 2 + a), mt[:, a], ACT.Copy).then_inc(mg_hi_s, 1)
            st.leave(KD // 2)
            residual(RM, KD // 2, 1, lambda m_: row(hb, m_)[:, META:TM], n2["sq"][:, 0, 0:T], True)
            act.wait_ge(NF2["sum"], 1)
            phase_end()
            block_norm(NF2, T)
            feed_forward(("f2a", "f2b", "f2c"), RD2, T, True)
            fetch_root()
            act.wait_ge(NOUT["sum"], 1)
            root(NOUT, ps[:, 6], n2["sq"][:, 0, 0:T])

        @block.vector
        def _(dve):
            st = Stream()
            over = [0]
            own = Own(dve, own_s["dve"])
            v = nc.vector
            tt, ts, stt = v.tensor_tensor, v.tensor_scalar, v.scalar_tensor_tensor

            def phase_end():
                over[0] += 1
                dve.drain().then_inc(phase_over, 1)
                dve.wait_ge(phase_over, 3 * over[0])

            def cut(k):
                s, use = st.slot(k)
                dve.wait_ge(hi_ready[s], use + 1)
                tt(w_lo[:, s], w_raw[:, s], w_hi[:, s].bitcast(F32), ALU.subtract).then_inc(lo_ready[s], 1)

            def after(k):
                cut(k + 2)

            def sum_squares(R, n, acc, sq):
                for k in range(n):
                    dve.wait_ge(R["sq"], k + 1)
                    if k:
                        dve.wait_ge(R["add"], k)
                        tt(acc, acc, sq, ALU.add).then_inc(R["add"], 1)
                    else:
                        v.tensor_copy(acc, sq).then_inc(R["add"], 1)

            def norm_apply(N, src, gain, shift, tmp, rt_, hi, lo, inverted=False):
                if not inverted:
                    dve.wait_ge(N["root"], 1)
                    own.link(v.reciprocal(rt_, rt_))
                for k in range(KD + 1):
                    if k < KD:
                        if k > 1:
                            dve.wait_ge(N["lo"], k - 1)
                        stt(tmp(k), src(k), gain(k), rt_, ALU.mult, ALU.mult).then_inc(N["tmp"], 1)
                    if k:
                        dve.wait_ge(N["hi"], k)
                        stt(lo(k - 1), tmp(k - 1), shift(k - 1), hi(k - 1).bitcast(F32), ALU.add, ALU.subtract
                            ).then_inc(N["lo"], 1)

            def open_sums(R, acc, sq):
                v.memset(acc, 0.0).then_inc(R["add"], 1)
                v.memset(sq, 0.0).then_inc(R["sq"], 1)

            def add_square(R, m_, acc, sq):
                dve.wait_ge(R["sq"], m_ + 1)
                dve.wait_ge(R["add"], m_ + 1)
                tt(acc, acc, sq, ALU.add).then_inc(R["add"], 1)

            def close_sums(R, N, acc, sq):
                dve.wait_ge(R["sq"], KD + 1)
                dve.wait_ge(R["add"], KD + 1)
                tt(acc, acc, sq, ALU.add).then_inc(N["sum"], 1)

            for s in range(2):
                dve.sem_inc(lo_ready[s], 1)
            for R in (RC, RF, RM, RD1, RD2, *RP.values()):
                dve.sem_inc(R["res"], 2)
            dve.sem_inc(dve_ft, 1)
            dve.sem_inc(YA["res"], 2)
            for tag in ("f1a", "f2a"):
                dve.sem_inc(ffn[tag][0]["up"], 1)
                dve.sem_inc(ffn[tag][0]["lo"], 1)

            v.memset(ones_d[:], 1.0 / D)
            v.memset(ones_h[:], 1.0 / P)
            v.memset(eps[:], EPS)
            v.memset(tiny[:], 2.0 ** -100)
            v.memset(zero[:], 0.0).then_inc(consts_set, 1)
            dve.wait_ge(vec_in_s, 16)
            lb = vec[:, VEC["lb"]:VEC["lb"] + 4 * HEADS].rearrange("p (n c) -> p n c", n=2)
            own.link(tt(lbt[:, 0], lb[:, 0], lb[:, 1], ALU.max))
            tt(lbt[:, 1:3], lb, lbt[:, 0:1].broadcast_to([P, 2, 2 * HEADS]), ALU.subtract).then_inc(consts_set, 1)
            lam = vec[:, VEC["lam"]:VEC["lam"] + KD]
            own.link(ts(rgc[:, 0], lam, -1.0, None, ALU.mult))
            tt(rgc[:, 0], rgc[:, 0], lam, ALU.max).then_inc(consts_set, 1)
            dve.wait_ge(small["act"], 2)
            tt(c_lo[:], csil[:], c_hi[:].bitcast(F32), ALU.subtract).then_inc(consts_set, 1)
            dve.wait_ge(small["act"], 3)
            own.link(tt(lbt[:, 3], lbt[:, 1], lbt[:, 2], ALU.add))
            own.link(v.reciprocal(lbt[:, 3], lbt[:, 3]))
            own.link(tt(lbt[:, 4], lbt[:, 1], lbt[:, 3], ALU.mult))
            own.mark(ts(lbt[:, 5], lbt[:, 4], -1.0, 1.0, ALU.mult, ALU.add))
            dve.wait_ge(small["act"], 4)
            z, w, w2, p_ = rgc[:, 1], rgc[:, 2], rgc[:, 3], rgc[:, 4]
            own.link(ts(w, z, 2.0, None, ALU.add))
            own.link(v.reciprocal(w, w))
            own.link(tt(w, w, z, ALU.mult))
            own.link(tt(w2, w, w, ALU.mult))
            own.link(ts(p_, w2, 1.0 / 19, None, ALU.mult))
            for n in range(17, 1, -2):
                own.link(stt(p_, p_, 1.0 / n, w2, ALU.add, ALU.mult))
            own.link(stt(p_, p_, 1.0, w, ALU.add, ALU.mult))
            own.link(ts(rgc[:, 5], lam, -1.0, 0.0, ALU.mult, ALU.max))
            own.link(stt(p_, p_, 2.0, rgc[:, 5], ALU.mult, ALU.add))
            ts(rgc[:, 6], p_, -8.0, None, ALU.mult)
            own.mark(ts(rgc[:, 7], p_, 8.0, None, ALU.mult))
            sum_squares(R0, KD, st_sum[:, 0], st_sq[:])
            dve.wait_ge(R0["add"], KD)
            dve.sem_inc(N0["sum"], 1)
            sum_squares(R0C, KD, st_sum[:, 1, 0:TC], st_sq[:, 0:TC])
            dve.wait_ge(R0C["add"], KD)
            dve.sem_inc(N0C["sum"], 1)
            for n in range(3):
                dve.wait_ge(ada_part, n + 1)
                v.tensor_copy(ada_row[:, n], ps[0:2, n])
            dve.wait_ge(N0["root"], 1)
            own.mark(v.reciprocal(st_sq[:], st_sq[:]))
            dve.wait_ge(ada_part, 4)
            v.tensor_copy(ada_row[:, 3], ps[0:2, 3]).then_inc(ada_copied, 1)
            cut(0)
            cut(1)
            dve.wait_ge(ada_done, 1)
            own.link(tt(ada0[:, 0:16], ps[:, 7, 0:32].rearrange("p (m n) -> p m n", n=2),
                        vec[:, VEC["ada_b0"]:VEC["ada_b0"] + 16].unsqueeze(2).broadcast_to([P, 16, 2]), ALU.add))
            g0 = vec[:, VEC["norm_g0"]:VEC["norm_g0"] + KD]
            for n in range(2):
                own.mark(stt(scale[:, n], ada0[:, 8:16, n:n + 1].rearrange("p k n -> p (k n)"), 1.0, g0,
                             ALU.add, ALU.mult))
            own.wait()
            norm_apply(N0, lambda k: x0[:, k], lambda k: scale[:, 0, k:k + 1], lambda k: ada0[:, k, 0:1],
                       lambda k: st_tmp[:, k % 2], st_sq[:], lambda k: h_hi[:, k], lambda k: h_lo[:, k], inverted=True)
            norm_apply(N0C, lambda k: xc[:, k], lambda k: scale[:, 1, k:k + 1], lambda k: ada0[:, k, 1:2],
                       lambda k: st_tmpc[:, k % 2], st_tmpc[:, 2], lambda k: hc_hi[:, k], lambda k: hc_lo[:, k])
            dve.wait_ge(const_in_s, 16)

            def tree(l):
                if l == 0:
                    return f_st[:]
                at = TA - (TA >> (l - 1))
                return f_tree[:, :, at:at + (TA >> l)]

            def dve_head(i, j, f):
                def pe(n):
                    dve.wait_ge(pe_scan, j * PE_SCAN + n)

                def mine(n):
                    dve.wait_ge(dve_scan, j * DVE_SCAN + n)

                def next_block(k):
                    if i is not None or k < EARLY:
                        after(k)

                def prepare():
                    if i is None:
                        return
                    dve.wait_ge(acc_free, i * 6 + 7)
                    if j is not None:
                        mine(11)
                        pe(17)
                    for d in range(2):
                        own.mark(ts(f_st[:, d], f_st[:, d], lbt[:, 5, ds(i + d * HEADS, 1)],
                                    lbt[:, 4, ds(i + d * HEADS, 1)], ALU.mult, ALU.add))
                    own.wait()
                    own.mark(ts(K[:], f_st[:], -1.0, 1.0, ALU.mult, ALU.add))
                    tt(Q[:], q_st[:].unsqueeze(1).broadcast_to([P, 2, T]), f_st[:, :, TC:TA], ALU.mult)
                    own.wait()
                    tt(ksum[:], K[:, 0, TC:TA], K[:, 1, TC:TA], ALU.add).then_inc(gates_ready, 1)

                def place(l, bank, signal=False):
                    last = v.copy_predicated(ST[:], masks[:, l].unsqueeze(1).broadcast_to([P, TT, P]),
                                             ps[:, bank].rearrange("p (t s) -> p t s", t=TT))
                    if signal:
                        last.then_inc(dve_scan, 1)
                    else:
                        own.mark(last)

                def merge(l):
                    n = 2 ** l
                    prev = tree(l).rearrange("p d (m h) -> p d m h", h=2)
                    if l == 0:
                        dve.wait_ge(gates_ready, j + 1)
                        pe(2)
                    own.mark(tt(tree(l + 1), prev[:, :, :, 0], prev[:, :, :, 1], ALU.mult))
                    if l == 0:
                        place(LEVELS, 4)
                    own.wait()
                    pe((3, 4, 6, 7, 8, 9, 10)[l])
                    if l:
                        mine(l)
                    for t, t0, size in ((Q, TC, T), (K, 0, TA)):
                        for d in range(2):
                            half = 1 - d if t is Q else d
                            part = t[:, d].rearrange("p (m h n) -> p m h n", h=2, n=n)[:, :, half]
                            by = prev[:, d, t0 // (2 * n):, 1 - half].unsqueeze(2).broadcast_to(
                                [P, size // (2 * n), n])
                            last = tt(part, part, by, ALU.mult)
                    last.then_inc(dve_scan, 1)
                    place(l, 5 - l % 2, l == LEVELS - 1)

                def passed(g_):
                    pe((12, 14, 16)[g_])
                    whole_tile = tree(LEVELS)
                    acc = ps[:, 4 + g_ % 2].rearrange("p (x c) -> p x c", c=P)
                    for x, n in enumerate(range(2 * g_, min(2 * g_ + 2, 5))):
                        if n == 0:
                            own.mark(v.tensor_copy(states[:, 0], acc[:, 0:2]))
                        else:
                            if x or g_ == 0:
                                own.wait()
                            for d in range(2):
                                tile_ = ORDER[d][n]
                                last = stt(states[:, n, d], states[:, n - 1, d], whole_tile[:, d, tile_:tile_ + 1],
                                           acc[:, 2 * x + d], ALU.mult, ALU.add)
                                if d == 1 and x == min(2, 5 - 2 * g_) - 1:
                                    last.then_inc(dve_scan, 1)
                                else:
                                    own.mark(last)

                def invert_root():
                    if f is not None:
                        dve.wait_ge(act_scan, (f + 1) * ACT_SCAN + 7)
                        own.link(v.reciprocal(rt[:], rt[:]))

                def gate_output():
                    if f is not None:
                        own.link(stt(ytmp[:], ps[:, 7], col("hg_g", 0), rt[:], ALU.mult, ALU.mult))
                        tt(ytmp[:], ytmp[:], z_cur[:], ALU.mult).then_inc(y_ready, 1)

                def cut_output():
                    if f is not None:
                        dve.wait_ge(y_hi_ready, f + 1)
                        tt(row(y_lo, f), ytmp[:], row(y_hi, f).bitcast(F32), ALU.subtract).then_inc(y_cut, 1)

                def take_z():
                    if j is not None:
                        v.tensor_copy(z_cur[:], z_st[:]).then_inc(z_taken, 1)

                if j is None:
                    if i is not None:
                        for k in range(6):
                            after(k)
                        prepare()
                    invert_root()
                    gate_output()
                    cut_output()
                    return
                next_block(0)
                merge(0)
                merge(1)
                merge(2)
                next_block(1)
                merge(3)
                merge(4)
                merge(5)
                next_block(2)
                merge(6)
                invert_root()
                passed(0)
                gate_output()
                next_block(3)
                mine(9)
                passed(1)
                cut_output()
                take_z()
                mine(10)
                passed(2)
                next_block(4)
                prepare()
                next_block(5)

            st.enter(0, 6)
            dve_head(0, None, None)
            st.leave(1)
            st.enter(0, 6)
            dve_head(1, 0, None)
            st.leave(1)
            with dve.Fori(0, HEADS - 2) as f:
                st.enter(f, 6)
                own.enter(f, PER["head"])
                dve_head(f + 2, f + 1, f)
            st.leave(HEADS - 2)
            own.leave(HEADS - 2)
            st.enter(0, EARLY)
            dve_head(None, HEADS - 1, HEADS - 2)
            st.leave(1)
            dve_head(None, None, HEADS - 1)

            def residual(R, trips, nb, out_row, factor, n, sums, N=None, ahead=True, done=0):
                if sums and not done:
                    open_sums(R, *sums)

                def one(i, cuts):
                    for a in range(2):
                        for q in range(nb):
                            if cuts:
                                after(a * nb + q)
                        st.wait_done(dve, a * nb + nb - 1)
                        m_ = i * 2 + (a + done)
                        r_ = out_row(m_)
                        acc = ps[:, 2 * a:2 * a + 2, 0:HALF] if n == TM else ps[:, 2 * a]
                        r_ = halves(r_) if n == TM else r_
                        stt(r_, acc, factor(m_), r_, ALU.mult, ALU.add).then_inc(R["res"], 1)
                        if sums:
                            add_square(R, m_, *sums)

                n_loop = trips if ahead else trips - 1
                with dve.Fori(0, n_loop) as i:
                    st.enter(i, 2 * nb)
                    one(i, True)
                st.leave(n_loop)
                if not ahead:
                    st.enter(0, 2 * nb)
                    one(trips - 1, False)
                    st.leave(1)
                if sums:
                    close_sums(R, N, *sums)

            dve.wait_ge(x1_in_s, 16)
            sums = (n1["sum"][:, 0], n1["sq"][:, 0])
            open_sums(RC, *sums)
            st.enter(0, EARLY)
            for k in range(EARLY):
                after(k)
                st.wait_done(dve, k)
                stt(x1[:, k], ps[:, k], gates[:, k, 0:1], x1[:, k], ALU.mult, ALU.add).then_inc(RC["res"], 1)
                add_square(RC, k, *sums)
            st.leave(1)
            residual(RC, (KD - EARLY) // 2, 2, lambda m_: row(x1, m_), lambda m_: row(gates, m_)[:, 0:1], T,
                     sums, N1, done=EARLY)
            own.link(stt(scale[:, 2], ada1[:, 8:16, 0:1].rearrange("p k n -> p (k n)"), 1.0,
                         vec[:, VEC["norm_g1"]:VEC["norm_g1"] + KD], ALU.add, ALU.mult))
            norm_apply(N1, lambda k: x1[:, k], lambda k: scale[:, 2, k:k + 1], lambda k: ada1[:, k, 0:1],
                       lambda k: n1["tmp"][:, k % 2], n1["sq"][:, 0], lambda k: g_hi[:, k], lambda k: g_lo[:, k])
            dve.wait_ge(dft_split["act"], 1)
            tt(F_lo[:], F_raw[:], F_hi[:].bitcast(F32), ALU.subtract).then_inc(dft_split["dve"], 1)
            dve.wait_ge(dft_split["act"], 2)
            flat = "p a b c d -> p (a b c d)"
            tt(C_lo[:].rearrange(flat), C_raw[:].rearrange(flat), C_hi[:].rearrange(flat).bitcast(F32),
               ALU.subtract).then_inc(dft_split["dve"], 1)
            dve.wait_ge(dft_split["dve"], 2)

            def dve_group(i, j):
                def lo(n, dst, src, hi):
                    if j is not None:
                        dve.wait_ge(act_ft, j * 8 + n)
                        tt(dst, src, hi.bitcast(F32), ALU.subtract).then_inc(dve_ft, 1)

                def next_block(k):
                    if i is not None:
                        after(k)

                def mirror(m_):
                    if j is None:
                        return
                    e = ps[:, 4 + 2 * m_]
                    dve.wait_ge(act_ft, j * 8 + (5 + 2 * m_))
                    dve.wait_ge(ft_acc, j * 4 + 6)
                    tt(yf[:, 1:256], e[:, 1:256], o_sb[:, 1:256], ALU.subtract)
                    tt(yf[:, 511:256:-1], e[:, 1:256], o_sb[:, 1:256], ALU.add)
                    own.link(v.tensor_copy(yf[:, 0:512:256], e[:, 0:512:256]))
                    dve.wait_ge(dve_ft, j * 8 + (5 + 2 * m_))
                    tt(yg[:], yf[:], zf_st[:, m_], ALU.mult).then_inc(dve_ft, 1)
                    dve.wait_ge(act_ft, j * 8 + (6 + 2 * m_))
                    tt(row(y_lo, j * 2 + m_), yg[:], row(y_hi, j * 2 + m_).bitcast(F32), ALU.subtract
                       ).then_inc(dve_ft, 1)

                next_block(0)
                lo(1, u_lo[:, 0], ps[:, 4], u_hi[:, 0])
                lo(2, u_lo[:, 1], ps[:, 5], u_hi[:, 1])
                next_block(1)
                lo(3, p_lo[:, 0], ps[:, 6], p_hi[:, 0])
                lo(4, p_lo[:, 1], ps[:, 7], p_hi[:, 1])
                next_block(2)
                mirror(0)
                next_block(3)
                mirror(1)

            st.enter(0, 4)
            dve_group(0, None)
            st.leave(1)
            with dve.Fori(0, GROUPS - 1) as j:
                st.enter(j, 4)
                own.enter(j, 2)
                dve_group(j + 1, j)
            st.leave(GROUPS - 1)
            own.leave(GROUPS - 1)
            dve_group(None, GROUPS - 1)

            residual(RF, KD // 2, 2, lambda m_: row(x1, m_), lambda m_: row(gates, m_ + KD)[:, 0:1], T,
                     (n1["sum"][:, 0], n1["sq"][:, 0]), NFIN)
            dve.wait_ge(NFIN["root"], 1)
            own.link(v.reciprocal(n1["sq"][:, 0], n1["sq"][:, 0]))
            for k in range(KD):
                stt(hb[:, k, META:TM], x1[:, k], col("final_g", k), n1["sq"][:, 0], ALU.mult, ALU.mult
                    ).then_inc(RA["res"], 1)
            dve.wait_ge(RA["res"], KD)
            dve.sem_inc(NF1["sum"], 1)

            def block_norm(N, name, n):
                c0 = TM - n
                norm_apply(N, lambda k: hb[:, k, c0:TM], lambda k: col(name, k), lambda k: zero[:],
                           lambda k: n2["tmp"][:, k % 2, 0:n], n2["sq"][:, 0, 0:n],
                           lambda k: n_hi[:, k, c0:TM], lambda k: n_lo[:, k, c0:TM])

            def feed_forward(tags, last_R, N, n, last):
                c0 = TM - n
                for tag, count in zip(tags, FF_GROUPS):
                    S, before = ffn[tag]
                    with dve.Fori(0, count) as i:
                        st.enter(i, 2)
                        after(0)
                        after(1)
                        st.wait_done(dve, 1)
                        dve.wait_ge(S["gate"], i + (before + 2))
                        dve.wait_ge(S["lo"], i + (before + 1))
                        acc = ps[:, 2:4, 0:HALF] if n == TM else ps[:, 2]
                        a, b_ = (halves(hid[:]), halves(sg[:])) if n == TM else (hid[:, 0:n], sg[:, 0:n])
                        tt(a, acc, b_, ALU.mult).then_inc(S["up"], 1)
                        dve.wait_ge(S["hi"], i + (before + 1))
                        tt(row(hid_lo, i)[:, c0:TM], hid[:, 0:n], row(hid_hi, i)[:, c0:TM].bitcast(F32),
                           ALU.subtract).then_inc(S["lo"], 1)
                    st.leave(count)
                    final = tag == tags[-1]
                    sums = (n2["sum"][:, 0, 0:n], n2["sq"][:, 0, 0:n]) if final else None
                    residual(last_R if final else RP[tag], KD // 2, 1, lambda m_: row(hb, m_)[:, c0:TM],
                             lambda m_: 0.5, n, sums, N, not (final and last))

            block_norm(NF1, "ffn1_g", TM)
            feed_forward(("f1a", "f1b", "f1c"), RD1, NMIX, TM, False)
            block_norm(NMIX, "mix_g", TM)

            own.mark(v.memset(vpad[:, 0:DW - 1], 0.0))
            own.link(v.memset(xpad[:, :, 0:RW - 1], 0.0))
            st.enter(0, 14)
            after(0)
            with dve.Fori(0, KD // 2) as i:
                st.enter(i, 14)
                own.enter(i, PER["mix"])

                def staged(k):
                    dve.wait_ge(mx_acc, i * 14 + (k + 3))

                def mine(n):
                    dve.wait_ge(mx_dve, i * 12 + n)

                def actv(n):
                    dve.wait_ge(mx_act, i * 8 + n)

                def tap(a, t):
                    dst = (row(cv, i * 2 + a), odd_taps)[t % 2]
                    src = vpad[:, META + t:META + t + T]
                    w_ = col("dw", i * 2 + (t * KD + a))
                    if t > 1:
                        own.wait(1)
                    if t == 0:
                        own.mark(ts(dst, src, w_, col("dwb", i * 2 + a), ALU.mult, ALU.add))
                    elif t == 1:
                        own.mark(ts(dst, src, w_, None, ALU.mult))
                    else:
                        own.mark(stt(dst, src, w_, dst, ALU.mult, ALU.add))
                    if t == DW - 1:
                        own.wait()
                        dst = row(cv, i * 2 + a)
                        own.link(tt(dst, dst, odd_taps, ALU.add))

                taps = [(a, t) for a in range(2) for t in range(DW)]

                def some_taps(count):
                    for _ in range(count):
                        tap(*taps.pop(0))

                def product(a):
                    staged((1, 5)[a])
                    tt(vpad[:, DW - 1:DW - 1 + TM], gvs[:], ggs[:], ALU.mult).then_inc(mx_dve, 1)
                    mine((1, 6)[a])

                after(1)
                product(0)
                some_taps(5)
                after(2)
                some_taps(5)
                after(3)
                for a in range(2):
                    staged(2 + a)
                for t in range(RW):
                    for a in range(2):
                        src = xpad[:, a, t:t + TM]
                        w_ = col("rw", i * 2 + (t * KD + a))
                        if t:
                            own.wait(1)
                        if t == 0:
                            own.mark(ts(xr[:, a], src, w_, col("rb", i * 2 + a), ALU.mult, ALU.add))
                        elif t < RW - 1:
                            own.mark(stt(xr[:, a], src, w_, xr[:, a], ALU.mult, ALU.add))
                        elif a == 0:
                            stt(xr[:, a], src, w_, xr[:, a], ALU.mult, ALU.add).then_inc(mx_dve, 1)
                        else:
                            own.wait()
                            stt(xr[:, a], src, w_, xr[:, a], ALU.mult, ALU.add).then_inc(mx_dve, 1)
                after(4)
                for a in range(2):
                    actv(1 + a)
                    tt(xr_lo[:, a], xr[:, a], xr_hi[:, a].bitcast(F32), ALU.subtract).then_inc(mx_dve, 1)
                some_taps(4)
                after(5)
                some_taps(6)
                after(6)
                some_taps(3)
                after(7)
                some_taps(6)
                after(8)
                some_taps(2)
                product(1)
                some_taps(2)
                after(9)
                some_taps(2)
                after(10)
                for a in range(2):
                    actv(3 + a)
                    tt(ii[:, a], ii[:, a], xr[:, a], ALU.mult)
                    stt(pp[:, a], (gvs, ggs)[a][:], 1.0, pp[:, a], ALU.add, ALU.mult).then_inc(mx_dve, 1)
                some_taps(4)
                after(11)
                for a in range(2):
                    actv(5 + a)
                    own.link(tt(ii[:, a], ii[:, a], pp[:, a], ALU.mult))
                    own.link(v.tensor_tensor_scan(pp[:, a], rr[:, a], ii[:, a], 0.0, ALU.mult, ALU.add))
                    staged(7 + a)
                    tt(yst[:, a], yst[:, a], pp[:, a, META:TM], ALU.mult).then_inc(mx_dve, 1)
                some_taps(2)
                after(12)
                some_taps(6)
                for a in range(2):
                    actv(7 + a)
                    tt(row(a_lo, i * 2 + a), yst[:, a], row(a_hi, i * 2 + a).bitcast(F32), ALU.subtract
                       ).then_inc(mx_dve, 1)
                after(13)
                some_taps(7)
                after(14)
                some_taps(len(taps))
            st.leave(KD // 2)
            own.leave(KD // 2)
            dve.sem_inc(conv_done, 1)

            lroot = n2["sq"][:, 0, 0:T]

            def gated(i, a, done):
                m_ = i * 2 + (a + done)
                if m_ != 0:
                    after(a)
                st.wait_done(dve, a)
                tt(row(gate[:, 0], m_), ps[:, 2 * (a % 2)], row(gate[:, 0], m_), ALU.mult).then_inc(YA["res"], 1)

            dve.wait_ge(mx_acc, KD // 2 * 14 + 2)
            st.enter(0, 4)
            for k in range(4):
                gated(0, k, 0)
            st.leave(1)
            dve.wait_ge(ln_pe, 1)
            for k in range(KD):
                tt(cv[:, k], cv[:, k], ps[:, 6], ALU.subtract).then_inc(ln_dve, 1)
            st.enter(0, 2)
            gated(0, 0, 4)
            gated(0, 1, 4)
            st.leave(1)
            dve.wait_ge(ln_act, KD + 1)
            own.link(v.reciprocal(lroot, lroot))
            st.enter(0, 2)
            for a in range(2):
                gated(0, a, 6)
                for k in range(4 * a, 4 * a + 5):
                    if k < 4 * a + 4:
                        stt(cv[:, k], cv[:, k], col("ln_g", k), lroot, ALU.mult, ALU.mult).then_inc(ln_norm, 1)
                    if k > 4 * a:
                        dve.wait_ge(ln_hi, k)
                        tt(n_lo[:, k - 1, 0:T], cv[:, k - 1], n_hi[:, k - 1, 0:T].bitcast(F32), ALU.subtract
                           ).then_inc(ln_lo, 1)
            st.leave(1)

            with dve.Fori(0, KD // 2) as i:
                st.enter(i, 2)
                for a in range(2):
                    m_ = i * 2 + a
                    after(a)
                    st.wait_done(dve, a)
                    stt(mt[:, a], ps[:, 2 * a], col("cpb", m_), row(gate[:, 1], m_), ALU.add, ALU.mult
                        ).then_inc(YA["res"], 1)
                    dve.wait_ge(YA["res"], i * 2 + (a + KD + 3))
                    tt(mt[:, a], mt[:, a], row(gate[:, 0], m_), ALU.add).then_inc(mg_sum, 1)
                    dve.wait_ge(mg_hi_s, m_ + 1)
                    tt(row(mg_lo, m_), mt[:, a], row(mg_hi, m_).bitcast(F32), ALU.subtract).then_inc(mg_lo_s, 1)
            st.leave(KD // 2)
            residual(RM, KD // 2, 1, lambda m_: row(hb, m_)[:, META:TM], lambda m_: 1.0, T,
                     (n2["sum"][:, 0, 0:T], n2["sq"][:, 0, 0:T]), NF2)
            phase_end()
            block_norm(NF2, "ffn2_g", T)
            feed_forward(("f2a", "f2b", "f2c"), RD2, NOUT, T, True)
            dve.wait_ge(NOUT["root"], 1)
            own.link(v.reciprocal(n2["sq"][:, 0, 0:T], n2["sq"][:, 0, 0:T]))
            for k in range(KD):
                stt(fin[:, k], hb[:, k, META:TM], col("out_g", k), n2["sq"][:, 0, 0:T], ALU.mult, ALU.mult
                    ).then_inc(NOUT["lo"], 1)


def _cols(a):
    return np.asarray(a).reshape(-1, P).T


def _blocks(w, ks=None):
    w = np.asarray(w)
    k, m = w.shape[0] // P, w.shape[1] // P
    tiles = w.reshape(k, P, m, P).transpose(2, 1, 0, 3)
    groups, at = [], 0
    for n in ks or (KD,) * (k // KD):
        part = tiles[:, :, at:at + n]
        if n < KD:
            part = np.concatenate([part, np.zeros((m, P, KD - n, P), w.dtype)], axis=2)
        groups.append(part.reshape(m, P, BLK))
        at += n
    return groups


def _stream(i):
    out = []
    a1 = _blocks(i["ada_w"][1])[0]
    hg = _blocks(i["hg_w_in"][0])[0].reshape(5, HEADS, P, BLK)
    for h in range(HEADS):
        out += [*hg[:, h], a1[h]]
    wo = _blocks(i["hg_w_out"][0])
    out += [*wo[0][:EARLY], *wo[1][:EARLY]]
    for m in range(EARLY, KD):
        out += [wo[0][m], wo[1][m]]
    fi = _blocks(i["ft_w_in"][0])[0].reshape(2, HEADS, P, BLK)
    for g in range(GROUPS):
        out += [fi[0, 2 * g], fi[0, 2 * g + 1], fi[1, 2 * g], fi[1, 2 * g + 1]]
    fo = _blocks(i["ft_w_out"][0])
    for m in range(KD):
        out += [fo[0][m], fo[1][m]]

    def feed_forward(name):
        gu, down = _blocks(i[name + "_w_gu_2"][0])[0], _blocks(i[name + "_w_down_2"][0], FF_GROUPS)
        blocks, at = [], 0
        for n, d in zip(FF_GROUPS, down):
            for j in range(at, at + n):
                blocks += [gu[j], gu[FT + j]]
            blocks += list(d)
            at += n
        return blocks

    out += feed_forward("ffn1")
    wi = _blocks(i["w_in_2"][0])[0].reshape(6, KD, P, BLK)
    heads = []
    for name in ("rg_w_a_2", "rg_w_x_2"):
        w = np.asarray(i[name][0]).reshape(4, 2, P, 2, P).transpose(0, 2, 3, 1, 4).reshape(4, P, 4 * P)
        heads.append(np.concatenate([w, np.zeros_like(w)], axis=2))
    for n in range(KD // 2):
        a, b = 2 * n, 2 * n + 1
        out += [wi[2, a], wi[3, a], wi[0, a], wi[0, b], wi[2, b], wi[3, b], heads[0][n],
                wi[1, a], wi[1, b], heads[1][n], wi[4, a], wi[5, a], wi[4, b], wi[5, b]]
    rn, cp = _blocks(i["rnn_w_proj_2"][0])[0], _blocks(i["conv_w_proj_2"][0])[0]
    out += [*rn, *cp]
    out += list(_blocks(i["w_out_2"][0])[0])
    out += feed_forward("ffn2")
    return np.stack(out)


def _ada(i):
    a0, a1 = _blocks(i["ada_w"][0])[0], _blocks(i["ada_w"][1])[0]
    return np.ascontiguousarray(a0[:16]), np.concatenate([a0[16:], a1[16:]])


def _vectors(i):
    c = np.stack([_cols(i["c"][0]), _cols(i["c_ctx"])], axis=2).reshape(P, 2 * KD)
    lb = np.asarray(i["hg_lb_logits"]).reshape(2, 2, HEADS, P).transpose(3, 0, 1, 2).reshape(P, -1)
    b0, b1 = _cols(i["ada_b"][0]), _cols(i["ada_b"][1])
    parts = [c, b0[:, :16], b0[:, 16:], b1[:, 16:], b1[:, :16], _cols(i["norm_g"][0]), _cols(i["norm_g"][1]), lb,
             _cols(i["hg_norm_g"][0]), _cols(i["final_g"]), _cols(i["ffn1_norm_2"][0]), _cols(i["mix_norm_2"][0]),
             _cols(i["b_in_2"][0]), _cols(i["rnn_conv_w_2"][0]), _cols(i["rnn_conv_b_2"][0]),
             _cols(i["rg_b_a_2"][0]), _cols(i["rg_b_x_2"][0]), _cols(i["rg_lambda_2"][0]),
             _cols(i["conv_dw_w_2"][0]), _cols(i["conv_dw_b_2"][0]), _cols(i["conv_ln_g_2"][0]),
             _cols(i["conv_ln_b_2"][0]), _cols(i["conv_b_proj_2"][0]), _cols(i["ffn2_norm_2"][0]),
             _cols(i["final_norm_2"])]
    return np.ascontiguousarray(np.concatenate(parts, axis=1))


def _turned(a):
    a = np.asarray(a)
    return np.ascontiguousarray(a.reshape(a.shape[0], KD, P).transpose(2, 1, 0))


def _tables():
    s, t = np.arange(P)[:, None], np.arange(P)[None, :]
    masks = [(s // (2 * n) == t // (2 * n)) & (s // n != t // n) for n in (2 ** l for l in range(LEVELS))]
    masks = np.stack(masks + [s == t], axis=1).astype(np.int32)
    tok = np.arange(T)[:, None]
    seq = np.concatenate([np.cos(2 * np.pi * (tok * np.arange(257)[None] % T) / T),
                          np.sin(2 * np.pi * (tok * np.arange(1, 256)[None] % T) / T)], axis=1) / np.sqrt(T)
    seq = seq.reshape(TT, P, T).transpose(1, 0, 2).astype(np.float32)
    ch = np.arange(256)
    ang = 2 * np.pi * (ch[:, None] * ch[None] % 256) / 256
    chan = np.stack([np.cos(ang), np.sin(ang)]) / np.sqrt(256)
    chan = chan.reshape(2, 2, P, 2, P).transpose(2, 0, 1, 3, 4).astype(np.float32)
    return masks, np.eye(P, dtype=np.float32), np.ascontiguousarray(seq), np.ascontiguousarray(chan)


def kernel(**inputs):
    import concourse.bacc as _bacc
    from concourse.bass_utils import run_bass_kernel_spmd as _run

    nc = _bacc.Bacc("TRN2", target_bir_lowering=False, num_devices=1)
    i = {k: np.asarray(v) for k, v in inputs.items()}
    masks, ident, seq, chan = _tables()
    given = {"weights": _stream(i), "ada_weights": _ada(i)[0], "gate_weights": _ada(i)[1], "x": _turned(i["x"][0]), "ctx": _turned(i["ctx"][0]),
             "meta": _turned(i["meta_tokens_2"]), "vectors": _vectors(i), "masks": masks,
             "identity": ident, "seq_dft": seq, "chan_dft": chan}
    arrays, args = {}, []
    for name, a in given.items():
        arrays[f"in_{name}_dram"] = a
        args.append(nc.dram_tensor(f"in_{name}_dram", a.shape, mybir.dt.from_np(a.dtype), kind="ExternalInput").ap())
    args.append(nc.dram_tensor("out_0_dram", (P, KD, T), F32, kind="ExternalOutput").ap())
    program(nc, *args)
    r = _run(nc, [arrays], core_ids=[0])
    return np.ascontiguousarray(r.results[0]["out_0_dram"].transpose(2, 1, 0).reshape(1, T, D))
```
